# Optimizing a Trainium2 kernel written in Bass

```python
import jax, jax.numpy as jnp
from jax import lax
import numpy as np

D_MODEL = 1024
BATCH = 1
SEQ = 1024
DEPTH = 1

HEAD_DIM = 64
ATTN_WIDTH = 3 * D_MODEL // 4
N_ATTN_HEADS = ATTN_WIDTH // HEAD_DIM
CONV_WIDTH = D_MODEL - ATTN_WIDTH
MIX_WIDTH = ATTN_WIDTH + CONV_WIDTH
IN_WIDTH = 4 * ATTN_WIDTH + 4 * CONV_WIDTH
CONV_K = 3
DILATED_PATTERNS = ((128, 1), (512, 4), (2048, 16))
BLOCK = 128
ROPE_THETA = 10000.0
NORM_EPS = 1e-6


def rmsnorm(x, g):
    xf = x.astype(jnp.float32)
    y = xf * lax.rsqrt(jnp.mean(xf * xf, axis=-1, keepdims=True) + NORM_EPS)
    return (y * g.astype(jnp.float32)).astype(x.dtype)

def rope(t, pos):
    half = t.shape[-1] // 2
    inv_freq = ROPE_THETA ** (-jnp.arange(half, dtype=jnp.float32) * 2.0 / t.shape[-1])
    ang = pos.astype(jnp.float32)[:, None] * inv_freq[None, :]
    cos = jnp.cos(ang)[None, :, None, :]
    sin = jnp.sin(ang)[None, :, None, :]
    tf = t.astype(jnp.float32)
    t1, t2 = tf[..., :half], tf[..., half:]
    out = jnp.concatenate([t1 * cos - t2 * sin, t2 * cos + t1 * sin], axis=-1)
    return out.astype(t.dtype)

def banded_window_attn(q, k, v, window_keys):
    N, L, H, hd = q.shape
    Lp = -(-L // BLOCK) * BLOCK
    padw = ((0, 0), (0, Lp - L), (0, 0), (0, 0))
    q, k, v = jnp.pad(q, padw), jnp.pad(k, padw), jnp.pad(v, padw)
    nb = Lp // BLOCK
    qb = q.reshape(N, nb, BLOCK, H, hd)
    kb = k.reshape(N, nb, BLOCK, H, hd)
    vb = v.reshape(N, nb, BLOCK, H, hd)
    shift = ((0, 0), (1, 0), (0, 0), (0, 0), (0, 0))
    kk = jnp.concatenate([jnp.pad(kb, shift)[:, :-1], kb], axis=2)
    vv = jnp.concatenate([jnp.pad(vb, shift)[:, :-1], vb], axis=2)
    s = jnp.einsum('nbqhd,nbkhd->nbhqk', qb, kk).astype(jnp.float32) * (hd ** -0.5)
    qi = jnp.arange(BLOCK)[:, None]
    kj = jnp.arange(2 * BLOCK)[None, :]
    dist = qi + BLOCK - kj
    key_abs = jnp.arange(nb)[:, None, None] * BLOCK + kj[None] - BLOCK
    valid = (dist >= 0)[None] & (dist <= window_keys)[None] & (key_abs >= 0)
    s = jnp.where(valid[None, :, None], s, -jnp.inf)
    m = jnp.max(s, axis=-1, keepdims=True)
    p = jnp.exp(s - m)
    den = jnp.sum(p, axis=-1, keepdims=True)
    lse = (m + jnp.log(den))[..., 0]
    o = jnp.einsum('nbhqk,nbkhd->nbqhd', (p / den).astype(v.dtype), vv)
    o = o.reshape(N, Lp, H, hd)[:, :L]
    lse = lse.transpose(0, 1, 3, 2).reshape(N, Lp, H)[:, :L]
    return o, lse

def dilated_window_attn(q, k, v, window, dilation):
    B, S, H, hd = q.shape
    L = S // dilation

    def to_res(t):
        return t.reshape(B, L, dilation, H, hd).transpose(0, 2, 1, 3, 4).reshape(B * dilation, L, H, hd)

    o, lse = banded_window_attn(to_res(q), to_res(k), to_res(v), window // dilation)
    o = o.reshape(B, dilation, L, H, hd).transpose(0, 2, 1, 3, 4).reshape(B, S, H, hd)
    lse = lse.reshape(B, dilation, L, H).transpose(0, 2, 1, 3).reshape(B, S, H)
    return o, lse

def causal_depthwise_conv(u, w):
    S = u.shape[1]
    up = jnp.pad(u, ((0, 0), (CONV_K - 1, 0), (0, 0)))
    y = up[:, 0:S] * w[0]
    for j in range(1, CONV_K):
        y = y + up[:, j:j + S] * w[j]
    return y

def first_inputs(seed: int = 0) -> dict:
    key = jax.random.key(seed)
    ks = jax.random.split(key, 6)
    x = jax.random.normal(ks[0], (BATCH, SEQ, D_MODEL), jnp.float32)
    norm_pre_g = 1.0 + 0.01 * jax.random.normal(ks[1], (D_MODEL,), jnp.float32)
    w_in = jax.random.normal(ks[2], (D_MODEL, IN_WIDTH), jnp.float32) * D_MODEL ** -0.5
    conv_w = jax.random.normal(ks[3], (CONV_K, CONV_WIDTH), jnp.float32) * CONV_K ** -0.5
    w_out = jax.random.normal(ks[4], (MIX_WIDTH, D_MODEL), jnp.float32) * MIX_WIDTH ** -0.5
    norm_post_g = 1.0 + 0.01 * jax.random.normal(ks[5], (D_MODEL,), jnp.float32)
    return {"x": x, "norm_pre_g": norm_pre_g, "w_in": w_in, "conv_w": conv_w,
            "w_out": w_out, "norm_post_g": norm_post_g}

def first_block(x, norm_pre_g, w_in, conv_w, w_out, norm_post_g):
    B, S, _ = x.shape
    pos = jnp.arange(S)
    for _layer in range(DEPTH):
        h = rmsnorm(x, norm_pre_g)
        z = jnp.einsum('bsd,de->bse', h, w_in)
        A, C = ATTN_WIDTH, CONV_WIDTH
        cuts = np.cumsum([A, A, A, A, C, C, C])
        q, k, v, g_attn, c_h, c_b, c_c, g_conv = jnp.split(z, cuts, axis=-1)

        q = rope(q.reshape(B, S, N_ATTN_HEADS, HEAD_DIM), pos)
        k = rope(k.reshape(B, S, N_ATTN_HEADS, HEAD_DIM), pos)
        v = v.reshape(B, S, N_ATTN_HEADS, HEAD_DIM)
        outs, lses = [], []
        for window, dilation in DILATED_PATTERNS:
            o_i, lse_i = dilated_window_attn(q, k, v, window, dilation)
            outs.append(o_i)
            lses.append(lse_i)
        mix_w = jax.nn.softmax(jnp.stack(lses, axis=0), axis=0)
        o = jnp.sum(mix_w[..., None] * jnp.stack(outs, axis=0).astype(jnp.float32), axis=0)
        attn_out = o.astype(x.dtype).reshape(B, S, ATTN_WIDTH) * jax.nn.silu(g_attn)

        conv_out = c_b * causal_depthwise_conv(c_c * c_h, conv_w.astype(x.dtype))
        conv_out = conv_out * jax.nn.silu(g_conv)

        mixed = jnp.concatenate([attn_out, conv_out], axis=-1)
        y = jnp.einsum('bse,ed->bsd', mixed, w_out)
        x = x + rmsnorm(y, norm_post_g)
    return x


N_MEM = 256
EPS = 1e-6
MLSTM_HEADS = 4
MLSTM_HEAD_DIM = D_MODEL // MLSTM_HEADS
MLSTM_DIM = MLSTM_HEADS * MLSTM_HEAD_DIM
MLSTM_CHUNK = 128
CONV_WIDTH_2 = 4
SGU_GROUPS = 8
SGU_GROUP_DIM = D_MODEL // SGU_GROUPS
SGU_DIM = SGU_GROUPS * SGU_GROUP_DIM
SGU_CHUNK = 128
N_BRANCH = 2
IN_WIDTHS = (2 * MLSTM_DIM, MLSTM_DIM, MLSTM_DIM, MLSTM_HEADS, MLSTM_HEADS, SGU_DIM, SGU_DIM, N_BRANCH * D_MODEL)
IN_DIM = sum(IN_WIDTHS)
SPLIT_POINTS = tuple(int(s) for s in np.cumsum(IN_WIDTHS)[:-1])
XATTN_HEADS = 4
XATTN_HEAD_DIM = D_MODEL // XATTN_HEADS
XATTN_DIM = XATTN_HEADS * XATTN_HEAD_DIM
MOE_GROUPS = 4
EXPERTS_PER_GROUP = 8
N_EXPERTS = MOE_GROUPS * EXPERTS_PER_GROUP
MOE_TOPK = 2
EXPERT_FF = D_MODEL // 2
MOE_BLOCK = 128


def rmsnorm_2(x, g):
    x32 = x.astype(jnp.float32)
    y = x32 * lax.rsqrt(jnp.mean(x32 * x32, axis=-1, keepdims=True) + EPS)
    return (y * g.astype(jnp.float32)).astype(x.dtype)

def causal_depthwise_conv_2(x, w, b):
    c = x.shape[-1]
    y = lax.conv_general_dilated(x, w[:, None, :].astype(x.dtype), window_strides=(1,),
                                 padding=[(CONV_WIDTH_2 - 1, 0)],
                                 dimension_numbers=('NWC', 'WIO', 'NWC'),
                                 feature_group_count=c)
    return y + b.astype(x.dtype)

def mlstm_chunkwise(q, k, v, i_pre, f_pre):
    B, S, H, dh = q.shape
    L = MLSTM_CHUNK
    nc = S // L
    f32 = jnp.float32

    def to_chunks(a):
        return a.astype(f32).reshape(B, nc, L, H, dh).transpose(1, 0, 3, 2, 4)

    qc = to_chunks(q)
    kc = to_chunks(k) * (dh ** -0.5)
    vc = to_chunks(v)
    logf = jax.nn.log_sigmoid(f_pre.astype(f32)).reshape(B, nc, L, H).transpose(1, 0, 3, 2)
    ig = i_pre.astype(f32).reshape(B, nc, L, H).transpose(1, 0, 3, 2)
    causal = jnp.tril(jnp.ones((L, L), dtype=bool))

    def step(carry, inp):
        C, n, m = carry
        q_, k_, v_, lf, ic = inp
        b = jnp.cumsum(lf, axis=-1)
        dmat = jnp.where(causal, b[..., :, None] - b[..., None, :] + ic[..., None, :], -jnp.inf)
        inter = b + m[..., None]
        m_t = jnp.maximum(inter, jnp.max(dmat, axis=-1))
        dexp = jnp.exp(dmat - m_t[..., None])
        inter_w = jnp.exp(inter - m_t)
        s = jnp.einsum('bhtd,bhsd->bhts', q_, k_) * dexp
        num = jnp.einsum('bhts,bhsd->bhtd', s, v_) + inter_w[..., None] * jnp.einsum('bhtd,bhde->bhte', q_, C)
        den = jnp.sum(s, axis=-1) + inter_w * jnp.einsum('bhtd,bhd->bht', q_, n)
        h = num / jnp.maximum(jnp.abs(den), jnp.exp(-m_t))[..., None]
        b_last = b[..., -1]
        w_log = b_last[..., None] - b + ic
        m_new = jnp.maximum(b_last + m, jnp.max(w_log, axis=-1))
        decay = jnp.exp(b_last + m - m_new)
        ws = jnp.exp(w_log - m_new[..., None])
        C_new = decay[..., None, None] * C + jnp.einsum('bhs,bhsd,bhse->bhde', ws, k_, v_)
        n_new = decay[..., None] * n + jnp.einsum('bhs,bhsd->bhd', ws, k_)
        return (C_new, n_new, m_new), h

    init = (jnp.zeros((B, H, dh, dh), f32), jnp.zeros((B, H, dh), f32), jnp.zeros((B, H), f32))
    _, hs = lax.scan(step, init, (qc, kc, vc, logf, ig))
    return hs.transpose(1, 0, 3, 2, 4).reshape(B, S, H, dh).astype(q.dtype)

def spatial_gating(u, v, sgu_norm_g, w_s, b_s):
    B, S, _ = u.shape
    nc = S // SGU_CHUNK
    u = jax.nn.gelu(u)
    v = rmsnorm_2(jax.nn.gelu(v), sgu_norm_g)
    vb = v.reshape(B, nc, SGU_CHUNK, SGU_GROUPS, SGU_GROUP_DIM)
    w_causal = jnp.tril(w_s).astype(v.dtype)
    mixed = jnp.einsum('gts,bcsgd->bctgd', w_causal, vb) + b_s.T.astype(v.dtype)[:, :, None]
    return u * mixed.reshape(B, S, SGU_DIM)

def hybrid_mixer(xn, w_in, b_gate, b_if, conv_w, conv_b, mh_norm_g, sgu_norm_g, w_s, b_s, w_out):
    B, S, _ = xn.shape
    proj = xn @ w_in
    qk, v, o, i_pre, f_pre, u, sv, gates = jnp.split(proj, SPLIT_POINTS, axis=-1)
    qk = jax.nn.silu(causal_depthwise_conv_2(qk, conv_w, conv_b))
    q, k = jnp.split(qk, 2, axis=-1)
    b_i, b_f = jnp.split(b_if, 2)
    hd = (B, S, MLSTM_HEADS, MLSTM_HEAD_DIM)
    h = mlstm_chunkwise(q.reshape(hd), k.reshape(hd), v.reshape(hd), i_pre + b_i, f_pre + b_f)
    y_a = rmsnorm_2(h, mh_norm_g.reshape(MLSTM_HEADS, MLSTM_HEAD_DIM)).reshape(B, S, MLSTM_DIM) * jax.nn.sigmoid(o)
    y_b = spatial_gating(u, sv, sgu_norm_g, w_s, b_s)
    g_a, g_b = jnp.split(jax.nn.sigmoid(gates + b_gate), 2, axis=-1)
    return (g_a * y_a + g_b * y_b) @ w_out

def memory_cross_attention(xn, mn, w_xq, w_xkv, w_xo):
    B, S, _ = xn.shape
    M = mn.shape[1]
    q = (xn @ w_xq).reshape(B, S, XATTN_HEADS, XATTN_HEAD_DIM)
    k, v = jnp.split(mn @ w_xkv, 2, axis=-1)
    k = k.reshape(B, M, XATTN_HEADS, XATTN_HEAD_DIM)
    v = v.reshape(B, M, XATTN_HEADS, XATTN_HEAD_DIM)
    scores = jnp.einsum('bshd,bmhd->bhsm', q, k).astype(jnp.float32) * (XATTN_HEAD_DIM ** -0.5)
    p = jax.nn.softmax(scores, axis=-1).astype(v.dtype)
    out = jnp.einsum('bhsm,bmhd->bshd', p, v).reshape(B, S, XATTN_DIM)
    return out @ w_xo

def hierarchical_moe(xn, w_rg, b_rg, w_re, b_re, w1, w3, w2):
    B, S, D = xn.shape
    N = B * S
    xt = xn.reshape(N, D)
    g_logits = (xt @ w_rg + b_rg).astype(jnp.float32)
    g_idx = jnp.argmax(g_logits, axis=-1)
    p_g = jnp.take_along_axis(jax.nn.softmax(g_logits, axis=-1), g_idx[:, None], axis=1)
    e_logits = (xt @ w_re + b_re).astype(jnp.float32).reshape(N, MOE_GROUPS, EXPERTS_PER_GROUP)
    e_in_group = jnp.take_along_axis(e_logits, g_idx[:, None, None], axis=1)[:, 0]
    top_v, top_i = lax.top_k(e_in_group, MOE_TOPK)
    gate = p_g * jax.nn.softmax(top_v, axis=-1)
    expert = g_idx[:, None].astype(jnp.int32) * EXPERTS_PER_GROUP + top_i.astype(jnp.int32)

    A = N * MOE_TOPK
    e_flat = expert.reshape(A)
    tok_flat = jnp.repeat(jnp.arange(N, dtype=jnp.int32), MOE_TOPK)
    order = jnp.argsort(e_flat)
    e_sorted = e_flat[order]
    counts = jnp.bincount(e_flat, length=N_EXPERTS)
    starts = jnp.cumsum(counts) - counts
    padded = (counts + MOE_BLOCK - 1) // MOE_BLOCK * MOE_BLOCK
    pends = jnp.cumsum(padded)
    pstarts = pends - padded
    dest_sorted = (pstarts[e_sorted] + jnp.arange(A, dtype=jnp.int32) - starts[e_sorted]).astype(jnp.int32)
    n_blocks = -(-A // MOE_BLOCK) + N_EXPERTS
    P = n_blocks * MOE_BLOCK
    buf_tok = jnp.zeros((P,), jnp.int32).at[dest_sorted].set(tok_flat[order])
    block_expert = jnp.minimum(
        jnp.searchsorted(pends, jnp.arange(n_blocks, dtype=jnp.int32) * MOE_BLOCK, side='right'),
        N_EXPERTS - 1).astype(jnp.int32)

    def block_ffn(args):
        tok, e = args
        xb = xt[tok]
        hb = jax.nn.silu(xb @ w1[e]) * (xb @ w3[e])
        return hb @ w2[e]

    out_buf = lax.map(block_ffn, (buf_tok.reshape(n_blocks, MOE_BLOCK), block_expert)).reshape(P, D)
    dest = jnp.zeros((A,), jnp.int32).at[order].set(dest_sorted)
    y_assign = out_buf[dest].reshape(N, MOE_TOPK, D)
    y = jnp.einsum('nk,nkd->nd', gate.astype(xt.dtype), y_assign)
    return y.reshape(B, S, D)

def second_inputs(seed: int = 0) -> dict:
    key = jax.random.key(seed)
    ks = jax.random.split(key, 32)
    D, L = D_MODEL, DEPTH

    def nrm(k, shape, scale):
        return jax.random.normal(k, shape, jnp.float32) * scale

    def gain(k, shape):
        return 1.0 + 0.02 * jax.random.normal(k, shape, jnp.float32)

    b_i = nrm(ks[4], (L, MLSTM_HEADS), 0.1)
    b_f = jnp.linspace(3.0, 6.0, MLSTM_HEADS, dtype=jnp.float32)[None, :] + nrm(ks[5], (L, MLSTM_HEADS), 0.1)
    return {
        'x': nrm(ks[0], (BATCH, SEQ, D), 1.0),
        'mem': nrm(ks[1], (BATCH, N_MEM, D), 1.0),
        'norm_mix_g': gain(ks[2], (L, D)),
        'w_in': nrm(ks[3], (L, D, IN_DIM), D ** -0.5),
        'b_gate': nrm(ks[6], (L, N_BRANCH * D), 0.02),
        'b_if': jnp.concatenate([b_i, b_f], axis=-1),
        'conv_w': nrm(ks[7], (L, CONV_WIDTH_2, 2 * MLSTM_DIM), CONV_WIDTH_2 ** -0.5),
        'conv_b': nrm(ks[8], (L, 2 * MLSTM_DIM), 0.02),
        'mh_norm_g': gain(ks[9], (L, MLSTM_DIM)),
        'sgu_norm_g': gain(ks[10], (L, SGU_DIM)),
        'w_s': nrm(ks[11], (L, SGU_GROUPS, SGU_CHUNK, SGU_CHUNK), SGU_CHUNK ** -0.5),
        'b_s': gain(ks[12], (L, SGU_GROUPS, SGU_CHUNK)),
        'w_out': nrm(ks[13], (L, D, D), D ** -0.5),
        'norm_x_g': gain(ks[14], (L, D)),
        'norm_mem_g': gain(ks[15], (L, D)),
        'w_xq': nrm(ks[16], (L, D, XATTN_DIM), D ** -0.5),
        'w_xkv': nrm(ks[17], (L, D, 2 * XATTN_DIM), D ** -0.5),
        'w_xo': nrm(ks[18], (L, XATTN_DIM, D), XATTN_DIM ** -0.5),
        'norm_moe_g': gain(ks[19], (L, D)),
        'w_rg': nrm(ks[20], (L, D, MOE_GROUPS), D ** -0.5),
        'b_rg': nrm(ks[21], (L, MOE_GROUPS), 0.01),
        'w_re': nrm(ks[22], (L, D, N_EXPERTS), D ** -0.5),
        'b_re': nrm(ks[23], (L, N_EXPERTS), 0.01),
        'w1': nrm(ks[24], (L, N_EXPERTS, D, EXPERT_FF), D ** -0.5),
        'w3': nrm(ks[25], (L, N_EXPERTS, D, EXPERT_FF), D ** -0.5),
        'w2': nrm(ks[26], (L, N_EXPERTS, EXPERT_FF, D), EXPERT_FF ** -0.5),
        'norm_f_g': gain(ks[27], (D,)),
    }

def second_block(x, mem, norm_mix_g, w_in, b_gate, b_if, conv_w, conv_b, mh_norm_g, sgu_norm_g, w_s, b_s, w_out,
              norm_x_g, norm_mem_g, w_xq, w_xkv, w_xo, norm_moe_g, w_rg, b_rg, w_re, b_re, w1, w3, w2, norm_f_g):
    for l in range(DEPTH):
        x = x + hybrid_mixer(rmsnorm_2(x, norm_mix_g[l]), w_in[l], b_gate[l], b_if[l], conv_w[l], conv_b[l],
                             mh_norm_g[l], sgu_norm_g[l], w_s[l], b_s[l], w_out[l])
        x = x + memory_cross_attention(rmsnorm_2(x, norm_x_g[l]), rmsnorm_2(mem, norm_mem_g[l]),
                                       w_xq[l], w_xkv[l], w_xo[l])
        x = x + hierarchical_moe(rmsnorm_2(x, norm_moe_g[l]), w_rg[l], b_rg[l], w_re[l], b_re[l],
                                 w1[l], w3[l], w2[l])
    return rmsnorm_2(x, norm_f_g)


def setup_inputs(seed=0):
    out = dict(first_inputs(seed))
    for name, value in second_inputs(seed + 1).items():
        if name != "x":
            out[name + "_2"] = value
    return out


def reference(
    x, norm_pre_g, w_in, conv_w, w_out, norm_post_g, mem_2, norm_mix_g_2, w_in_2, b_gate_2,
    b_if_2, conv_w_2, conv_b_2, mh_norm_g_2, sgu_norm_g_2, w_s_2, b_s_2, w_out_2, norm_x_g_2,
    norm_mem_g_2, w_xq_2, w_xkv_2, w_xo_2, norm_moe_g_2, w_rg_2, b_rg_2, w_re_2, b_re_2, w1_2,
    w3_2, w2_2, norm_f_g_2,
):
    x = first_block(
        x, norm_pre_g, w_in, conv_w, w_out, norm_post_g,
    )
    return second_block(
        x, mem_2, norm_mix_g_2, w_in_2, b_gate_2, b_if_2, conv_w_2, conv_b_2, mh_norm_g_2,
        sgu_norm_g_2, w_s_2, b_s_2, w_out_2, norm_x_g_2, norm_mem_g_2, w_xq_2, w_xkv_2, w_xo_2,
        norm_moe_g_2, w_rg_2, b_rg_2, w_re_2, b_re_2, w1_2, w3_2, w2_2, norm_f_g_2,
    )


_drawn_inputs = setup_inputs


def setup_inputs(seed=0):
    import zlib

    import numpy as np

    out = dict(_drawn_inputs(seed))
    spreads = {}
    factors = {'norm_post_g': 4.059,
     'norm_mix_g_2': 3.753,
     'b_gate_2': 8.0,
     'conv_b_2': 49.031,
     'mh_norm_g_2': 6.629,
     'sgu_norm_g_2': 8.0,
     'b_s_2': 5.117,
     'norm_x_g_2': 8.0,
     'norm_mem_g_2': 8.0,
     'norm_moe_g_2': 3.042,
     'b_rg_2': 34.19,
     'b_re_2': 19.67,
     'norm_f_g_2': 7.917}
    for name, (base, spread) in spreads.items():
        noise = np.random.default_rng([zlib.crc32(name.encode()), seed]).standard_normal(out[name].shape)
        drawn = base * np.exp(spread * noise) if base else spread * noise
        out[name] = __import__('jax').numpy.asarray(drawn.astype(out[name].dtype))
    for name, factor in factors.items():
        out[name] = (out[name] * factor).astype(out[name].dtype)
    return out
```

```python
from contextlib import ExitStack

import numpy as np

import concourse.bass as bass
from concourse import mybir

F32 = mybir.dt.float32
I32 = mybir.dt.int32
U32 = mybir.dt.uint32
ALU = mybir.AluOpType
ACT = mybir.ActivationFunctionType
AX = mybir.AxisListType.X

P = 128
D = 1024
S = 1024
KC = D // P
NT = S // P
BANK = 512
EPS = 1e-6
NEG = -1e30

HD = 64
AW = 768
NH = AW // HD
CW = 256
SCALE = HD ** -0.5
MH, MD, MV = 4, 256, 257
NMEM = 256
NE, NG, EPG, FF = 32, 4, 8, 512
NBLK = 2 * S // P + NE

CONST_COLS = dict(ident=P, ones=P, causal=P, before=P, iota=P, tokid=NT, blk=NBLK, sel=MH * P, iota32=NT * NE,
                  cos=NT * 32, sin=NT * 32, logc=S)
CONST_AT = {}
_at = 0
for _n, _w in CONST_COLS.items():
    CONST_AT[_n] = _at
    _at += _w
CONST_W = _at


def shape_constants():
    c = {n: np.zeros((P, w), np.float32) for n, w in CONST_COLS.items()}
    p = np.arange(P)
    c["ident"][p, p] = 1
    c["ones"][:] = 1
    c["causal"][:] = p[:, None] <= p[None, :]
    c["before"][:] = p[:, None] < p[None, :]
    c["iota"][:] = p[None, :]
    c["tokid"][:] = p[:, None] + P * np.arange(NT)[None, :]
    c["blk"][:] = P * np.arange(NBLK)[None, :]
    for h in range(MH):
        c["sel"][h, h * P:(h + 1) * P] = 1
    c["iota32"][:] = np.tile(np.arange(NE), NT)[None, :]
    inv = np.float32(10000.0) ** (-np.arange(32, dtype=np.float32) * np.float32(2.0) / np.float32(64))
    ang = np.arange(S, dtype=np.float32)[:, None] * inv[None, :].astype(np.float32)
    c["cos"][:] = np.cos(ang).reshape(NT, P, 32).transpose(1, 0, 2).reshape(P, -1)
    c["sin"][:] = np.sin(ang).reshape(NT, P, 32).transpose(1, 0, 2).reshape(P, -1)
    d = p[:, None] + (S - P) - np.arange(S)[None, :]
    n = sum(((d >= 0) & (d <= w) & (d % r == 0)).astype(np.float32) for w, r in ((128, 1), (512, 4), (2048, 16)))
    c["logc"][:] = np.where(n > 0, np.log(np.maximum(n, 1)) / np.float32(SCALE), NEG)
    return np.ascontiguousarray(np.concatenate([c[n] for n in CONST_COLS], axis=1).astype(np.float32))


class Tally:

    def __init__(self, nc, ctx, name):
        self.sem, self.n = ctx.enter_context(nc.semaphore(name)), 0

    def inc(self, ins, by=1):
        ins.then_inc(self.sem, by)
        self.n += by
        return self.n


class Core:

    def __init__(self, nc, io, ctx):
        self.nc, self.io, self.ctx, self.in_use = nc, io, ctx, []
        self.small = ctx.enter_context(nc.sbuf_tensor("const_small", [P, CONST_AT["cos"]], F32))
        self.const_in = ctx.enter_context(nc.semaphore("const_in"))
        self.dve_chain = Tally(nc, ctx, "dve_chain")
        self.act_chain = Tally(nc, ctx, "act_chain")
        self.pool_chain = Tally(nc, ctx, "pool_chain")
        self.ring = ctx.enter_context(nc.sbuf_tensor("weight_ring", [P, 2, KC * BANK], F32))
        self.panel_landed = [ctx.enter_context(nc.semaphore(f"panel_landed{b}")) for b in range(2)]
        self.n_panels = 0
        self.landed_total, self.landed_target = [0, 0], {}

    def sem(self, name):
        self.in_use.append(self.nc.alloc_semaphore(name=name))
        return self.in_use[-1]

    def retire_semaphores(self):
        self.nc.clear_and_free_semaphores(self.in_use)
        self.in_use = []
        self.nc.all_engine_barrier()

    def const(self, name):
        return self.small[:, CONST_AT[name]:CONST_AT[name] + CONST_COLS[name]]

    def const_dram(self, name):
        return self.io["consts"][:, CONST_AT[name]:CONST_AT[name] + CONST_COLS[name]]

    def vstep(self, dve, ins):
        dve.wait_ge(self.dve_chain.sem, self.dve_chain.inc(ins))

    def astep(self, act, ins):
        act.wait_ge(self.act_chain.sem, self.act_chain.inc(ins))

    def gstep(self, pool, ins):
        pool.wait_ge(self.pool_chain.sem, self.pool_chain.inc(ins))


def load_constants(c):
    nc = c.nc
    with nc.Block() as block:
        @block.sync
        def _(sp):
            sp.dma_start(c.small[:, :], c.io["consts"][:, 0:CONST_AT["cos"]]).then_inc(c.const_in, 16)
            sp.wait_ge(c.const_in, 16)


def column_of(gain):
    return gain.rearrange("(p k) -> p k", k=KC)


def norm_transposed(c, tag, src, gain, hT, n_tiles=NT, keep=None, gain_row=None):
    nc = c.nc
    src_t = src.rearrange("(t p) d -> t p d", p=P)
    with ExitStack() as s:
        x = s.enter_context(nc.sbuf_tensor(f"{tag}_x", [P, 2, D], F32))
        sq = s.enter_context(nc.sbuf_tensor(f"{tag}_sq", [P, D], F32))
        g = s.enter_context(nc.sbuf_tensor(f"{tag}_g", [P, KC], F32))
        ss = s.enter_context(nc.sbuf_tensor(f"{tag}_ss", [P, n_tiles], F32))
        rms = s.enter_context(nc.sbuf_tensor(f"{tag}_rms", [P, n_tiles], F32))
        rstd = s.enter_context(nc.sbuf_tensor(f"{tag}_rstd", [P, n_tiles], F32))
        eps = s.enter_context(nc.sbuf_tensor(f"{tag}_eps", [P, 1], F32))
        ps = s.enter_context(nc.psum_tensor(f"{tag}_ps", [P, 2, D], F32))
        g_in, x_in = c.sem(f"{tag}_g_in"), [c.sem(f"{tag}_x_in0"), c.sem(f"{tag}_x_in1")]
        rms_ready, xn_ready = c.sem(f"{tag}_rms"), c.sem(f"{tag}_xn")
        turned, taken = c.sem(f"{tag}_turned"), c.sem(f"{tag}_taken")
        eps_ready = c.sem(f"{tag}_eps")
        if keep is not None:
            keep_t = keep.rearrange("(t p) d -> t p d", p=P)
            grow = s.enter_context(nc.sbuf_tensor(f"{tag}_grow", [P, D], F32))
            xg = s.enter_context(nc.sbuf_tensor(f"{tag}_xg", [P, 2, D], F32))
            xg_ready, xg_out = c.sem(f"{tag}_xg_ready"), [c.sem(f"{tag}_xg_out0"), c.sem(f"{tag}_xg_out1")]
        with nc.Block() as block:
            @block.sync
            def _(sp):
                sp.dma_start(g[:, :], column_of(gain)).then_inc(g_in, 16)
                if keep is not None:
                    sp.dma_start(grow[:, :], gain_row.partition_broadcast(P)).then_inc(g_in, 16)
                for t in range(n_tiles):
                    if t >= 2:
                        sp.wait_ge(turned, t - 1)
                        if keep is not None:
                            sp.wait_ge(xg_ready, t - 1)
                    sp.dma_start(x[:, t % 2, :], src_t[t]).then_inc(x_in[t % 2], 16)
                    if keep is not None and t >= 1:
                        sp.wait_ge(xg_ready, t)
                        sp.dma_start(keep_t[t - 1], xg[:, (t - 1) % 2, :]).then_inc(xg_out[(t - 1) % 2], 16)
                if keep is not None:
                    t = n_tiles
                    sp.wait_ge(xg_ready, t)
                    sp.dma_start(keep_t[t - 1], xg[:, (t - 1) % 2, :]).then_inc(xg_out[(t - 1) % 2], 16)
                    sp.wait_ge(xg_out[0], 16 * (n_tiles // 2))
                    sp.wait_ge(xg_out[1], 16 * (n_tiles // 2))

            @block.scalar
            def _(act):
                act.wait_ge(eps_ready, 1)
                for t in range(n_tiles):
                    act.wait_ge(x_in[t % 2], 16 * (t // 2 + 1))
                    c.astep(act, nc.scalar.activation(sq[:, :], x[:, t % 2, :], ACT.Square, accum_out=ss[:, t:t + 1]))
                    nc.scalar.activation(rms[:, t:t + 1], ss[:, t:t + 1], ACT.Sqrt, scale=1.0 / D,
                                         bias=eps[:, :]).then_inc(rms_ready, 1)

            @block.vector
            def _(dve):
                nc.vector.memset(eps[:, :], EPS).then_inc(eps_ready, 1)

                def evacuate(t):
                    dve.wait_ge(turned, t + 1)
                    nc.vector.tensor_tensor(hT[:, :, t * P:(t + 1) * P],
                                            ps[:, t % 2, :].rearrange("p (k n) -> p k n", k=KC),
                                            g[:, :].unsqueeze(2).to_broadcast([P, KC, P]), ALU.mult).then_inc(taken, 1)

                dve.wait_ge(g_in, 16 if keep is None else 32)
                for t in range(n_tiles):
                    dve.wait_ge(rms_ready, t + 1)
                    c.vstep(dve, nc.vector.reciprocal(rstd[:, t:t + 1], rms[:, t:t + 1]))
                    ins = nc.vector.tensor_scalar(x[:, t % 2, :], x[:, t % 2, :], rstd[:, t:t + 1], None, ALU.mult)
                    ins.then_inc(xn_ready, 1)
                    if keep is not None:
                        dve.wait_ge(xn_ready, t + 1)
                        if t >= 2:
                            dve.wait_ge(xg_out[t % 2], 16 * (t // 2))
                        nc.vector.tensor_tensor(xg[:, t % 2, :], x[:, t % 2, :], grow[:, :],
                                                ALU.mult).then_inc(xg_ready, 1)
                    if t >= 1:
                        evacuate(t - 1)
                evacuate(n_tiles - 1)

            @block.tensor
            def _(pe):
                for t in range(n_tiles):
                    pe.wait_ge(xn_ready, t + 1)
                    if t >= 2:
                        pe.wait_ge(taken, t - 1)
                    for k in range(KC):
                        ins = pe.transpose(ps[:, t % 2, k * P:(k + 1) * P], x[:, t % 2, k::KC], c.const("ident"))
                    ins.then_inc(turned, 1)


class Panels:

    def __init__(self, c, sources):
        self.c, self.base, self.sources = c, c.n_panels, sources
        c.n_panels += len(sources)

    def view(self, i, w):
        return self.c.ring[:, (self.base + i) % 2, 0:KC * w].rearrange("p (k n) -> p k n", k=KC)

    def arrived(self, pe, i):
        n = self.base + i
        pe.wait_ge(self.c.panel_landed[n % 2], self.c.landed_target[n])


def panels_of(c, list_of):
    p = Panels(c, list_of)
    for i, (pieces, w) in enumerate(list_of):
        n = p.base + i
        c.landed_total[n % 2] += 16 * len(pieces)
        c.landed_target[n] = c.landed_total[n % 2]
    return p


def load_panels(c, sp, p, done=None, groups=()):
    for i, (pieces, w) in enumerate(p.sources):
        n = p.base + i
        if i >= 2:
            sp.wait_ge(done, 1 + max(g for g, group in enumerate(groups) if group[0] == i - 2))
        at = 0
        for src in pieces:
            wide = src.shape[-1]
            sp.dma_start(p.view(i, w)[:, :, at:at + wide], src).then_inc(c.panel_landed[n % 2], 16)
            at += wide


def by_rows(w, a, b):
    return w.rearrange("(p k) n -> p k n", k=KC)[:, :, a:b]


def by_chunks(w, a, b):
    return w.rearrange("(k p) n -> p k n", p=P)[:, :, a:b]


def matmul_groups(pe, c, panels, groups, hT, ps, n_banks, done, freed):
    for g, (i, kind, a, w, t) in enumerate(groups):
        if g == 0 or groups[g - 1][0] != i:
            panels.arrived(pe, i)
        if g >= n_banks:
            pe.wait_ge(freed, g - n_banks + 1)
        view = panels.view(i, panels.sources[i][1])
        hT_i = hT(i) if callable(hT) else hT
        for k in range(KC):
            if kind == "rows":
                ins = pe.matmul(ps[:, g % n_banks, 0:w], hT_i[:, k, t * P:(t + 1) * P], view[:, k, a:a + w],
                                start=(k == 0), stop=(k == KC - 1))
            else:
                ins = pe.matmul(ps[:, g % n_banks, 0:w], view[:, k, a:a + P], hT_i[:, k, t * w:(t + 1) * w],
                                start=(k == 0), stop=(k == KC - 1))
        ins.then_inc(done, 1)
        yield g


def project_first(c, hT, qkT, v, mixT):
    nc, io = c.nc, c.io
    w = io["w_in"]
    qk_cols, v_at, g_at, c_at = 2 * AW, 2 * AW, 3 * AW, 4 * AW
    sources, groups = [], []
    for i in range(qk_cols // BANK):
        sources.append(([by_rows(w, i * BANK, (i + 1) * BANK)], BANK))
        groups += [(i, "rows", 0, BANK, t) for t in range(NT)]
    n_qk = len(groups)
    for a, wd in ((0, BANK), (BANK, AW - BANK)):
        groups += [(len(sources), "rows", 0, wd, t) for t in range(NT)]
        sources.append(([by_rows(w, v_at + a, v_at + a + wd)], wd))
    n_v = len(groups)
    gate_of = {}
    for a, wd in ((0, BANK), (BANK, AW - BANK)):
        for sub in range(wd // P):
            for half in range(2):
                gate_of[len(groups)] = (a // P + sub, half)
                groups.append((len(sources), "cols", sub * P, BANK, half))
        sources.append(([by_rows(w, g_at + a, g_at + a + wd)], wd))
    n_g = len(groups)
    for j in range(CW // P):
        for half in range(2):
            for kind in range(4):
                groups.append((len(sources), "cols", kind * P, BANK, half))
        sources.append(([by_rows(w, c_at + kind * CW + j * P, c_at + kind * CW + (j + 1) * P)
                         for kind in range(4)], BANK))
    panels = panels_of(c, sources)
    NB = 4
    with ExitStack() as s:
        cs = s.enter_context(nc.sbuf_tensor("rope_cs", [P, 2 * NT * 32], F32))
        rot = s.enter_context(nc.sbuf_tensor("rope_rot", [P, 2, BANK], F32))
        rb = s.enter_context(nc.sbuf_tensor("rope_b", [P, BANK], F32))
        cw = s.enter_context(nc.sbuf_tensor("conv_taps", [P, 3, CW // P], F32))
        cz = s.enter_context(nc.sbuf_tensor("conv_z", [P, 4, S], F32))
        cu = s.enter_context(nc.sbuf_tensor("conv_u", [P, S + 2], F32))
        ps = s.enter_context(nc.psum_tensor("p1_ps", [P, NB, BANK], F32))
        pt = s.enter_context(nc.psum_tensor("p1_pt", [P, 2, BANK], F32))
        tables_in = c.sem("rope_tables_in")
        done, freed = c.sem("p1_done"), c.sem("p1_freed")
        rot_ready, rot_turned, rot_kept = c.sem("rot_ready"), c.sem("rot_turned"), c.sem("rot_kept")
        conv_done = c.sem("conv_done")
        cos = cs[:, 0:NT * 32].rearrange("p (t f) -> p t f", t=NT)
        sin = cs[:, NT * 32:2 * NT * 32].rearrange("p (t f) -> p t f", t=NT)
        NHB = BANK // HD
        with nc.Block() as block:
            @block.sync
            def _(sp):
                load_panels(c, sp, panels, done, groups)

            @block.gpsimd
            def _(pool):
                a = CONST_AT["cos"]
                pool.dma_start(cs[:, :], io["consts"][:, a:a + 2 * NT * 32]).then_inc(tables_in, 16)
                for j in range(CW // P):
                    with nc.allow_non_contiguous_dma(reason="a few hundred taps, once"):
                        pool.dma_start(cw[:, :, j:j + 1],
                                       io["conv_w"][:, j * P:(j + 1) * P].rearrange("j (c o) -> c j o", o=1)
                                       ).then_inc(tables_in, 16)

            @block.tensor
            def _(pe):
                def turn(g):
                    pe.wait_ge(rot_ready, g + 1)
                    if g >= 2:
                        pe.wait_ge(rot_kept, g - 1)
                    for j in range(BANK // P):
                        ins = pe.transpose(pt[:, g % 2, j * P:(j + 1) * P], rot[:, g % 2, j * P:(j + 1) * P],
                                           c.const("ident"))
                    ins.then_inc(rot_turned, 1)

                for g in matmul_groups(pe, c, panels, groups, hT, ps, NB, done, freed):
                    if 1 <= g <= n_qk:
                        turn(g - 1)

            @block.vector
            def _(dve):
                dve.wait_ge(tables_in, 16 * (1 + CW // P))
                for g in range(n_qk):
                    t = g % NT
                    z = ps[:, g % NB, :].rearrange("p (h a f) -> p h a f", h=NHB, a=2)
                    r = rot[:, g % 2, :].rearrange("p (h a f) -> p h a f", h=NHB, a=2)
                    b = rb[:, :].rearrange("p (h a f) -> p h a f", h=NHB, a=2)
                    cb = cos[:, t, :].unsqueeze(1).to_broadcast([P, NHB, 32])
                    sb = sin[:, t, :].unsqueeze(1).to_broadcast([P, NHB, 32])
                    dve.wait_ge(done, g + 1)
                    if g >= 2:
                        dve.wait_ge(rot_turned, g - 1)
                    nc.vector.tensor_tensor(r[:, :, 0, :], z[:, :, 0, :], cb, ALU.mult)
                    nc.vector.tensor_tensor(r[:, :, 1, :], z[:, :, 1, :], cb, ALU.mult)
                    nc.vector.tensor_tensor(b[:, :, 0, :], z[:, :, 1, :], sb, ALU.mult)
                    nc.vector.tensor_tensor(b[:, :, 1, :], z[:, :, 0, :], sb, ALU.mult).then_inc(freed, 1)
                    dve.wait_ge(freed, g + 1)
                    nc.vector.tensor_tensor(r[:, :, 0, :], r[:, :, 0, :], b[:, :, 0, :], ALU.subtract)
                    ins = nc.vector.tensor_tensor(r[:, :, 1, :], r[:, :, 1, :], b[:, :, 1, :], ALU.add)
                    ins.then_inc(rot_ready, 1)
                    dve.wait_ge(rot_ready, g + 1)
                for j in range(CW // P):
                    dve.wait_ge(freed, n_g + 8 * (j + 1))
                    c.vstep(dve, nc.vector.memset(cu[:, 0:2], 0.0))
                    c.vstep(dve, nc.vector.tensor_tensor(cu[:, 2:S + 2], cz[:, 2, :], cz[:, 0, :], ALU.mult))
                    c.vstep(dve, nc.vector.tensor_scalar(cz[:, 0, :], cu[:, 0:S], cw[:, 0, j:j + 1], None, ALU.mult))
                    for tap in (1, 2):
                        c.vstep(dve, nc.vector.scalar_tensor_tensor(cz[:, 0, :], cu[:, tap:tap + S],
                                                                    cw[:, tap, j:j + 1], cz[:, 0, :],
                                                                    ALU.mult, ALU.add))
                    c.vstep(dve, nc.vector.tensor_tensor(cz[:, 0, :], cz[:, 0, :], cz[:, 1, :], ALU.mult))
                    nc.vector.tensor_tensor(mixT[:, AW // P + j, :], cz[:, 0, :], cz[:, 3, :],
                                            ALU.mult).then_inc(conv_done, 1)

            @block.scalar
            def _(act):
                def keep(g):
                    i, t = g // NT, g % NT
                    act.wait_ge(rot_turned, g + 1)
                    nc.scalar.activation(qkT[:, 4 * i:4 * i + 4, t * P:(t + 1) * P],
                                         pt[:, g % 2, :].rearrange("p (j n) -> p j n", j=4),
                                         ACT.Copy).then_inc(rot_kept, 1)

                for g in range(n_qk):
                    keep(g)
                act.wait_ge(freed, n_qk)
                for g in range(n_qk, len(groups)):
                    i, kind, a, wd, t = groups[g]
                    act.wait_ge(done, g + 1)
                    if g < n_v:
                        at = 0 if g - n_qk < NT else BANK
                        ins = nc.scalar.activation(v[:, t, at:at + wd], ps[:, g % NB, 0:wd], ACT.Copy)
                    elif g < n_g:
                        chunk, half = gate_of[g]
                        ins = nc.scalar.activation(mixT[:, chunk, half * BANK:(half + 1) * BANK], ps[:, g % NB, :],
                                                   ACT.Silu)
                    else:
                        j, r = divmod(g - n_g, 8)
                        half, which = divmod(r, 4)
                        if r == 0 and j:
                            act.wait_ge(conv_done, j)
                        ins = nc.scalar.activation(cz[:, which, half * BANK:(half + 1) * BANK], ps[:, g % NB, :],
                                                   ACT.Silu if which == 3 else ACT.Copy)
                    ins.then_inc(freed, 1)


def attention(c, qkT, v, mixT):
    nc, io = c.nc, c.io
    steps = [(hp * 2 + h, hp, a) for hp in range(NH // 2) for a in range(NT) for h in range(2)]
    N = len(steps)
    with ExitStack() as s:
        logc = s.enter_context(nc.sbuf_tensor("logc", [P, S], F32))
        sc = s.enter_context(nc.sbuf_tensor("att_scores", [P, 3, S], F32))
        pT = s.enter_context(nc.sbuf_tensor("att_pT", [P, 2, S], F32))
        mx = s.enter_context(nc.sbuf_tensor("att_max", [P, N], F32))
        nmx = s.enter_context(nc.sbuf_tensor("att_negmax", [P, N], F32))
        den = s.enter_context(nc.sbuf_tensor("att_den", [P, N], F32))
        rden = s.enter_context(nc.sbuf_tensor("att_rden", [P, N], F32))
        on = s.enter_context(nc.sbuf_tensor("att_out", [P, 2, P], F32))
        ps_s = s.enter_context(nc.psum_tensor("att_ps_s", [P, 2, S], F32))
        ps_t = s.enter_context(nc.psum_tensor("att_ps_t", [P, S], F32))
        ps_o = s.enter_context(nc.psum_tensor("att_ps_o", [P, BANK], F32))
        ps_m = s.enter_context(nc.psum_tensor("att_ps_m", [P, BANK], F32))
        logc_in = c.sem("logc_in")
        scored, maxed, expd = c.sem("att_scored"), c.sem("att_maxed"), c.sem("att_expd")
        turned, kept = c.sem("att_turned"), c.sem("att_kept")
        summed, normed = c.sem("att_summed"), c.sem("att_normed")
        pair_turned, pair_kept = c.sem("att_pair_turned"), c.sem("att_pair_kept")
        with nc.Block() as block:
            @block.sync
            def _(sp):
                sp.dma_start(logc[:, :], c.const_dram("logc")).then_inc(logc_in, 16)

            @block.tensor
            def _(pe):
                def scores(i):
                    h, hp, a = steps[i]
                    lo, n = HD * (h % 2), (a + 1) * P
                    if i >= 2:
                        pe.wait_ge(maxed, i - 1)
                    for u in range(0, n, BANK):
                        m = min(BANK, n - u)
                        ins = pe.matmul(ps_s[:, i % 2, u:u + m], qkT[lo:lo + HD, hp, a * P:(a + 1) * P],
                                        qkT[lo:lo + HD, AW // P + hp, u:u + m], start=True, stop=True)
                    ins.then_inc(scored, 1)

                def turn(i):
                    a = steps[i][2]
                    pe.wait_ge(expd, i + 1)
                    if i >= 1:
                        pe.wait_ge(kept, i)
                    for j in range(a + 1):
                        ins = pe.transpose(ps_t[:, j * P:(j + 1) * P], sc[:, i % 3, j * P:(j + 1) * P],
                                           c.const("ident"))
                    ins.then_inc(turned, 1)

                def values(i):
                    h, hp, a = steps[i]
                    pe.wait_ge(kept, i + 1)
                    if i >= 1:
                        pe.wait_ge(normed, i)
                    at = (i % 2) * HD
                    for j in range(a + 1):
                        ins = pe.matmul(ps_o[:, at:at + HD], pT[:, i % 2, j * P:(j + 1) * P],
                                        v[:, j, h * HD:(h + 1) * HD], start=(j == 0), stop=(j == a))
                    ins.then_inc(summed, 1)

                def pair(m):
                    pe.wait_ge(normed, 2 * m + 2)
                    if m >= 1:
                        pe.wait_ge(pair_kept, m)
                    pe.transpose(ps_m[:, 0:P], on[:, m % 2, :], c.const("ident")).then_inc(pair_turned, 1)

                for i in range(N + 4):
                    if i < N:
                        scores(i)
                    if 1 <= i <= N:
                        turn(i - 1)
                    if 2 <= i <= N + 1:
                        values(i - 2)
                    if i >= 4 and i % 2 == 0:
                        pair((i - 4) // 2)

            @block.vector
            def _(dve):
                dve.wait_ge(logc_in, 16)

                def maxes(i):
                    a = steps[i][2]
                    n = (a + 1) * P
                    dve.wait_ge(scored, i + 1)
                    if i >= 3:
                        dve.wait_ge(turned, i - 2)
                    c.vstep(dve, nc.vector.tensor_tensor_reduce(sc[:, i % 3, 0:n], ps_s[:, i % 2, 0:n], logc[:, S - n:S],
                                                                SCALE, NEG, ALU.add, ALU.max, mx[:, i:i + 1]))
                    nc.vector.tensor_scalar(nmx[:, i:i + 1], mx[:, i:i + 1], -1.0, None, ALU.mult).then_inc(maxed, 1)

                def norm(i):
                    h, hp, a = steps[i]
                    m, at = i // 2, (i % 2) * HD
                    dve.wait_ge(expd, i + 1)
                    c.vstep(dve, nc.vector.reciprocal(rden[:, i:i + 1], den[:, i:i + 1]))
                    dve.wait_ge(summed, i + 1)
                    if m >= 2:
                        dve.wait_ge(pair_turned, m - 1)
                    nc.vector.tensor_scalar(on[:, m % 2, at:at + HD], ps_o[:, at:at + HD], rden[:, i:i + 1], None,
                                            ALU.mult).then_inc(normed, 1)

                def gate(m):
                    h, hp, a = steps[2 * m]
                    dve.wait_ge(pair_turned, m + 1)
                    nc.vector.tensor_tensor(mixT[:, hp, a * P:(a + 1) * P], ps_m[:, 0:P], mixT[:, hp, a * P:(a + 1) * P],
                                            ALU.mult).then_inc(pair_kept, 1)

                for i in range(N + 4):
                    if i < N:
                        maxes(i)
                    if 2 <= i <= N + 1:
                        norm(i - 2)
                    if i >= 4 and i % 2 == 0:
                        gate((i - 4) // 2)

            @block.scalar
            def _(act):
                for i in range(N + 1):
                    if i < N:
                        n = (steps[i][2] + 1) * P
                        act.wait_ge(maxed, i + 1)
                        nc.scalar.activation(sc[:, i % 3, 0:n], sc[:, i % 3, 0:n], ACT.Exp, bias=nmx[:, i:i + 1],
                                             accum_out=den[:, i:i + 1]).then_inc(expd, 1)
                    if i >= 1:
                        n = (steps[i - 1][2] + 1) * P
                        act.wait_ge(turned, i)
                        if i >= 3:
                            act.wait_ge(summed, i - 2)
                        nc.scalar.activation(pT[:, (i - 1) % 2, 0:n], ps_t[:, 0:n], ACT.Copy).then_inc(kept, 1)


def project_out(c, tag, mT, w, src, dst, post_gain=None):
    nc = c.nc
    src_t, dst_t = src.rearrange("(t p) d -> t p d", p=P), dst.rearrange("(t p) d -> t p d", p=P)
    panels = panels_of(c, [([by_chunks(w, n * BANK, (n + 1) * BANK)], BANK) for n in range(2)])
    with ExitStack() as s:
        x = s.enter_context(nc.sbuf_tensor(f"{tag}_x", [P, 2, D], F32))
        y = s.enter_context(nc.sbuf_tensor(f"{tag}_y", [P, 2, D], F32))
        if post_gain is not None:
            sq = s.enter_context(nc.sbuf_tensor(f"{tag}_sq", [P, D], F32))
            g = s.enter_context(nc.sbuf_tensor(f"{tag}_g", [P, D], F32))
        ss = s.enter_context(nc.sbuf_tensor(f"{tag}_ss", [P, 3 * NT], F32))
        eps = s.enter_context(nc.sbuf_tensor(f"{tag}_eps", [P, 1], F32))
        ps = s.enter_context(nc.psum_tensor(f"{tag}_ps", [P, 3, D], F32))
        g_in, x_in = c.sem(f"{tag}_g_in"), [c.sem(f"{tag}_x_in{b}") for b in range(2)]
        y_out = [c.sem(f"{tag}_y_out{b}") for b in range(2)]
        done, rms_ready, y_ready = c.sem(f"{tag}_done"), c.sem(f"{tag}_rms"), c.sem(f"{tag}_y_ready")
        eps_ready = c.sem(f"{tag}_eps_ready")
        with nc.Block() as block:
            @block.sync
            def _(sp):
                load_panels(c, sp, panels)
                if post_gain is not None:
                    sp.dma_start(g[:, :], post_gain.partition_broadcast(P)).then_inc(g_in, 16)
                for t in range(NT + 1):
                    if t < NT:
                        if t >= 2:
                            sp.wait_ge(y_ready, t - 1)
                        sp.dma_start(x[:, t % 2, :], src_t[t]).then_inc(x_in[t % 2], 16)
                    if t >= 1:
                        sp.wait_ge(y_ready, t)
                        sp.dma_start(dst_t[t - 1], y[:, (t - 1) % 2, :]).then_inc(y_out[(t - 1) % 2], 16)
                for b in range(2):
                    sp.wait_ge(y_out[b], 16 * NT // 2)

            @block.tensor
            def _(pe):
                for t in range(NT):
                    if t >= 3:
                        pe.wait_ge(y_ready, t - 2)
                    for n in range(2):
                        if t == 0:
                            panels.arrived(pe, n)
                        for k in range(KC):
                            ins = pe.matmul(ps[:, t % 3, n * BANK:(n + 1) * BANK], mT[:, k, t * P:(t + 1) * P],
                                            panels.view(n, BANK)[:, k, :], start=(k == 0), stop=(k == KC - 1))
                    ins.then_inc(done, 1)

            if post_gain is not None:
                @block.scalar
                def _(act):
                    act.wait_ge(eps_ready, 1)
                    for t in range(NT):
                        act.wait_ge(done, t + 1)
                        c.astep(act, nc.scalar.activation(sq[:, :], ps[:, t % 3, :], ACT.Square,
                                                          accum_out=ss[:, t:t + 1]))
                        nc.scalar.activation(ss[:, NT + t:NT + t + 1], ss[:, t:t + 1], ACT.Sqrt, scale=1.0 / D,
                                             bias=eps[:, :]).then_inc(rms_ready, 1)

            @block.vector
            def _(dve):
                if post_gain is not None:
                    nc.vector.memset(eps[:, :], EPS).then_inc(eps_ready, 1)
                    dve.wait_ge(g_in, 16)
                for t in range(NT):
                    dve.wait_ge(done, t + 1)
                    if t >= 2:
                        dve.wait_ge(y_out[t % 2], 16 * (t // 2))
                    dve.wait_ge(x_in[t % 2], 16 * (t // 2 + 1))
                    yt = y[:, t % 2, :]
                    if post_gain is None:
                        nc.vector.tensor_tensor(yt, ps[:, t % 3, :], x[:, t % 2, :], ALU.add).then_inc(y_ready, 1)
                    else:
                        dve.wait_ge(rms_ready, t + 1)
                        r = ss[:, 2 * NT + t:2 * NT + t + 1]
                        c.vstep(dve, nc.vector.reciprocal(r, ss[:, NT + t:NT + t + 1]))
                        c.vstep(dve, nc.vector.scalar_tensor_tensor(yt, ps[:, t % 3, :], r, g[:, :], ALU.mult, ALU.mult))
                        nc.vector.tensor_tensor(yt, yt, x[:, t % 2, :], ALU.add).then_inc(y_ready, 1)


def first_block(c, x, x1):
    nc, io = c.nc, c.io
    with ExitStack() as s:
        mixT = s.enter_context(nc.sbuf_tensor("mixT", [P, KC, S], F32))
        with ExitStack() as s2:
            qkT = s2.enter_context(nc.sbuf_tensor("qkT", [P, 2 * AW // P, S], F32))
            v = s2.enter_context(nc.sbuf_tensor("v", [P, NT, AW], F32))
            with ExitStack() as s3:
                hT = s3.enter_context(nc.sbuf_tensor("hT", [P, KC, S], F32))
                norm_transposed(c, "n1", x, io["norm_pre_g"], hT)
                project_first(c, hT, qkT, v, mixT)
            attention(c, qkT, v, mixT)
        project_out(c, "o1", mixT, io["w_out"], x, x1, post_gain=io["norm_post_g"])


IF_AT, U_AT, SV_AT, GA_AT, GB_AT = 4 * D, 4 * D + 8, 5 * D + 8, 6 * D + 8, 7 * D + 8
V_AT, O_AT = 2 * D, 3 * D


def row_panels(w, at, panel0):
    sources = [([by_rows(w, at + n * BANK, at + (n + 1) * BANK)], BANK) for n in range(D // BANK)]
    groups = [(panel0 + n, "rows", 0, BANK, t) for n in range(D // BANK) for t in range(NT)]
    return sources, groups


def spatial_gate(c, hT, yb_dram):
    nc, io = c.nc, c.io
    w = io["w_in_2"]
    sources, groups = [], []
    for at in (SV_AT, U_AT, GB_AT):
        a, b = row_panels(w, at, len(sources))
        sources, groups = sources + a, groups + b
    panels = panels_of(c, sources)
    per = len(groups) // 3
    NB = 4
    yb_t = yb_dram.rearrange("(t p) d -> t p d", p=P)
    with ExitStack() as s:
        sv = s.enter_context(nc.sbuf_tensor("sgu_v", [P, NT, D], F32))
        u = s.enter_context(nc.sbuf_tensor("sgu_u", [P, NT, D], F32))
        gb = s.enter_context(nc.sbuf_tensor("sgu_gate", [P, NB, BANK], F32))
        gbias = s.enter_context(nc.sbuf_tensor("sgu_gate_bias", [P, D], F32))
        gain = s.enter_context(nc.sbuf_tensor("sgu_gain", [P, D], F32))
        sq = s.enter_context(nc.sbuf_tensor("sgu_sq", [P, D], F32))
        ws = s.enter_context(nc.sbuf_tensor("sgu_ws", [P, 8, P], F32))
        bs = s.enter_context(nc.sbuf_tensor("sgu_bs", [P, 8], F32))
        ss = s.enter_context(nc.sbuf_tensor("sgu_ss", [P, 2 * NT], F32))
        eps = s.enter_context(nc.sbuf_tensor("sgu_eps", [P, 1], F32))
        ps = s.enter_context(nc.psum_tensor("sgu_ps", [P, NB, BANK], F32))
        pm = s.enter_context(nc.psum_tensor("sgu_pm", [P, 2, BANK], F32))
        small_in, done, freed = c.sem("sgu_small_in"), c.sem("sgu_done"), c.sem("sgu_freed")
        eps_ready, ws_ready, v_ready = c.sem("sgu_eps_ready"), c.sem("sgu_ws_ready"), c.sem("sgu_v_ready")
        rms_ready, biased, gated = c.sem("sgu_rms"), c.sem("sgu_biased"), c.sem("sgu_gated")
        gate_ready, mixed, y_ready = c.sem("sgu_gate_ready"), c.sem("sgu_mixed"), c.sem("sgu_y_ready")
        y_out = c.sem("sgu_y_out")
        with nc.Block() as block:
            @block.sync
            def _(sp):
                load_panels(c, sp, panels, done, groups)
                sp.wait_ge(y_ready, 16)
                sp.dma_start(yb_t.rearrange("t p d -> p t d"), u[:, :, :]).then_inc(y_out, 16)
                sp.wait_ge(y_out, 16)

            @block.gpsimd
            def _(pool):
                pool.dma_start(gain[:, :], io["sgu_norm_g_2"].partition_broadcast(P)).then_inc(small_in, 16)
                pool.dma_start(gbias[:, :], io["b_gate_2"][D:2 * D].partition_broadcast(P)).then_inc(small_in, 16)
                pool.dma_start(ws[:, :, :], io["w_s_T"].rearrange("g s t -> s g t")).then_inc(small_in, 16)
                with nc.allow_non_contiguous_dma(reason="1024 biases, once"):
                    pool.dma_start(bs[:, :].unsqueeze(2), io["b_s_2"].rearrange("g (t o) -> t g o", o=1)
                                   ).then_inc(small_in, 16)

            @block.tensor
            def _(pe):
                for g in matmul_groups(pe, c, panels, groups, hT, ps, NB, done, freed):
                    pass
                pe.wait_ge(ws_ready, 1)
                pe.wait_ge(v_ready, NT)
                for n in range(16):
                    g, half = divmod(n, 2)
                    if n >= 2:
                        pe.wait_ge(y_ready, n - 1)
                    pe.matmul(pm[:, n % 2, :].rearrange("p (c d) -> p c d", c=4), ws[:, g, :],
                              sv[:, 4 * half:4 * half + 4, g * P:(g + 1) * P], start=True, stop=True
                              ).then_inc(mixed, 1)

            @block.scalar
            def _(act):
                act.wait_ge(eps_ready, 1)
                for g, (i, kind, a, wd, t) in enumerate(groups):
                    n = i % 2
                    if g < 2 * per:
                        act.wait_ge(done, g + 1)
                        dst = (sv if g < per else u)[:, t, n * BANK:(n + 1) * BANK]
                        nc.scalar.activation(dst, ps[:, g % NB, :], ACT.Gelu_apprx_tanh).then_inc(freed, 1)
                    else:
                        act.wait_ge(biased, g - 2 * per + 1)
                        nc.scalar.activation(gb[:, g % NB, :], gb[:, g % NB, :], ACT.Sigmoid).then_inc(gate_ready, 1)
                    if g == per:
                        act.wait_ge(freed, per)
                        for t in range(NT):
                            c.astep(act, nc.scalar.activation(sq[:, :], sv[:, t, :], ACT.Square,
                                                              accum_out=ss[:, t:t + 1]))
                        nc.scalar.activation(ss[:, NT:], ss[:, 0:NT], ACT.Sqrt, scale=1.0 / D,
                                             bias=eps[:, :]).then_inc(rms_ready, 1)

            @block.vector
            def _(dve):
                nc.vector.memset(eps[:, :], EPS).then_inc(eps_ready, 1)
                dve.wait_ge(small_in, 64)
                nc.vector.tensor_tensor(ws[:, :, :], ws[:, :, :], c.const("causal").unsqueeze(1).to_broadcast([P, 8, P]),
                                        ALU.mult).then_inc(ws_ready, 1)
                dve.wait_ge(rms_ready, 1)
                c.vstep(dve, nc.vector.reciprocal(ss[:, 0:NT], ss[:, NT:]))
                for t in range(NT):
                    nc.vector.scalar_tensor_tensor(sv[:, t, :], sv[:, t, :], ss[:, t:t + 1], gain[:, :],
                                                   ALU.mult, ALU.mult).then_inc(v_ready, 1)
                for g in range(2 * per, len(groups) + 1):
                    if g < len(groups):
                        n = groups[g][0] % 2
                        dve.wait_ge(done, g + 1)
                        if g - 2 * per >= NB:
                            dve.wait_ge(gated, g - 2 * per - NB + 1)
                        dve.wait_ge(freed, g)
                        nc.vector.tensor_tensor(gb[:, g % NB, :], ps[:, g % NB, :], gbias[:, n * BANK:(n + 1) * BANK],
                                                ALU.add).then_inc(freed, 1)
                        dve.wait_ge(freed, g + 1)
                        nc.vector.tensor_copy(ss[:, 0:1], ss[:, 0:1]).then_inc(biased, 1)
                    if g > 2 * per:
                        i, kind, a, wd, t = groups[g - 1]
                        n = i % 2
                        dve.wait_ge(gate_ready, g - 2 * per)
                        uu = u[:, t, n * BANK:(n + 1) * BANK]
                        nc.vector.tensor_tensor(uu, uu, gb[:, (g - 1) % NB, :], ALU.mult).then_inc(gated, 1)
                dve.wait_ge(gated, per)
                for n in range(16):
                    g, half = divmod(n, 2)
                    dve.wait_ge(mixed, n + 1)
                    uu = u[:, 4 * half:4 * half + 4, g * P:(g + 1) * P]
                    nc.vector.scalar_tensor_tensor(uu, pm[:, n % 2, :].rearrange("p (c d) -> p c d", c=4),
                                                   bs[:, g:g + 1], uu, ALU.add, ALU.mult).then_inc(y_ready, 1)


def output_gate(c, hT, og_dram):
    nc, io = c.nc, c.io
    w = io["w_in_2"]
    sources, groups = [], []
    for n in range(D // BANK):
        for at in (O_AT, GA_AT):
            groups += [(len(sources), "rows", 0, BANK, t) for t in range(NT)]
            sources.append(([by_rows(w, at + n * BANK, at + (n + 1) * BANK)], BANK))
    panels = panels_of(c, sources)
    NB = 4
    with ExitStack() as s:
        og = s.enter_context(nc.sbuf_tensor("og", [P, NT, D], F32))
        ga = s.enter_context(nc.sbuf_tensor("og_gate", [P, NB, BANK], F32))
        gbias = s.enter_context(nc.sbuf_tensor("og_bias", [P, D], F32))
        ps = s.enter_context(nc.psum_tensor("og_ps", [P, NB, BANK], F32))
        bias_in, done, freed = c.sem("og_bias_in"), c.sem("og_done"), c.sem("og_freed")
        biased, gate_ready, gated, out = c.sem("og_biased"), c.sem("og_gate_ready"), c.sem("og_gated"), c.sem("og_out")
        with nc.Block() as block:
            @block.sync
            def _(sp):
                sp.dma_start(gbias[:, :], io["b_gate_2"][0:D].partition_broadcast(P)).then_inc(bias_in, 16)
                load_panels(c, sp, panels, done, groups)
                sp.wait_ge(gated, len(groups) // 2)
                sp.dma_start(og_dram.rearrange("(t p) d -> p t d", p=P), og[:, :, :]).then_inc(out, 16)
                sp.wait_ge(out, 16)

            @block.tensor
            def _(pe):
                for g in matmul_groups(pe, c, panels, groups, hT, ps, NB, done, freed):
                    pass

            @block.scalar
            def _(act):
                gates = 0
                for g, (i, kind, a, wd, t) in enumerate(groups):
                    if i % 2 == 0:
                        act.wait_ge(done, g + 1)
                        act.wait_ge(freed, g)
                        n = i // 2
                        nc.scalar.activation(og[:, t, n * BANK:(n + 1) * BANK], ps[:, g % NB, :],
                                             ACT.Sigmoid).then_inc(freed, 1)
                    else:
                        gates += 1
                        act.wait_ge(biased, gates)
                        nc.scalar.activation(ga[:, g % NB, :], ga[:, g % NB, :], ACT.Sigmoid).then_inc(gate_ready, 1)

            @block.vector
            def _(dve):
                dve.wait_ge(bias_in, 16)
                gates = 0
                for g, (i, kind, a, wd, t) in enumerate(groups):
                    if i % 2 == 0:
                        continue
                    n = i // 2
                    dve.wait_ge(done, g + 1)
                    dve.wait_ge(freed, g)
                    nc.vector.tensor_tensor(ga[:, g % NB, :], ps[:, g % NB, :], gbias[:, n * BANK:(n + 1) * BANK],
                                            ALU.add).then_inc(freed, 1)
                    dve.wait_ge(freed, g + 1)
                    nc.vector.tensor_copy(gbias[:, 0:1], gbias[:, 0:1]).then_inc(biased, 1)
                    gates += 1
                    dve.wait_ge(gate_ready, gates)
                    oo = og[:, t, n * BANK:(n + 1) * BANK]
                    nc.vector.tensor_tensor(oo, oo, ga[:, g % NB, :], ALU.mult).then_inc(gated, 1)


def project_qkv(c, hT, qkT, v, rows):
    nc, io = c.nc, c.io
    w = io["w_in_2"]
    sources, groups = row_panels(w, V_AT, 0)
    n_v = len(groups)
    for n in range(2 * D // BANK):
        for sub in range(BANK // P):
            groups += [(len(sources), "cols", sub * P, BANK, half) for half in range(2)]
        sources.append(([by_rows(w, n * BANK, (n + 1) * BANK)], BANK))
    panels = panels_of(c, sources)
    NB, NSUB, TAPS = 4, 2 * D // P, 4
    with ExitStack() as s:
        z = s.enter_context(nc.sbuf_tensor("qk_z", [P, 2, S + 3], F32))
        y = s.enter_context(nc.sbuf_tensor("qk_y", [P, 2, S], F32))
        cw = s.enter_context(nc.sbuf_tensor("qk_taps", [P, TAPS, NSUB], F32))
        cb = s.enter_context(nc.sbuf_tensor("qk_bias", [P, NSUB], F32))
        wif = s.enter_context(nc.sbuf_tensor("w_if", [P, KC, 36], F32))
        bif = s.enter_context(nc.sbuf_tensor("b_if", [36, 1], F32))
        ps = s.enter_context(nc.psum_tensor("qkv_ps", [P, NB, BANK], F32))
        pif = s.enter_context(nc.psum_tensor("if_ps", [P, 2, BANK], F32))
        small_in, if_in, wif_zero = c.sem("qkv_small_in"), c.sem("if_in"), c.sem("wif_zero")
        done, freed, if_done = c.sem("qkv_done"), c.sem("qkv_freed"), c.sem("if_done")
        pads, conv_ready, silu_done = c.sem("qk_pads"), c.sem("qk_conv_ready"), c.sem("qk_silu_done")
        with nc.Block() as block:
            @block.sync
            def _(sp):
                load_panels(c, sp, panels, done, groups)

            @block.gpsimd
            def _(pool):
                nc.gpsimd.memset(wif[:, :, :], 0.0).then_inc(wif_zero, 1)
                pool.wait_ge(wif_zero, 1)
                for k in range(2):
                    at = IF_AT + 4 * k
                    with nc.allow_non_contiguous_dma(reason="8 columns, once"):
                        pool.dma_start(wif[:, :, 32 * k:32 * k + 4], by_rows(w, at, at + 4)).then_inc(if_in, 16)
                        pool.dma_start(bif[32 * k:32 * k + 4, :],
                                       io["b_if_2"][4 * k:4 * k + 4].rearrange("(h o) -> h o", o=1)).then_inc(if_in, 16)
                with nc.allow_non_contiguous_dma(reason="the taps, once"):
                    for j in range(TAPS):
                        pool.dma_start(cw[:, j, :].unsqueeze(2), io["conv_w_2"][j].rearrange("(k p o) -> p k o", p=P, o=1)
                                       ).then_inc(small_in, 16)
                    pool.dma_start(cb[:, :].unsqueeze(2), io["conv_b_2"].rearrange("(k p o) -> p k o", p=P, o=1)
                                   ).then_inc(small_in, 16)

            @block.tensor
            def _(pe):
                pe.wait_ge(if_in, 64)
                for half in range(2):
                    for k in range(KC):
                        ins = pe.matmul(pif[0:36, half, :], wif[:, k, :], hT[:, k, half * BANK:(half + 1) * BANK],
                                        start=(k == 0), stop=(k == KC - 1))
                ins.then_inc(if_done, 1)
                for g in matmul_groups(pe, c, panels, groups, hT, ps, NB, done, freed):
                    pass

            @block.scalar
            def _(act):
                act.wait_ge(small_in, 16 * (TAPS + 1))
                act.wait_ge(pads, 1)

                def silu(j):
                    act.wait_ge(conv_ready, j + 1)
                    nc.scalar.activation(qkT[:, j, :], y[:, j % 2, :], ACT.Silu, bias=cb[:, j:j + 1]
                                         ).then_inc(silu_done, 1)

                for g, (i, kind, a, wd, t) in enumerate(groups):
                    act.wait_ge(done, g + 1)
                    if g < n_v:
                        n = i
                        dst = v[:, t, 2 * n:2 * n + 2, 0:MD]
                        nc.scalar.activation(dst, ps[:, g % NB, :].rearrange("p (h d) -> p h d", h=2),
                                             ACT.Copy).then_inc(freed, 1)
                    else:
                        j, half = divmod(g - n_v, 2)
                        if j >= 2:
                            act.wait_ge(conv_ready, j - 1)
                        nc.scalar.activation(z[:, j % 2, 3 + half * BANK:3 + (half + 1) * BANK], ps[:, g % NB, :],
                                             ACT.Copy).then_inc(freed, 1)
                        if half == 1 and j >= 1:
                            silu(j - 1)
                silu(NSUB - 1)

            @block.vector
            def _(dve):
                nc.vector.memset(z[:, :, 0:3], 0.0)
                nc.vector.memset(v[:, :, :, MD:MV], 1.0).then_inc(pads, 1)
                dve.wait_ge(pads, 1)
                dve.wait_ge(small_in, 16 * (TAPS + 1))
                dve.wait_ge(if_done, 1)
                nc.vector.tensor_scalar(rows[:, 0, :], pif[0:MH, :, :].rearrange("p a n -> p (a n)"), bif[0:MH, :],
                                        None, ALU.add)
                nc.vector.tensor_scalar(rows[:, 1, :], pif[32:32 + MH, :, :].rearrange("p a n -> p (a n)"),
                                        bif[32:32 + MH, :], None, ALU.add)
                for j in range(NSUB):
                    dve.wait_ge(freed, n_v + 2 * (j + 1))
                    if j >= 2:
                        dve.wait_ge(silu_done, j - 1)
                    zz, yy = z[:, j % 2, :], y[:, j % 2, :]
                    c.vstep(dve, nc.vector.tensor_scalar(yy, zz[:, 0:S], cw[:, 0, j:j + 1], None, ALU.mult))
                    for tap in range(1, TAPS):
                        ins = nc.vector.scalar_tensor_tensor(yy, zz[:, tap:tap + S], cw[:, tap, j:j + 1], yy,
                                                             ALU.mult, ALU.add)
                        if tap < TAPS - 1:
                            c.vstep(dve, ins)
                    ins.then_inc(conv_ready, 1)


R_I, R_F, R_B, R_A, R_M = range(5)
R_WS, R_IW, R_T, R_FLOOR = R_I, R_F, R_B, R_B


def mlstm_rows(c, rows, cols, decay):
    nc = c.nc
    with ExitStack() as s:
        m = s.enter_context(nc.sbuf_tensor("ml_m", [MH, NT + 1], F32))
        dec = s.enter_context(nc.sbuf_tensor("ml_decay", [MH, NT], F32))
        pc = s.enter_context(nc.psum_tensor("ml_pc", [P, NT, 4, MH], F32))
        pd = s.enter_context(nc.psum_tensor("ml_pd", [P, MH, NT], F32))
        absd, expd, lnd = c.sem("ml_absd"), c.sem("ml_expd"), c.sem("ml_lnd")
        diffs, weights, turned = c.sem("ml_diffs"), c.sem("ml_weights"), c.sem("ml_turned")

        def chunks(r):
            return rows[:, r, :].rearrange("p (c n) -> p c n", c=NT)

        with nc.Block() as block:
            @block.vector
            def _(dve):
                nc.vector.scalar_tensor_tensor(rows[:, R_T, :], rows[:, R_F, :], -1.0, rows[:, R_F, :],
                                               ALU.mult, ALU.max).then_inc(absd, 1)
                dve.wait_ge(expd, 1)
                nc.vector.tensor_scalar(rows[:, R_T, :], rows[:, R_T, :], 1.0, None, ALU.add).then_inc(absd, 1)
                dve.wait_ge(lnd, 1)
                c.vstep(dve, nc.vector.scalar_tensor_tensor(rows[:, R_F, :], rows[:, R_F, :], 0.0, rows[:, R_T, :],
                                                            ALU.min, ALU.subtract))
                one = c.const("ones")[0:MH, :]
                for t in range(NT):
                    sl = slice(t * P, (t + 1) * P)
                    ins = nc.vector.tensor_tensor_scan(rows[:, R_B, sl], one, rows[:, R_F, sl], 0.0, ALU.mult, ALU.add)
                c.vstep(dve, ins)
                nc.vector.memset(m[:, 0:1], 0.0)
                c.vstep(dve, nc.vector.tensor_tensor(rows[:, R_A, :], rows[:, R_I, :], rows[:, R_B, :], ALU.subtract))
                for t in range(NT):
                    sl = slice(t * P, (t + 1) * P)
                    last = slice((t + 1) * P - 1, (t + 1) * P)
                    c.vstep(dve, nc.vector.tensor_tensor_scan(rows[:, R_M, sl], one, rows[:, R_A, sl], m[:, t:t + 1],
                                                              ALU.mult, ALU.max))
                    c.vstep(dve, nc.vector.tensor_tensor(m[:, t + 1:t + 2], rows[:, R_B, last], rows[:, R_M, last],
                                                         ALU.add))
                before = m[:, 0:NT]
                final = chunks(R_M)[:, :, P - 1]
                nc.vector.tensor_tensor(chunks(R_IW), before.unsqueeze(2).to_broadcast([MH, NT, P]), chunks(R_M),
                                        ALU.subtract)
                nc.vector.tensor_tensor(chunks(R_WS), chunks(R_A), final.unsqueeze(2).to_broadcast([MH, NT, P]),
                                        ALU.subtract)
                nc.vector.tensor_tensor(dec[:, :], before, final, ALU.subtract)
                c.vstep(dve, nc.vector.tensor_tensor(rows[:, R_FLOOR, :], rows[:, R_B, :], rows[:, R_M, :], ALU.add))
                nc.vector.tensor_scalar(rows[:, R_FLOOR, :], rows[:, R_FLOOR, :], -1.0, None, ALU.mult).then_inc(diffs, 1)
                dve.wait_ge(turned, 1)
                nc.vector.tensor_copy(cols[:, :, :, :], pc[:, :, :, :])
                c.vstep(dve, nc.vector.tensor_copy(decay[:, :, :], pd[:, :, :]))

            @block.scalar
            def _(act):
                act.wait_ge(absd, 1)
                nc.scalar.activation(rows[:, R_T, :], rows[:, R_T, :], ACT.Exp, scale=-1.0).then_inc(expd, 1)
                act.wait_ge(absd, 2)
                nc.scalar.activation(rows[:, R_T, :], rows[:, R_T, :], ACT.Ln).then_inc(lnd, 1)
                act.wait_ge(diffs, 1)
                for r in (R_IW, R_FLOOR, R_WS):
                    nc.scalar.activation(rows[:, r, :], rows[:, r, :], ACT.Exp)
                nc.scalar.activation(dec[:, :], dec[:, :], ACT.Exp).then_inc(weights, 1)

            @block.tensor
            def _(pe):
                pe.wait_ge(weights, 1)
                for t in range(NT):
                    for n, r in enumerate((R_A, R_IW, R_FLOOR, R_WS)):
                        pe.transpose(pc[:, t, n, :], rows[:, r, t * P:(t + 1) * P], c.const("ident")[0:MH, 0:MH])
                for h in range(MH):
                    ins = pe.matmul(pd[:, h, :], c.const("sel")[0:MH, h * P:(h + 1) * P], dec[:, :], start=True, stop=True)
                ins.then_inc(turned, 1)


def mlstm(c, qkT, v, rows, cols, decay, og_dram, yb_dram, mT, spare):
    nc, io = c.nc, c.io
    og_t, yb_t = og_dram.rearrange("(t p) d -> t p d", p=P), yb_dram.rearrange("(t p) d -> t p d", p=P)
    R = MD ** -0.5
    with ExitStack() as s:
        e = s.enter_context(nc.sbuf_tensor("ml_e", [P, MH, P], F32))
        se = s.enter_context(nc.sbuf_tensor("ml_se", [P, 2, MH, P], F32))
        nsb = s.enter_context(nc.sbuf_tensor("ml_num", [P, 2, MV], F32))
        st = s.enter_context(nc.sbuf_tensor("ml_state", [P, MH, 2, MV], F32))
        hh, gain, kn = spare[:, 4:6, :], spare[:, 6, :], spare[:, 7, :]
        sq = s.enter_context(nc.sbuf_tensor("ml_sq", [P, MD], F32))
        den = s.enter_context(nc.sbuf_tensor("ml_den", [P, 2], F32))
        ss = s.enter_context(nc.sbuf_tensor("ml_ss", [P, 3, MH], F32))
        eps = s.enter_context(nc.sbuf_tensor("ml_eps", [P, 1], F32))
        og, yb = spare[:, 0:2, :], spare[:, 2:4, :]
        p_a = s.enter_context(nc.psum_tensor("ml_p_a", [P, MH, P], F32))
        p_s = s.enter_context(nc.psum_tensor("ml_p_s", [P, MH, P], F32))
        p_n = s.enter_context(nc.psum_tensor("ml_p_n", [P, BANK], F32))
        p_i = s.enter_context(nc.psum_tensor("ml_p_i", [P, BANK], F32))
        p_t = s.enter_context(nc.psum_tensor("ml_p_t", [P, D], F32))
        p_c = s.enter_context(nc.psum_tensor("ml_p_c", [P, 2, BANK], F32))
        gain_in, tile_in = c.sem("ml_gain_in"), [c.sem("ml_tile_in0"), c.sem("ml_tile_in1")]
        start = c.sem("ml_start")
        a_bc, s_done, k_turned = c.sem("ml_a_bc"), c.sem("ml_s_done"), c.sem("ml_k_turned")
        n_done, c_done, m_turned = c.sem("ml_n_done"), c.sem("ml_c_done"), c.sem("ml_m_turned")
        e_pre, e_exp, se_ready = c.sem("ml_e_pre"), c.sem("ml_e_exp"), c.sem("ml_se_ready")
        kn_ready, nsb_ready = c.sem("ml_kn_ready"), c.sem("ml_nsb_ready")
        t_ready, h_ready, c_ready = c.sem("ml_t_ready"), c.sem("ml_h_ready"), c.sem("ml_c_ready")
        rms_ready, m_ready, m_kept = c.sem("ml_rms"), c.sem("ml_m_ready"), c.sem("ml_m_kept")
        with nc.Block() as block:
            @block.sync
            def _(sp):
                sp.dma_start(gain[:, :], io["mh_norm_g_2"].partition_broadcast(P)).then_inc(gain_in, 16)
                for t in range(NT):
                    if t >= 2:
                        sp.wait_ge(m_ready, t - 1)
                    sp.dma_start(og[:, t % 2, :], og_t[t]).then_inc(tile_in[t % 2], 16)
                    sp.dma_start(yb[:, t % 2, :], yb_t[t]).then_inc(tile_in[t % 2], 16)

            @block.tensor
            def _(pe):
                def scores(t):
                    pe.wait_ge(e_pre, t)
                    for h in range(MH):
                        ins = pe.matmul(p_a[:, h, :], c.const("sel")[0:MH, h * P:(h + 1) * P],
                                        rows[:, R_M, t * P:(t + 1) * P], start=True, stop=True)
                    ins.then_inc(a_bc, 1)
                    pe.wait_ge(se_ready, t)
                    sl = slice(t * P, (t + 1) * P)
                    for h in range(MH):
                        for k in range(2):
                            ins = pe.matmul(p_s[:, h, :], qkT[:, KC + 2 * h + k, sl], qkT[:, 2 * h + k, sl],
                                            start=(k == 0), stop=(k == 1))
                    ins.then_inc(s_done, 1)

                def turn_keys(t):
                    if t >= 2:
                        pe.wait_ge(m_kept, t - 1)
                    for j in range(KC):
                        ins = pe.transpose(p_t[:, j * P:(j + 1) * P], qkT[:, KC + j, t * P:(t + 1) * P], c.const("ident"))
                    ins.then_inc(k_turned, 1)

                def turn_mixed(t, keys):
                    pe.wait_ge(m_ready, t + 1)
                    pe.wait_ge(kn_ready, keys)
                    for j in range(KC):
                        ins = pe.transpose(p_t[:, j * P:(j + 1) * P], hh[:, t % 2, j * P:(j + 1) * P], c.const("ident"))
                    ins.then_inc(m_turned, 1)

                pe.wait_ge(start, 1)
                scores(0)
                turn_keys(0)
                for t in range(NT):
                    if t + 1 < NT:
                        scores(t + 1)
                    sl = slice(t * P, (t + 1) * P)
                    pe.wait_ge(se_ready, t + 1)
                    pe.wait_ge(kn_ready, t + 1)
                    for h in range(MH):
                        u = MH * t + h
                        pe.wait_ge(nsb_ready, u)
                        pe.wait_ge(t_ready, u)
                        pe.matmul(p_n[:, 0:MV], se[:, t % 2, h, :], v[:, t, h, :], start=True, stop=True)
                        if t >= 1:
                            pe.wait_ge(c_ready, u - MH + 1)
                        for k in range(2):
                            ins = pe.matmul(p_i[:, 0:MV], qkT[:, 2 * h + k, sl], st[:, h, k, :],
                                            start=(k == 0), stop=(k == 1))
                        ins.then_inc(n_done, 1)
                        pe.wait_ge(c_ready, u)
                        for k in range(2):
                            ins = pe.matmul(p_c[:, k, 0:MV], kn[:, (2 * h + k) * P:(2 * h + k + 1) * P], v[:, t, h, :],
                                            start=True, stop=True)
                        ins.then_inc(c_done, 1)
                    if t >= 1:
                        turn_mixed(t - 1, t + 1)
                    if t + 1 < NT:
                        turn_keys(t + 1)
                pe.wait_ge(m_kept, NT - 1)
                turn_mixed(NT - 1, NT)

            @block.vector
            def _(dve):
                def gaps(t):
                    dve.wait_ge(a_bc, t + 1)
                    for h in range(MH):
                        ins = nc.vector.tensor_scalar(e[:, h, :], p_a[:, h, :], cols[:, t, 0, h:h + 1], 0.0,
                                                      ALU.subtract, ALU.max)
                    ins.then_inc(e_pre, 1)

                def weigh(t):
                    dve.wait_ge(e_exp, t + 1)
                    c.vstep(dve, nc.vector.scalar_tensor_tensor(
                        e[:, :, :], e[:, :, :], R, c.const("causal").unsqueeze(1).to_broadcast([P, MH, P]),
                        ALU.mult, ALU.mult))
                    dve.wait_ge(s_done, t + 1)
                    if t >= 2:
                        dve.wait_ge(n_done, MH * (t - 1))
                    nc.vector.tensor_tensor(se[:, t % 2, :, :], e[:, :, :], p_s[:, :, :], ALU.mult).then_inc(se_ready, 1)
                    dve.wait_ge(se_ready, t + 1)

                def head(t, h):
                    u = MH * t + h
                    dve.wait_ge(nsb_ready, u + 1)
                    n = nsb[:, u % 2, :]
                    nc.vector.scalar_tensor_tensor(n, p_i[:, 0:MV], cols[:, t, 1, h:h + 1], n, ALU.mult, ALU.add
                                                   ).then_inc(t_ready, 1)
                    dve.wait_ge(t_ready, u + 1)
                    c.vstep(dve, nc.vector.scalar_tensor_tensor(den[:, 0:1], n[:, MD:MV], -1.0, n[:, MD:MV],
                                                                ALU.mult, ALU.max))
                    c.vstep(dve, nc.vector.tensor_scalar(den[:, 0:1], den[:, 0:1], cols[:, t, 2, h:h + 1], None, ALU.max))
                    c.vstep(dve, nc.vector.reciprocal(den[:, 1:2], den[:, 0:1]))
                    if t >= 2 and h == 0:
                        dve.wait_ge(m_turned, t - 1)
                    nc.vector.tensor_scalar(hh[:, t % 2, h * MD:(h + 1) * MD], n[:, 0:MD], den[:, 1:2], None, ALU.mult
                                            ).then_inc(h_ready, 1)
                    dve.wait_ge(c_done, u + 1)
                    sh = st[:, h, :, :]
                    nc.vector.scalar_tensor_tensor(sh, sh, decay[:, h, t:t + 1], p_c[:, :, 0:MV], ALU.mult, ALU.add
                                                   ).then_inc(c_ready, 1)

                def mix(t):
                    m = hh[:, t % 2, :]
                    dve.wait_ge(rms_ready, t + 1)
                    c.vstep(dve, nc.vector.reciprocal(ss[:, 2, :], ss[:, 1, :]))
                    heads = m.rearrange("p (h d) -> p h d", h=MH)
                    c.vstep(dve, nc.vector.tensor_tensor(heads, heads, ss[:, 2, :].unsqueeze(2).to_broadcast([P, MH, MD]),
                                                         ALU.mult))
                    c.vstep(dve, nc.vector.tensor_tensor(m, m, gain[:, :], ALU.mult))
                    dve.wait_ge(tile_in[t % 2], 32 * (t // 2 + 1))
                    c.vstep(dve, nc.vector.tensor_tensor(m, m, og[:, t % 2, :], ALU.mult))
                    nc.vector.tensor_tensor(m, m, yb[:, t % 2, :], ALU.add).then_inc(m_ready, 1)

                nc.vector.memset(eps[:, :], EPS)
                nc.vector.memset(st[:, :, :, :], 0.0).then_inc(start, 1)
                dve.wait_ge(start, 1)
                dve.wait_ge(gain_in, 16)
                gaps(0)
                weigh(0)
                for t in range(NT):
                    if t + 1 < NT:
                        gaps(t + 1)
                    head(t, 0)
                    head(t, 1)
                    if t + 1 < NT:
                        weigh(t + 1)
                    head(t, 2)
                    head(t, 3)
                    mix(t)

            @block.scalar
            def _(act):
                def exps(t):
                    act.wait_ge(e_pre, t + 1)
                    nc.scalar.activation(e[:, :, :], e[:, :, :], ACT.Exp, scale=-1.0).then_inc(e_exp, 1)

                def keys(t):
                    act.wait_ge(k_turned, t + 1)
                    act.wait_ge(c_done, MH * t)
                    for h in range(MH):
                        c.astep(act, nc.scalar.activation(kn[:, h * MD:(h + 1) * MD], p_t[:, h * MD:(h + 1) * MD],
                                                          ACT.Copy, scale=cols[:, t, 3, h:h + 1]))
                    nc.scalar.activation(kn[:, :], kn[:, :], ACT.Copy, scale=R).then_inc(kn_ready, 1)

                def keep_mixed(t):
                    act.wait_ge(m_turned, t + 1)
                    nc.scalar.activation(mT[:, :, t * P:(t + 1) * P], p_t[:, :].rearrange("p (k n) -> p k n", k=KC),
                                         ACT.Copy).then_inc(m_kept, 1)

                act.wait_ge(start, 1)
                exps(0)
                keys(0)
                for t in range(NT):
                    if t + 1 < NT:
                        exps(t + 1)
                    for h in range(MH):
                        u = MH * t + h
                        act.wait_ge(n_done, u + 1)
                        if u >= 2:
                            act.wait_ge(h_ready, u - 1)
                        nc.scalar.activation(nsb[:, u % 2, :], p_n[:, 0:MV], ACT.Copy).then_inc(nsb_ready, 1)
                    for h in range(MH):
                        act.wait_ge(h_ready, MH * t + h + 1)
                        c.astep(act, nc.scalar.activation(sq[:, :], hh[:, t % 2, h * MD:(h + 1) * MD], ACT.Square,
                                                          accum_out=ss[:, 0, h:h + 1]))
                    act.wait_ge(m_ready, t)
                    nc.scalar.activation(ss[:, 1, :], ss[:, 0, :], ACT.Sqrt, scale=1.0 / MD, bias=eps[:, :]
                                         ).then_inc(rms_ready, 1)
                    if t >= 1:
                        keep_mixed(t - 1)
                    if t + 1 < NT:
                        keys(t + 1)
                keep_mixed(NT - 1)


def second_mixer(c, x1, x2, og, yb):
    nc, io = c.nc, c.io
    with ExitStack() as s:
        hT = s.enter_context(nc.sbuf_tensor("h2T", [P, KC, S], F32))
        norm_transposed(c, "n2", x1, io["norm_mix_g_2"], hT)
        spatial_gate(c, hT, yb)
        output_gate(c, hT, og)
        qkT = s.enter_context(nc.sbuf_tensor("qk2T", [P, 2 * KC, S], F32))
        v = s.enter_context(nc.sbuf_tensor("v2", [P, NT, MH, MV], F32))
        rows = s.enter_context(nc.sbuf_tensor("ml_rows", [MH, 5, S], F32))
        cols = s.enter_context(nc.sbuf_tensor("ml_cols", [P, NT, 4, MH], F32))
        decay = s.enter_context(nc.sbuf_tensor("ml_decays", [P, MH, NT], F32))
        project_qkv(c, hT, qkT, v, rows)
        mlstm_rows(c, rows, cols, decay)
        mT = qkT[:, 0:KC, :]
        mlstm(c, qkT, v, rows, cols, decay, og, yb, mT, hT)
        project_out(c, "o2", mT, io["w_out_2"], x1, x2)


def memory_projections(c, xT, mnT, qT, kT, v, y_slots=None):
    nc, io = c.nc, c.io
    wq, wkv = io["w_xq_2"], io["w_xkv_2"]
    sources, groups, keep = [], [], []
    for n in range(D // BANK):
        for sub in range(BANK // P):
            keep.append((kT[:, 4 * n + sub, :], NMEM))
            groups.append((len(sources), "cols", sub * P, NMEM, 0))
        sources.append(([by_rows(wkv, n * BANK, (n + 1) * BANK)], BANK))
    for n in range(D // BANK):
        for t in range(NMEM // P):
            keep.append((v[:, t, n * BANK:(n + 1) * BANK], BANK))
            groups.append((len(sources), "rows", 0, BANK, t))
        sources.append(([by_rows(wkv, D + n * BANK, D + (n + 1) * BANK)], BANK))
    of_memory = len(sources)
    for n in range(D // BANK):
        for sub in range(BANK // P):
            for half in range(2):
                keep.append((qT[:, 4 * n + sub, half * BANK:(half + 1) * BANK], BANK))
                groups.append((len(sources), "cols", sub * P, BANK, half))
        sources.append(([by_rows(wq, n * BANK, (n + 1) * BANK)], BANK))
    panels = panels_of(c, sources)
    NB = 4
    with ExitStack() as s:
        zero = s.enter_context(nc.sbuf_tensor("xp_zero", [P, D], F32))
        ps = s.enter_context(nc.psum_tensor("xp_ps", [P, NB, BANK], F32))
        done, freed = c.sem("xp_done"), c.sem("xp_freed")
        zero_ready, cleared = c.sem("xp_zero_ready"), c.sem("xp_cleared")
        with nc.Block() as block:
            @block.gpsimd
            def _(pool):
                nc.gpsimd.memset(zero[:, :], 0.0).then_inc(zero_ready, 1)
                pool.wait_ge(zero_ready, 1)
                if y_slots is not None:
                    for b in range(2 * S // P, NBLK):
                        pool.dma_start(y_slots[b * P:(b + 1) * P, :], zero[:, :]).then_inc(cleared, 16)
                    pool.wait_ge(cleared, 16 * NE)

            @block.sync
            def _(sp):
                load_panels(c, sp, panels, done, groups)

            @block.tensor
            def _(pe):
                for g in matmul_groups(pe, c, panels, groups, lambda i: mnT if i < of_memory else xT, ps, NB,
                                       done, freed):
                    pass

            @block.scalar
            def _(act):
                for g, (dst, n) in enumerate(keep):
                    act.wait_ge(done, g + 1)
                    nc.scalar.activation(dst, ps[:, g % NB, 0:n], ACT.Copy).then_inc(freed, 1)


def memory_attention(c, qT, kT, v, oT):
    nc = c.nc
    steps = [(h, half, t) for h in range(4) for half in range(2) for t in range(4)]
    N, R = len(steps), MD ** -0.5
    with ExitStack() as s:
        pr = s.enter_context(nc.sbuf_tensor("xa_p", [P, 2, NMEM], F32))
        pT = s.enter_context(nc.sbuf_tensor("xa_pT", [P, 2, 2, BANK], F32))
        mx = s.enter_context(nc.sbuf_tensor("xa_max", [P, 4, N], F32))
        ps = s.enter_context(nc.psum_tensor("xa_ps", [P, 2, BANK], F32))
        pt = s.enter_context(nc.psum_tensor("xa_pt", [P, 2, BANK], F32))
        po = s.enter_context(nc.psum_tensor("xa_po", [P, 2, BANK], F32))
        scored, maxed, expd, normed = (c.sem(f"xa_{n}") for n in ("scored", "maxed", "expd", "normed"))
        turned, kept, summed, out_kept = (c.sem(f"xa_{n}") for n in ("turned", "kept", "summed", "out_kept"))
        with nc.Block() as block:
            @block.tensor
            def _(pe):
                def scores(i):
                    h, half, t = steps[i]
                    if i >= 2:
                        pe.wait_ge(expd, i - 1)
                    at = (4 * half + t) * P
                    for k in range(2):
                        ins = pe.matmul(ps[:, i % 2, 0:NMEM], qT[:, 2 * h + k, at:at + P], kT[:, 2 * h + k, :],
                                        start=(k == 0), stop=(k == 1))
                    ins.then_inc(scored, 1)

                def turn(i):
                    pe.wait_ge(normed, i + 1)
                    if i >= 2:
                        pe.wait_ge(kept, i - 1)
                    for m in range(2):
                        ins = pe.transpose(pt[:, i % 2, m * P:(m + 1) * P], pr[:, i % 2, m * P:(m + 1) * P], c.const("ident"))
                    ins.then_inc(turned, 1)

                def values(q):
                    pe.wait_ge(kept, 4 * (q + 1))
                    h = q // 2
                    for e in range(2):
                        n = 2 * q + e
                        if n >= 2:
                            pe.wait_ge(out_kept, n - 1)
                        for m in range(2):
                            ins = pe.matmul(po[:, n % 2, :], v[:, m, (2 * h + e) * P:(2 * h + e + 1) * P],
                                            pT[:, q % 2, m, :], start=(m == 0), stop=(m == 1))
                        ins.then_inc(summed, 1)

                for i in range(N + 3):
                    if i < N:
                        scores(i)
                    if 1 <= i <= N:
                        turn(i - 1)
                    if i >= 6 and (i - 2) % 4 == 0:
                        values((i - 6) // 4)

            @block.vector
            def _(dve):
                for i in range(N + 1):
                    if i < N:
                        dve.wait_ge(scored, i + 1)
                        c.vstep(dve, nc.vector.tensor_reduce(mx[:, 0, i:i + 1], ps[:, i % 2, 0:NMEM], AX, ALU.max))
                        nc.vector.tensor_scalar(mx[:, 1, i:i + 1], mx[:, 0, i:i + 1], -R, None, ALU.mult
                                                ).then_inc(maxed, 1)
                    if i >= 1:
                        n = i - 1
                        dve.wait_ge(expd, n + 1)
                        c.vstep(dve, nc.vector.reciprocal(mx[:, 3, n:n + 1], mx[:, 2, n:n + 1]))
                        nc.vector.tensor_scalar(pr[:, n % 2, :], pr[:, n % 2, :], mx[:, 3, n:n + 1], None, ALU.mult
                                                ).then_inc(normed, 1)

            @block.scalar
            def _(act):
                def keep_out(n):
                    act.wait_ge(summed, n + 1)
                    q, e = divmod(n, 2)
                    h, half = divmod(q, 2)
                    nc.scalar.activation(oT[:, 2 * h + e, half * BANK:(half + 1) * BANK], po[:, n % 2, :], ACT.Copy
                                         ).then_inc(out_kept, 1)

                for i in range(N + 3):
                    if i < N:
                        act.wait_ge(maxed, i + 1)
                        if i >= 2:
                            act.wait_ge(turned, i - 1)
                        nc.scalar.activation(pr[:, i % 2, :], ps[:, i % 2, 0:NMEM], ACT.Exp, bias=mx[:, 1, i:i + 1],
                                             scale=R, accum_out=mx[:, 2, i:i + 1]).then_inc(expd, 1)
                    if 1 <= i <= N:
                        n = i - 1
                        q, t = divmod(n, 4)
                        act.wait_ge(turned, n + 1)
                        if q >= 2:
                            act.wait_ge(summed, 2 * (q - 1))
                        nc.scalar.activation(pT[:, q % 2, :, t * P:(t + 1) * P],
                                             pt[:, n % 2, 0:2 * P].rearrange("p (m n) -> p m n", m=2), ACT.Copy
                                             ).then_inc(kept, 1)
                    if i >= 6 and (i - 2) % 4 == 0:
                        keep_out((i - 6) // 4 * 2)
                        keep_out((i - 6) // 4 * 2 + 1)


def cross_attention(c, x2, x3, y_slots=None):
    nc, io = c.nc, c.io
    with ExitStack() as s:
        oT = s.enter_context(nc.sbuf_tensor("oT", [P, KC, S], F32))
        with ExitStack() as s2:
            hT = s2.enter_context(nc.sbuf_tensor("h3T", [P, KC, S], F32))
            mnT = s2.enter_context(nc.sbuf_tensor("mnT", [P, KC, NMEM], F32))
            qT = s2.enter_context(nc.sbuf_tensor("q3T", [P, KC, S], F32))
            kT = s2.enter_context(nc.sbuf_tensor("k3T", [P, KC, NMEM], F32))
            v = s2.enter_context(nc.sbuf_tensor("v3", [P, NMEM // P, D], F32))
            norm_transposed(c, "nm", io["mem_2"], io["norm_mem_g_2"], mnT, n_tiles=NMEM // P)
            norm_transposed(c, "n3", x2, io["norm_x_g_2"], hT)
            memory_projections(c, hT, mnT, qT, kT, v, y_slots)
            memory_attention(c, qT, kT, v, oT)
        project_out(c, "o3", oT, io["w_xo_2"], x2, x3)


def route(c, hT, gates, dest, slot_token, block_expert, n_blocks):
    nc, io = c.nc, c.io
    NR = NG + NE
    with ExitStack() as s:
        def sb(name, shape, dt=F32):
            return s.enter_context(nc.sbuf_tensor(f"rt_{name}", shape, dt))

        wr, bias, lg = sb("w", [P, KC, NR]), sb("bias", [P, NR]), sb("logits", [P, NT, NR])
        el, e4, e32 = sb("el", [P, NT, NE]), sb("e4", [P, NT, NG]), sb("e32", [P, NT, NE])
        oh1, oh2, oh = sb("oh1", [P, NT, NE]), sb("oh2", [P, NT, NE]), sb("oh", [P, NT, NE])
        gm, pg, idx = sb("gmax", [P, NT]), sb("pgroup", [P, NT]), sb("idx", [P, NT])
        v1, v2, r = sb("v1", [P, NT]), sb("v2", [P, NT]), sb("r", [P, NT])
        cnt_i, padded, pend, start = sb("cnt_i", [P, NE], I32), sb("padded", [P, NE]), sb("pend", [P, NE]), sb("start", [P, NE])
        cmp = sb("cmp", [P, NBLK, NE])
        be, nb = sb("be", [P, NBLK]), sb("nb", [P, 1])
        dest_f, lo_i, lo, hi = sb("dest_f", [P, 2, NT]), sb("lo_i", [P, 2, NT], I32), sb("lo", [P, 2, NT]), sb("hi", [P, 2, NT])
        d1, d2 = sb("d1", [P, 2 * NT, P]), sb("d2", [P, 2 * NT, NBLK])
        pl = s.enter_context(nc.psum_tensor("rt_pl", [P, NT, 64], F32))
        pk = s.enter_context(nc.psum_tensor("rt_pk", [P, NT, 64], F32))
        pn = s.enter_context(nc.psum_tensor("rt_pn", [P, BANK], F32))
        pt = s.enter_context(nc.psum_tensor("rt_pt", [P, BANK], F32))
        w_in, scored = c.sem("rt_w_in"), c.sem("rt_scored")
        pre, expd, chosen = c.sem("rt_pre"), c.sem("rt_expd"), c.sem("rt_chosen")
        ranked, placed, tabled = c.sem("rt_ranked"), c.sem("rt_placed"), c.sem("rt_tabled")
        iota32 = c.const("iota32").rearrange("p (t e) -> p t e", t=NT)
        iota4 = iota32[:, :, 0:NG]

        def bc(x, n):
            return x.unsqueeze(2).to_broadcast([P, NT, n])

        with nc.Block() as block:
            @block.sync
            def _(sp):
                with nc.allow_non_contiguous_dma(reason="36 columns, once"):
                    sp.dma_start(wr[:, :, 0:NG], by_rows(io["w_rg_2"], 0, NG)).then_inc(w_in, 16)
                    sp.dma_start(wr[:, :, NG:], by_rows(io["w_re_2"], 0, NE)).then_inc(w_in, 16)
                sp.dma_start(bias[:, 0:NG], io["b_rg_2"].partition_broadcast(P)).then_inc(w_in, 16)
                sp.dma_start(bias[:, NG:], io["b_re_2"].partition_broadcast(P)).then_inc(w_in, 16)

            @block.tensor
            def _(pe):
                pe.wait_ge(w_in, 64)
                for t in range(NT):
                    for k in range(KC):
                        ins = pe.matmul(pl[:, t, 0:NR], hT[:, k, t * P:(t + 1) * P], wr[:, k, :],
                                        start=(k == 0), stop=(k == KC - 1))
                ins.then_inc(scored, 1)
                pe.wait_ge(chosen, 1)
                for t in range(NT):
                    for j in range(t):
                        pe.matmul(pk[:, t, 0:NE], c.const("ones"), oh[:, j, :], start=(j == 0), stop=False)
                    pe.matmul(pk[:, t, 0:NE], c.const("before"), oh[:, t, :], start=(t == 0), stop=True)
                for j in range(NT):
                    ins = pe.matmul(pn[:, 0:NE], c.const("ones"), oh[:, j, :], start=(j == 0), stop=(j == NT - 1))
                ins.then_inc(ranked, 1)
                pe.wait_ge(placed, 1)
                for n in range(2 * NT):
                    ins = pe.matmul(pt[:, 0:NBLK], d1[:, n, :], d2[:, n, :], start=(n == 0), stop=(n == 2 * NT - 1))
                ins.then_inc(tabled, 1)

            @block.scalar
            def _(act):
                act.wait_ge(pre, 1)
                nc.scalar.activation(e4[:, :, :], e4[:, :, :], ACT.Exp).then_inc(expd, 1)
                act.wait_ge(pre, 2)
                nc.scalar.activation(v2[:, :], v2[:, :], ACT.Exp).then_inc(expd, 1)

            @block.vector
            def _(dve):
                V = nc.vector

                def step(ins):
                    c.vstep(dve, ins)

                def first_of_max(values, n, top, onehot, iota, spare):
                    step(V.tensor_reduce(top[:, :], values, AX, ALU.max))
                    step(V.tensor_tensor(spare, values, bc(top[:, :], n), ALU.is_equal))
                    step(V.scalar_tensor_tensor(spare, spare, -64.0, iota, ALU.mult, ALU.add))
                    step(V.tensor_reduce(idx[:, :], spare, AX, ALU.min))
                    step(V.tensor_scalar(idx[:, :], idx[:, :], 64.0, None, ALU.add))
                    step(V.tensor_tensor(onehot, iota, bc(idx[:, :], n), ALU.is_equal))

                dve.wait_ge(scored, 1)
                step(V.tensor_tensor(lg[:, :, :], pl[:, :, 0:NR], bias[:, :].unsqueeze(1).to_broadcast([P, NT, NR]), ALU.add))
                first_of_max(lg[:, :, 0:NG], NG, gm, oh1[:, :, 0:NG], iota4, e32[:, :, 0:NG])
                V.tensor_tensor(e4[:, :, :], lg[:, :, 0:NG], bc(gm[:, :], NG), ALU.subtract).then_inc(pre, 1)
                step(V.tensor_scalar(oh1[:, :, 0:NG], oh1[:, :, 0:NG], -NEG, NEG, ALU.mult, ALU.add))
                for g in range(NG):
                    ins = V.tensor_tensor(el[:, :, g * EPG:(g + 1) * EPG], lg[:, :, NG + g * EPG:NG + (g + 1) * EPG],
                                          oh1[:, :, g:g + 1].to_broadcast([P, NT, EPG]), ALU.add)
                step(ins)
                first_of_max(el[:, :, :], NE, v1, oh1[:, :, :], iota32, e32[:, :, :])
                step(V.scalar_tensor_tensor(el[:, :, :], oh1[:, :, :], 3 * NEG, el[:, :, :], ALU.mult, ALU.add))
                first_of_max(el[:, :, :], NE, v2, oh2[:, :, :], iota32, e32[:, :, :])
                V.tensor_tensor(oh[:, :, :], oh1[:, :, :], oh2[:, :, :], ALU.add).then_inc(chosen, 1)
                V.tensor_tensor(v2[:, :], v2[:, :], v1[:, :], ALU.subtract).then_inc(pre, 1)
                dve.wait_ge(expd, 1)
                step(V.tensor_reduce(pg[:, :], e4[:, :, :], AX, ALU.add))
                step(V.reciprocal(pg[:, :], pg[:, :]))
                dve.wait_ge(expd, 2)
                step(V.tensor_scalar(r[:, :], v2[:, :], 1.0, None, ALU.add))
                step(V.reciprocal(r[:, :], r[:, :]))
                step(V.tensor_tensor(gates[:, 0, :], pg[:, :], r[:, :], ALU.mult))
                step(V.tensor_tensor(gates[:, 1, :], gates[:, 0, :], v2[:, :], ALU.mult))
                dve.wait_ge(ranked, 1)
                step(V.tensor_scalar(cnt_i[:, :], pn[:, 0:NE], float(P - 1), None, ALU.add))
                step(V.tensor_scalar(cnt_i[:, :], cnt_i[:, :], 7, 7, ALU.arith_shift_right, ALU.logical_shift_left))
                step(V.tensor_copy(padded[:, :], cnt_i[:, :]))
                step(V.tensor_tensor_scan(pend[:, :], c.const("ones")[:, 0:NE], padded[:, :], 0.0, ALU.mult, ALU.add))
                step(V.tensor_tensor(start[:, :], pend[:, :], padded[:, :], ALU.subtract))
                step(V.tensor_tensor(el[:, :, :], pk[:, :, 0:NE], start[:, :].unsqueeze(1).to_broadcast([P, NT, NE]), ALU.add))
                for k, o in enumerate((oh1, oh2)):
                    step(V.tensor_tensor(e32[:, :, :], o[:, :, :], el[:, :, :], ALU.mult))
                    step(V.tensor_reduce(dest_f[:, k, :], e32[:, :, :], AX, ALU.add))
                step(V.tensor_copy(dest[:, :, :], dest_f[:, :, :]))
                step(V.tensor_copy(lo_i[:, :, :], dest_f[:, :, :]))
                step(V.tensor_scalar(lo_i[:, :, :], lo_i[:, :, :], P - 1, None, ALU.bitwise_and))
                step(V.tensor_copy(lo[:, :, :], lo_i[:, :, :]))
                step(V.tensor_tensor(hi[:, :, :], dest_f[:, :, :], lo[:, :, :], ALU.subtract))
                for n in range(2 * NT):
                    k, t = divmod(n, NT)
                    V.tensor_scalar(d1[:, n, :], c.const("iota"), lo[:, k, t:t + 1], None, ALU.is_equal)
                    ins = V.tensor_scalar(d2[:, n, :], c.const("blk"), hi[:, k, t:t + 1], c.const("tokid")[:, t:t + 1],
                                          ALU.is_equal, ALU.mult)
                ins.then_inc(placed, 1)
                step(V.tensor_tensor(cmp[:, :, :], pend[:, :].unsqueeze(1).to_broadcast([P, NBLK, NE]),
                                     c.const("blk").unsqueeze(2).to_broadcast([P, NBLK, NE]), ALU.is_le))
                step(V.tensor_reduce(be[:, :], cmp[:, :, :], AX, ALU.add))
                step(V.tensor_scalar(block_expert[:, :], be[:, :], float(NE - 1), None, ALU.min))
                step(V.tensor_scalar(nb[:, :], pend[:, NE - 1:NE], 1.0 / P, None, ALU.mult))
                V.tensor_copy(n_blocks[:, 0:1], nb[:, :])
                step(V.tensor_scalar(n_blocks[:, 1:2], nb[:, :], -1.0, None, ALU.add))
                step(V.tensor_scalar(n_blocks[:, 2:3], n_blocks[:, 1:2], 1, None, ALU.bitwise_and))
                step(V.tensor_scalar(n_blocks[:, 1:2], n_blocks[:, 1:2], 1, None, ALU.arith_shift_right))
                dve.wait_ge(tabled, 1)
                V.memset(slot_token[:, NBLK:], 0)
                step(V.tensor_copy(slot_token[:, 0:NBLK], pt[:, 0:NBLK]))


def experts(c, xn, y_slots, slot_token, block_expert, n_blocks):
    nc, io = c.nc, c.io
    KF = FF // P
    w1 = io["w1_2"].rearrange("e (p k) f -> e p (k f)", k=KC)
    w3 = io["w3_2"].rearrange("e (p k) f -> e p (k f)", k=KC)
    w2 = io["w2_2"].rearrange("e (p k) d -> e p (k d)", k=KF)
    y_b = y_slots.rearrange("(b p) d -> b p d", p=P)
    with ExitStack() as s:
        def sb(name, shape, dt=F32):
            return s.enter_context(nc.sbuf_tensor(f"ex_{name}", shape, dt))

        w1s, w3s, w2s = sb("w1", [P, 2, KC * FF]), sb("w3", [P, 2, KC * FF]), sb("w2", [P, 2, KF * D])
        idx, xg, xT = sb("idx", [P, 2], I32), sb("x", [P, 2, D]), sb("xT", [P, 2, D])
        a, h, hT, y = sb("a", [P, 2, FF]), sb("h", [P, 2, FF]), sb("hT", [P, 2, FF]), sb("y", [P, 2, D])
        p_x = s.enter_context(nc.psum_tensor("ex_px", [P, D], F32))
        p_a = s.enter_context(nc.psum_tensor("ex_pa", [P, FF], F32))
        p_b = s.enter_context(nc.psum_tensor("ex_pb", [P, FF], F32))
        p_h = s.enter_context(nc.psum_tensor("ex_ph", [P, FF], F32))
        p_y = s.enter_context(nc.psum_tensor("ex_py", [P, D], F32))

        def pair(name):
            return [c.sem(f"ex_{name}{j}") for j in range(2)]

        w1_in, w3_in, w2_in = pair("w1_in"), pair("w3_in"), pair("w2_in")
        idx_ready, x_in, x_turned, x_kept = pair("idx"), pair("x_in"), pair("x_turned"), pair("x_kept")
        a_done, b_done, a_ready, h_ready = pair("a_done"), pair("b_done"), pair("a_ready"), pair("h_ready")
        h_turned, h_kept, y_done, y_ready, y_out = (pair("h_turned"), pair("h_kept"), pair("y_done"), pair("y_ready"),
                                                    pair("y_out"))
        gathers = c.sem("ex_gathers")
        stored = c.sem("ex_stored")

        def wait(eng, sem, value):
            if not isinstance(value, int) or value > 0:
                eng.wait_ge(sem, value)

        def last(i, j):
            return (i - 1, 1) if j == 0 else (i, 0)

        def next_(i, j):
            return (i, 1) if j == 0 else (i + 1, 0)

        def upto_last(i, j):
            return i if j == 0 else i + 1

        def over_blocks(eng, body, tail=None):
            n = eng.value_load(n_blocks[0:1, 0:1], min_val=2 * S // P, max_val=NBLK)
            for j in range(2):
                body(0, j)
            with eng.Fori(1, NBLK // 2) as i:
                for j in range(2):
                    with eng.If(2 * i + j < n):
                        body(i, j)
            if tail:
                end = eng.value_load(n_blocks[0:1, 1:2], min_val=S // P - 1, max_val=NBLK // 2 - 1)
                odd = eng.value_load(n_blocks[0:1, 2:3], min_val=0, max_val=1)
                for j in range(2):
                    with eng.If(odd == j):
                        tail(end, j)
            return n

        with nc.Block() as block:
            @block.sync
            def _(sp):
                def load(i, j):
                    b = 2 * i + j
                    at = slice(b, b + 1) if isinstance(b, int) else bass.ds(b, 1)
                    e = sp.value_load(block_expert[0:1, at], min_val=0, max_val=NE - 1)
                    wait(sp, a_done[j], i)
                    sp.dma_start(w1s[:, j, :], w1[bass.ds(e, 1)].rearrange("e p n -> (e p) n")).then_inc(w1_in[j], 16)
                    wait(sp, b_done[j], i)
                    sp.dma_start(w3s[:, j, :], w3[bass.ds(e, 1)].rearrange("e p n -> (e p) n")).then_inc(w3_in[j], 16)
                    wait(sp, y_done[j], i)
                    sp.dma_start(w2s[:, j, :], w2[bass.ds(e, 1)].rearrange("e p n -> (e p) n")).then_inc(w2_in[j], 16)

                over_blocks(sp, load)

            @block.gpsimd
            def _(pool):
                def gather(i, j):
                    b = 2 * i + j
                    at = slice(b, b + 1) if isinstance(b, int) else bass.ds(b, 1)
                    wait(pool, x_turned[j], i)
                    nc.gpsimd.tensor_copy(idx[:, j:j + 1], slot_token[:, at]).then_inc(idx_ready[j], 1)
                    pool.wait_ge(idx_ready[j], i + 1)
                    pool.sem_inc(gathers, 1)
                    nc.gpsimd.indirect_dma_start(xg[:, j, :], None, xn,
                                                 bass.IndirectOffsetOnAxis(idx[:, j:j + 1].bitcast(U32), 0)
                                                 ).then_inc(x_in[j], 16)

                gather(0, 0)
                over_blocks(pool, lambda i, j: gather(*next_(i, j)))

            @block.tensor
            def _(pe):
                def turn_x(i, j):
                    pe.wait_ge(x_in[j], 16 * i + 16)
                    wait(pe, x_kept[1 - j], upto_last(i, j))
                    for k in range(KC):
                        ins = pe.transpose(p_x[:, k * P:(k + 1) * P], xg[:, j, k::KC], c.const("ident"))
                    ins.then_inc(x_turned[j], 1)

                def up(i, j, ps, w, w_in, freed, done):
                    pe.wait_ge(w_in[j], 16 * i + 16)
                    wait(pe, freed[1 - j], upto_last(i, j))
                    for k in range(KC):
                        ins = pe.matmul(ps[:, :], xT[:, j, k * P:(k + 1) * P], w[:, j, k * FF:(k + 1) * FF],
                                        start=(k == 0), stop=(k == KC - 1))
                    ins.then_inc(done[j], 1)

                def turn_h(i, j):
                    pe.wait_ge(h_ready[j], i + 1)
                    wait(pe, h_kept[1 - j], upto_last(i, j))
                    for k in range(KF):
                        ins = pe.transpose(p_h[:, k * P:(k + 1) * P], h[:, j, k::KF], c.const("ident"))
                    ins.then_inc(h_turned[j], 1)

                def down(i, j):
                    pe.wait_ge(h_kept[j], i + 1)
                    pe.wait_ge(w2_in[j], 16 * i + 16)
                    wait(pe, y_ready[1 - j], upto_last(i, j))
                    for n in range(2):
                        for k in range(KF):
                            ins = pe.matmul(p_y[:, n * BANK:(n + 1) * BANK], hT[:, j, k * P:(k + 1) * P],
                                            w2s[:, j, k * D + n * BANK:k * D + (n + 1) * BANK],
                                            start=(k == 0), stop=(k == KF - 1))
                    ins.then_inc(y_done[j], 1)

                def body(i, j):
                    first = isinstance(i, int) and i == 0 and j == 0
                    pe.wait_ge(x_kept[j], i + 1)
                    up(i, j, p_a, w1s, w1_in, a_ready, a_done)
                    if not first:
                        turn_h(*last(i, j))
                    up(i, j, p_b, w3s, w3_in, h_ready, b_done)
                    turn_x(*next_(i, j))
                    if not first:
                        down(*last(i, j))

                def tail(i, j):
                    turn_h(i, j)
                    down(i, j)

                turn_x(0, 0)
                over_blocks(pe, body, tail)

            @block.scalar
            def _(act):
                def silu(i, j):
                    act.wait_ge(a_done[j], i + 1)
                    wait(act, h_ready[j], i)
                    nc.scalar.activation(a[:, j, :], p_a[:, :], ACT.Silu).then_inc(a_ready[j], 1)

                def store(i, j):
                    b = 2 * i + j
                    at = slice(b, b + 1) if isinstance(b, int) else bass.ds(b, 1)
                    act.wait_ge(y_done[j], i + 1)
                    wait(act, y_out[j], 16 * i)
                    nc.scalar.activation(y[:, j, :], p_y[:, :], ACT.Copy).then_inc(y_ready[j], 1)
                    act.wait_ge(y_ready[j], i + 1)
                    act.dma_start(y_b[at].rearrange("e p n -> (e p) n"), y[:, j, :]).then_inc(y_out[j], 16)

                def body(i, j):
                    silu(i, j)
                    if not (isinstance(i, int) and i == 0 and j == 0):
                        store(*last(i, j))

                n = over_blocks(act, body, store)
                act.wait_ge(y_out[0], ((n + 1) >> 1) * 16)
                act.wait_ge(y_out[1], (n >> 1) * 16)
                act.sem_inc(stored, 1)

            @block.vector
            def _(dve):
                def keep_x(i, j):
                    dve.wait_ge(x_turned[j], i + 1)
                    wait(dve, b_done[j], i)
                    nc.vector.tensor_copy(xT[:, j, :], p_x[:, :]).then_inc(x_kept[j], 1)

                def keep_h(i, j):
                    dve.wait_ge(h_turned[j], i + 1)
                    wait(dve, y_done[j], i)
                    nc.vector.tensor_copy(hT[:, j, :], p_h[:, :]).then_inc(h_kept[j], 1)

                def body(i, j):
                    if not (isinstance(i, int) and i == 0 and j == 0):
                        keep_h(*last(i, j))
                    dve.wait_ge(b_done[j], i + 1)
                    dve.wait_ge(a_ready[j], i + 1)
                    wait(dve, h_turned[j], i)
                    nc.vector.tensor_tensor(h[:, j, :], a[:, j, :], p_b[:, :], ALU.mult).then_inc(h_ready[j], 1)
                    keep_x(*next_(i, j))

                keep_x(0, 0)
                over_blocks(dve, body, keep_h)


def combine(c, x3, y_slots, dest, gates, out):
    nc, io = c.nc, c.io
    x_t, out_t = x3.rearrange("(t p) d -> t p d", p=P), out.rearrange("(t p) d -> t p d", p=P)
    with ExitStack() as s:
        def sb(name, shape, dt=F32):
            return s.enter_context(nc.sbuf_tensor(f"cb_{name}", shape, dt))

        x, y = sb("x", [P, 4, D]), sb("y", [P, 4, 2, D])
        sq, gain, ss, eps = sb("sq", [P, D]), sb("gain", [P, D]), sb("ss", [P, 3, NT]), sb("eps", [P, 1])
        gain_in, eps_ready, added, rms_ready, ready = (c.sem(f"cb_{n}") for n in ("gain_in", "eps", "added", "rms", "ready"))
        x_in, y_in, out_done = ([c.sem(f"cb_{n}{b}") for b in range(4)] for n in ("x_in", "y_in", "out"))
        with nc.Block() as block:
            @block.sync
            def _(sp):
                sp.dma_start(gain[:, :], io["norm_f_g_2"].partition_broadcast(P)).then_inc(gain_in, 16)
                for t in range(NT + 1):
                    if t < NT:
                        if t >= 4:
                            sp.wait_ge(out_done[t % 4], 16)
                        sp.dma_start(x[:, t % 4, :], x_t[t]).then_inc(x_in[t % 4], 16)
                    if t >= 1:
                        sp.wait_ge(ready, t)
                        sp.dma_start(out_t[t - 1], x[:, (t - 1) % 4, :]).then_inc(out_done[(t - 1) % 4], 16)
                for b in range(4):
                    sp.wait_ge(out_done[b], 32)

            @block.gpsimd
            def _(pool):
                for t in range(NT):
                    if t >= 4:
                        pool.wait_ge(added, t - 3)
                    for k in range(2):
                        nc.gpsimd.indirect_dma_start(y[:, t % 4, k, :], None, y_slots,
                                                     bass.IndirectOffsetOnAxis(dest[:, k, t:t + 1].bitcast(U32), 0)
                                                     ).then_inc(y_in[t % 4], 16)

            @block.scalar
            def _(act):
                act.wait_ge(eps_ready, 1)
                for t in range(NT):
                    act.wait_ge(added, t + 1)
                    c.astep(act, nc.scalar.activation(sq[:, :], x[:, t % 4, :], ACT.Square, accum_out=ss[:, 0, t:t + 1]))
                    nc.scalar.activation(ss[:, 1, t:t + 1], ss[:, 0, t:t + 1], ACT.Sqrt, scale=1.0 / D, bias=eps[:, :]
                                         ).then_inc(rms_ready, 1)

            @block.vector
            def _(dve):
                nc.vector.memset(eps[:, :], EPS).then_inc(eps_ready, 1)
                dve.wait_ge(gain_in, 16)
                for t in range(NT):
                    xx = x[:, t % 4, :]
                    dve.wait_ge(x_in[t % 4], 16 * (t // 4 + 1))
                    dve.wait_ge(y_in[t % 4], 32 * (t // 4 + 1))
                    c.vstep(dve, nc.vector.scalar_tensor_tensor(xx, y[:, t % 4, 0, :], gates[:, 0, t:t + 1], xx,
                                                                ALU.mult, ALU.add))
                    nc.vector.scalar_tensor_tensor(xx, y[:, t % 4, 1, :], gates[:, 1, t:t + 1], xx, ALU.mult, ALU.add
                                                   ).then_inc(added, 1)
                    dve.wait_ge(rms_ready, t + 1)
                    c.vstep(dve, nc.vector.reciprocal(ss[:, 2, t:t + 1], ss[:, 1, t:t + 1]))
                    nc.vector.scalar_tensor_tensor(xx, xx, ss[:, 2, t:t + 1], gain[:, :], ALU.mult, ALU.mult
                                                   ).then_inc(ready, 1)


def mixture(c, x3, xn, y_slots, out):
    nc, io = c.nc, c.io
    with ExitStack() as s:
        gates = s.enter_context(nc.sbuf_tensor("gates", [P, 2, NT], F32))
        dest = s.enter_context(nc.sbuf_tensor("dest", [P, 2, NT], I32))
        slot_token = s.enter_context(nc.sbuf_tensor("slot_token", [P, NBLK + 1], I32))
        block_expert = s.enter_context(nc.sbuf_tensor("block_expert", [P, NBLK], I32))
        n_blocks = s.enter_context(nc.sbuf_tensor("n_blocks", [P, 3], I32))
        with ExitStack() as s2:
            hT = s2.enter_context(nc.sbuf_tensor("h4T", [P, KC, S], F32))
            norm_transposed(c, "n4", x3, io["norm_moe_g_2"], hT, keep=xn, gain_row=io["norm_moe_g_2"])
            route(c, hT, gates, dest, slot_token, block_expert, n_blocks)
        experts(c, xn, y_slots, slot_token, block_expert, n_blocks)
        combine(c, x3, y_slots, dest, gates, out)


INS = ["x", "norm_pre_g", "w_in", "conv_w", "w_out", "norm_post_g", "mem_2", "norm_mix_g_2", "w_in_2", "b_gate_2",
       "b_if_2", "conv_w_2", "conv_b_2", "mh_norm_g_2", "sgu_norm_g_2", "b_s_2", "w_out_2", "norm_x_g_2",
       "norm_mem_g_2", "w_xq_2", "w_xkv_2", "w_xo_2", "norm_moe_g_2", "w_rg_2", "b_rg_2", "w_re_2", "b_re_2", "w1_2",
       "w3_2", "w2_2", "norm_f_g_2"]
WHOLE = {"norm_pre_g", "w_in", "conv_w", "w_out", "norm_post_g", "norm_f_g_2"}


def build(nc, io):
    def scratch(name, rows):
        return nc.dram_tensor(name, (rows, D), F32, kind="Internal").ap()

    x1, x2, x3, xn = (scratch(f"{n}_rows", S) for n in ("x1", "x2", "x3", "xn"))
    og, yb, y_slots = scratch("og_rows", S), scratch("yb_rows", S), scratch("y_slots", NBLK * P)
    with ExitStack() as ctx:
        c = Core(nc, io, ctx)
        load_constants(c)
        first_block(c, io["x"], x1)
        second_mixer(c, x1, x2, og, yb)
        c.retire_semaphores()
        cross_attention(c, x2, x3, y_slots)
        mixture(c, x3, xn, y_slots, io["out"])


def kernel(**inputs):
    import concourse.bacc as bacc
    from concourse.bass_utils import run_bass_kernel_spmd as run

    nc = bacc.Bacc("TRN2", target_bir_lowering=False, num_devices=1)
    arrays = {}
    for name in INS:
        a = np.asarray(inputs[name])
        arrays[name] = np.ascontiguousarray(a if name in WHOLE else a[0])
    arrays["w_s_T"] = np.ascontiguousarray(np.asarray(inputs["w_s_2"])[0].transpose(0, 2, 1))
    arrays["consts"] = shape_constants()
    io = {n: nc.dram_tensor(n, a.shape, mybir.dt.from_np(a.dtype), kind="ExternalInput").ap() for n, a in arrays.items()}
    io["out"] = nc.dram_tensor("out", (S, D), F32, kind="ExternalOutput").ap()
    build(nc, io)
    r = run(nc, [arrays], core_ids=[0])
    return r.results[0]["out"].reshape(1, S, D)
```

```python
from contextlib import ExitStack

import numpy as np

import concourse.bass as bass
from concourse import mybir

F32 = mybir.dt.float32
F32R = mybir.dt.float32r
I32 = mybir.dt.int32
U32 = mybir.dt.uint32
ALU = mybir.AluOpType
ACT = mybir.ActivationFunctionType
AX = mybir.AxisListType.X

P = 128
D = 1024
S = 1024
KC = D // P
NT = S // P
BANK = 512
EPS = 1e-6
NEG = -1e30

HD = 64
AW = 768
NH = AW // HD
CW = 256
SCALE = HD ** -0.5
MH, MD, MV = 4, 256, 257
NMEM = 256
NE, NG, EPG, FF = 32, 4, 8, 512
NBLK = 2 * S // P + NE

CONST_COLS = dict(ident=P, ones=P, causal=P, before=P, iota=P, tokid=NT, blk=NBLK, sel=MH * P, iota32=NT * NE,
                  cos=NT * 32, sin=NT * 32, logc=S)
CONST_AT = {}
_at = 0
for _n, _w in CONST_COLS.items():
    CONST_AT[_n] = _at
    _at += _w
CONST_W = _at


def shape_constants():
    c = {n: np.zeros((P, w), np.float32) for n, w in CONST_COLS.items()}
    p = np.arange(P)
    c["ident"][p, p] = 1
    c["ones"][:] = 1
    c["causal"][:] = p[:, None] <= p[None, :]
    c["before"][:] = p[:, None] < p[None, :]
    c["iota"][:] = p[None, :]
    c["tokid"][:] = p[:, None] + P * np.arange(NT)[None, :]
    c["blk"][:] = P * np.arange(NBLK)[None, :]
    for h in range(MH):
        c["sel"][h, h * P:(h + 1) * P] = 1
    c["iota32"][:] = np.tile(np.arange(NE), NT)[None, :]
    inv = np.float32(10000.0) ** (-np.arange(32, dtype=np.float32) * np.float32(2.0) / np.float32(64))
    ang = np.arange(S, dtype=np.float32)[:, None] * inv[None, :].astype(np.float32)
    c["cos"][:] = np.cos(ang).reshape(NT, P, 32).transpose(1, 0, 2).reshape(P, -1)
    c["sin"][:] = np.sin(ang).reshape(NT, P, 32).transpose(1, 0, 2).reshape(P, -1)
    d = p[:, None] + (S - P) - np.arange(S)[None, :]
    n = sum(((d >= 0) & (d <= w) & (d % r == 0)).astype(np.float32) for w, r in ((128, 1), (512, 4), (2048, 16)))
    c["logc"][:] = np.where(n > 0, np.log(np.maximum(n, 1)) / np.float32(SCALE), NEG)
    return np.ascontiguousarray(np.concatenate([c[n] for n in CONST_COLS], axis=1).astype(np.float32))


class Tally:

    def __init__(self, nc, ctx, name):
        self.sem, self.n = ctx.enter_context(nc.semaphore(name)), 0

    def inc(self, ins, by=1):
        ins.then_inc(self.sem, by)
        self.n += by
        return self.n


class Core:

    def __init__(self, nc, io, ctx):
        self.nc, self.io, self.ctx, self.in_use = nc, io, ctx, []
        self.small = ctx.enter_context(nc.sbuf_tensor("const_small", [P, CONST_AT["cos"]], F32))
        self.const_in = ctx.enter_context(nc.semaphore("const_in"))
        self.dve_chain = Tally(nc, ctx, "dve_chain")
        self.act_chain = Tally(nc, ctx, "act_chain")
        self.pool_chain = Tally(nc, ctx, "pool_chain")
    def sem(self, name):
        self.in_use.append(self.nc.alloc_semaphore(name=name))
        return self.in_use[-1]

    def retire_semaphores(self):
        self.nc.clear_and_free_semaphores(self.in_use)
        self.in_use = []
        self.nc.all_engine_barrier()

    def const(self, name):
        return self.small[:, CONST_AT[name]:CONST_AT[name] + CONST_COLS[name]]

    def const_dram(self, name):
        return self.io["consts"][:, CONST_AT[name]:CONST_AT[name] + CONST_COLS[name]]

    def vstep(self, dve, ins):
        dve.wait_ge(self.dve_chain.sem, self.dve_chain.inc(ins))

    def astep(self, act, ins):
        act.wait_ge(self.act_chain.sem, self.act_chain.inc(ins))

    def gstep(self, pool, ins):
        pool.wait_ge(self.pool_chain.sem, self.pool_chain.inc(ins))


def load_constants(c):
    nc = c.nc
    with nc.Block() as block:
        @block.sync
        def _(sp):
            sp.dma_start(c.small[:, :], c.io["consts"][:, 0:CONST_AT["cos"]]).then_inc(c.const_in, 16)
            sp.wait_ge(c.const_in, 16)


def column_of(gain):
    return gain.rearrange("(p k) -> p k", k=KC)


class Split:

    def __init__(self, nc, stack, name, shape, side=None):
        self.hi = stack.enter_context(nc.sbuf_tensor(f"{name}_hi", shape, F32R, side=side))
        self.lo = stack.enter_context(nc.sbuf_tensor(f"{name}_lo", shape, F32R, side=side))


class Weights:

    def __init__(self, c, stack, tag, sources, groups, R=12, pre=KC, side=None):
        nc, tag = c.nc, f"{tag}_w"
        self.c, self.sources, self.groups, self.R, self.pre = c, sources, groups, R, pre
        self.raw = stack.enter_context(nc.sbuf_tensor(f"{tag}_raw", [P, 2, KC // 2 * BANK], F32, side=side))
        self.hi = stack.enter_context(nc.sbuf_tensor(f"{tag}_hi", [P, R, BANK], F32R, side=side))
        self.lo = stack.enter_context(nc.sbuf_tensor(f"{tag}_lo", [P, R, BANK], F32R, side=side))
        self.raw_in = [c.sem(f"{tag}_raw_in{b}") for b in range(2)]
        self.hi_done, self.lo_done = c.sem(f"{tag}_hi_done"), c.sem(f"{tag}_lo_done")
        self.chunk_used = c.sem(f"{tag}_chunk_used")
        self.done, self.freed = c.sem(f"{tag}_done"), c.sem(f"{tag}_freed")
        self.landed, total = [], [0, 0]
        for q in range(2 * len(sources)):
            total[q % 2] += 16 * len(sources[q // 2][0])
            self.landed.append(total[q % 2])
        self.first = {i: min((g for g, x in enumerate(groups) if x[0] == i), default=0) for i in range(len(sources))}
        self.last = {i: max((g for g, x in enumerate(groups) if x[0] == i), default=0) for i in range(len(sources))}
        self.n_chunks = KC * len(sources)

    def part(self, i0, i1):
        end = min(i1 + 1, len(self.sources))
        g0 = self.first[i0]
        g1 = self.last[i1 - 1] + 1
        return range(g0, g1), (2 * (i0 + 1), 2 * end), (self.pre if i0 == 0 else KC * (i0 + 1), KC * end)

    def half(self, q, w):
        return self.raw[:, q % 2, 0:KC // 2 * w].rearrange("p (k n) -> p k n", n=w)

    def load(self, sp, q0=0, q1=None):
        for q in range(q0, 2 * len(self.sources) if q1 is None else q1):
            pieces, w = self.sources[q // 2]
            if q >= 2:
                sp.wait_ge(self.lo_done, 4 * (q - 1))
            at, k0 = 0, KC // 2 * (q % 2)
            for src in pieces:
                wide = src.shape[-1]
                sp.dma_start(self.half(q, w)[:, :, at:at + wide], src[:, k0:k0 + KC // 2, :]
                             ).then_inc(self.raw_in[q % 2], 16)
                at += wide

    def round_hi(self, engine, emit, n):
        w = self.sources[n // KC][1]
        q = n // (KC // 2)
        engine.wait_ge(self.raw_in[q % 2], self.landed[q])
        if n >= self.R:
            i, k = divmod(n - self.R, KC)
            if k == KC - 1:
                engine.wait_ge(self.done, self.last[i] + 1)
            else:
                engine.wait_ge(self.chunk_used, (KC - 1) * i + k + 1)
        emit(self.hi[:, n % self.R, 0:w], self.half(q, w)[:, n % (KC // 2), :]).then_inc(self.hi_done, 1)

    def take_lo(self, engine, emit, n):
        w = self.sources[n // KC][1]
        engine.wait_ge(self.hi_done, n + 1)
        emit(self.lo[:, n % self.R, 0:w], self.half(n // (KC // 2), w)[:, n % (KC // 2), :],
             self.hi[:, n % self.R, 0:w].bitcast(F32), ALU.subtract).then_inc(self.lo_done, 1)

    def prepare(self, pool):
        for n in range(self.pre):
            self.round_hi(pool, self.c.nc.gpsimd.tensor_copy, n)
            self.take_lo(pool, self.c.nc.gpsimd.tensor_tensor, n)

    def take_los(self, pool, chunks=None):
        for n in range(*(chunks or (self.pre, self.n_chunks))):
            self.take_lo(pool, self.c.nc.gpsimd.tensor_tensor, n)

    def before(self, act, g):
        if g >= len(self.groups):
            return
        i = self.groups[g][0]
        spare = min(KC, self.R - KC)
        copy = lambda out, in_: self.c.nc.scalar.activation(out, in_, ACT.Copy)
        if g == 0:
            for n in range(self.pre, KC):
                self.round_hi(act, copy, n)
        if i + 1 < len(self.sources):
            for first, lo, hi in ((self.first[i] == g, 0, spare), (self.last[i] == g, spare, KC)):
                if first:
                    for n in range(KC * (i + 1) + lo, KC * (i + 1) + hi):
                        if n >= self.pre:
                            self.round_hi(act, copy, n)


def norm_transposed(c, tag, src, gain, hT, n_tiles=NT, keep=None, gain_row=None, plain=None, next_weights=None):
    nc = c.nc
    src_t = src.rearrange("(t p) d -> t p d", p=P)
    with ExitStack() as s:
        x = s.enter_context(nc.sbuf_tensor(f"{tag}_x", [P, 2, D], F32))
        sq = s.enter_context(nc.sbuf_tensor(f"{tag}_sq", [P, D], F32))
        g = s.enter_context(nc.sbuf_tensor(f"{tag}_g", [P, KC], F32))
        ss = s.enter_context(nc.sbuf_tensor(f"{tag}_ss", [P, n_tiles], F32))
        rms = s.enter_context(nc.sbuf_tensor(f"{tag}_rms", [P, n_tiles], F32))
        rstd = s.enter_context(nc.sbuf_tensor(f"{tag}_rstd", [P, n_tiles], F32))
        eps = s.enter_context(nc.sbuf_tensor(f"{tag}_eps", [P, 1], F32))
        ps = s.enter_context(nc.psum_tensor(f"{tag}_ps", [P, 2, D], F32))
        g_in, x_in = c.sem(f"{tag}_g_in"), [c.sem(f"{tag}_x_in0"), c.sem(f"{tag}_x_in1")]
        rms_ready, xn_ready = c.sem(f"{tag}_rms"), c.sem(f"{tag}_xn")
        turned, taken = c.sem(f"{tag}_turned"), c.sem(f"{tag}_taken")
        eps_ready = c.sem(f"{tag}_eps")
        if plain is None:
            full = s.enter_context(nc.sbuf_tensor(f"{tag}_full", [P, 2, KC, P], F32))
            rounded, rest = c.sem(f"{tag}_rounded"), c.sem(f"{tag}_rest")
        if keep is not None:
            keep_t = keep.rearrange("(t p) d -> t p d", p=P)
            grow = s.enter_context(nc.sbuf_tensor(f"{tag}_grow", [P, D], F32))
            xg = s.enter_context(nc.sbuf_tensor(f"{tag}_xg", [P, 2, D], F32))
            xg_ready, xg_out = c.sem(f"{tag}_xg_ready"), [c.sem(f"{tag}_xg_out0"), c.sem(f"{tag}_xg_out1")]
        with nc.Block() as block:
            @block.sync
            def _(sp):
                sp.dma_start(g[:, :], column_of(gain)).then_inc(g_in, 16)
                if keep is not None:
                    sp.dma_start(grow[:, :], gain_row.partition_broadcast(P)).then_inc(g_in, 16)
                for t in range(n_tiles):
                    if t >= 2:
                        sp.wait_ge(turned, t - 1)
                        if keep is not None:
                            sp.wait_ge(xg_ready, t - 1)
                    sp.dma_start(x[:, t % 2, :], src_t[t]).then_inc(x_in[t % 2], 16)
                    if t == 1 and next_weights:
                        next_weights.load(sp, 0, 2)
                    if keep is not None and t >= 1:
                        sp.wait_ge(xg_ready, t)
                        sp.dma_start(keep_t[t - 1], xg[:, (t - 1) % 2, :]).then_inc(xg_out[(t - 1) % 2], 16)
                if keep is not None:
                    t = n_tiles
                    sp.wait_ge(xg_ready, t)
                    sp.dma_start(keep_t[t - 1], xg[:, (t - 1) % 2, :]).then_inc(xg_out[(t - 1) % 2], 16)
                    sp.wait_ge(xg_out[0], 16 * (n_tiles // 2))
                    sp.wait_ge(xg_out[1], 16 * (n_tiles // 2))

            @block.scalar
            def _(act):
                def round_hi(t):
                    act.wait_ge(taken, t + 1)
                    nc.scalar.activation(hT.hi[:, :, t * P:(t + 1) * P], full[:, t % 2, :, :], ACT.Copy
                                         ).then_inc(rounded, 1)

                act.wait_ge(eps_ready, 1)
                for t in range(n_tiles):
                    act.wait_ge(x_in[t % 2], 16 * (t // 2 + 1))
                    c.astep(act, nc.scalar.activation(sq[:, :], x[:, t % 2, :], ACT.Square, accum_out=ss[:, t:t + 1]))
                    nc.scalar.activation(rms[:, t:t + 1], ss[:, t:t + 1], ACT.Sqrt, scale=1.0 / D,
                                         bias=eps[:, :]).then_inc(rms_ready, 1)
                    if plain is None and t >= 2:
                        round_hi(t - 2)
                if plain is None:
                    round_hi(n_tiles - 2)
                    round_hi(n_tiles - 1)

            @block.vector
            def _(dve):
                nc.vector.memset(eps[:, :], EPS).then_inc(eps_ready, 1)

                def evacuate(t):
                    dve.wait_ge(turned, t + 1)
                    if plain is None and t >= 2:
                        dve.wait_ge(rest, t - 1)
                    out = plain[:, :, t * P:(t + 1) * P] if plain is not None else full[:, t % 2, :, :]
                    nc.vector.tensor_tensor(out, ps[:, t % 2, :].rearrange("p (k n) -> p k n", k=KC),
                                            g[:, :].unsqueeze(2).to_broadcast([P, KC, P]), ALU.mult).then_inc(taken, 1)

                def take_rest(t):
                    sl = slice(t * P, (t + 1) * P)
                    dve.wait_ge(rounded, t + 1)
                    nc.vector.tensor_tensor(hT.lo[:, :, sl], full[:, t % 2, :, :], hT.hi[:, :, sl].bitcast(F32),
                                            ALU.subtract).then_inc(rest, 1)

                dve.wait_ge(g_in, 16 if keep is None else 32)
                for t in range(n_tiles):
                    dve.wait_ge(rms_ready, t + 1)
                    c.vstep(dve, nc.vector.reciprocal(rstd[:, t:t + 1], rms[:, t:t + 1]))
                    ins = nc.vector.tensor_scalar(x[:, t % 2, :], x[:, t % 2, :], rstd[:, t:t + 1], None, ALU.mult)
                    ins.then_inc(xn_ready, 1)
                    if keep is not None:
                        dve.wait_ge(xn_ready, t + 1)
                        if t >= 2:
                            dve.wait_ge(xg_out[t % 2], 16 * (t // 2))
                        nc.vector.tensor_tensor(xg[:, t % 2, :], x[:, t % 2, :], grow[:, :],
                                                ALU.mult).then_inc(xg_ready, 1)
                    if plain is None and t >= 3:
                        take_rest(t - 3)
                    if t >= 1:
                        evacuate(t - 1)
                if plain is None and n_tiles >= 3:
                    take_rest(n_tiles - 3)
                evacuate(n_tiles - 1)
                if plain is None:
                    for t in range(max(0, n_tiles - 2), n_tiles):
                        take_rest(t)

            @block.tensor
            def _(pe):
                for t in range(n_tiles):
                    pe.wait_ge(xn_ready, t + 1)
                    if t >= 2:
                        pe.wait_ge(taken, t - 1)
                    for k in range(KC):
                        ins = pe.transpose(ps[:, t % 2, k * P:(k + 1) * P], x[:, t % 2, k::KC], c.const("ident"))
                    ins.then_inc(turned, 1)

            @block.gpsimd
            def _(pool):
                if next_weights:
                    next_weights.prepare(pool)


def by_rows(w, a, b):
    return w.rearrange("(p k) n -> p k n", k=KC)[:, :, a:b]


def by_chunks(w, a, b):
    return w.rearrange("(k p) n -> p k n", p=P)[:, :, a:b]


def products(pe, out, stationary, moving, start, stop):
    (a, b), (x, y) = stationary, moving
    pe.matmul(out, a, x, start=start, stop=False)
    pe.matmul(out, a, y, start=False, stop=False)
    return pe.matmul(out, b, x, start=False, stop=stop)


def matmul_groups(pe, weights, hT, ps, n_banks, span=None):
    for g in span or range(len(weights.groups)):
        i, kind, a, w, t = weights.groups[g]
        if g >= n_banks:
            pe.wait_ge(weights.freed, g - n_banks + 1)
        x = hT(i) if callable(hT) else hT
        for k in range(KC):
            n = KC * i + k
            if g == weights.first[i]:
                pe.wait_ge(weights.lo_done, n + 1)
            slot = n % weights.R
            if kind == "rows":
                tok, col = slice(t * P, (t + 1) * P), slice(a, a + w)
                acts = (x.hi[:, k, tok], x.lo[:, k, tok])
                ins = products(pe, ps[:, g % n_banks, 0:w], acts, (weights.hi[:, slot, col], weights.lo[:, slot, col]),
                               k == 0, k == KC - 1)
            else:
                tok, col = slice(t * w, (t + 1) * w), slice(a, a + P)
                acts = (x.hi[:, k, tok], x.lo[:, k, tok])
                ins = products(pe, ps[:, g % n_banks, 0:w], (weights.hi[:, slot, col], weights.lo[:, slot, col]), acts,
                               k == 0, k == KC - 1)
            if g == weights.last[i] and k < KC - 1:
                ins.then_inc(weights.chunk_used, 1)
        ins.then_inc(weights.done, 1)
        yield g


def first_weights(c, stack):
    w = c.io["w_in"]
    qk_cols, v_at, g_at, c_at = 2 * AW, 2 * AW, 3 * AW, 4 * AW
    sources, groups, at = [], [], {}
    for i in range(qk_cols // BANK):
        sources.append(([by_rows(w, i * BANK, (i + 1) * BANK)], BANK))
        groups += [(i, "rows", 0, BANK, t) for t in range(NT)]
    at["v"] = len(groups)
    for a, wd in ((0, BANK), (BANK, AW - BANK)):
        groups += [(len(sources), "rows", 0, wd, t) for t in range(NT)]
        sources.append(([by_rows(w, v_at + a, v_at + a + wd)], wd))
    at["gate"] = len(groups)
    for a, wd in ((0, BANK), (BANK, AW - BANK)):
        for sub in range(wd // P):
            for half in range(2):
                at[len(groups)] = (a // P + sub, half)
                groups.append((len(sources), "cols", sub * P, BANK, half))
        sources.append(([by_rows(w, g_at + a, g_at + a + wd)], wd))
    at["conv"] = len(groups)
    for j in range(CW // P):
        for half in range(2):
            for kind in range(4):
                groups.append((len(sources), "cols", kind * P, BANK, half))
        sources.append(([by_rows(w, c_at + kind * CW + j * P, c_at + kind * CW + (j + 1) * P)
                         for kind in range(4)], BANK))
    weights = Weights(c, stack, "p1", sources, groups, R=11)
    weights.at = at
    return weights


def project_first(c, weights, hT, qk_dram, v_dram, mixT):
    nc, io = c.nc, c.io
    groups, at = weights.groups, weights.at
    n_qk, n_v, n_g = at["v"], at["gate"], at["conv"]
    v_rows = v_dram.rearrange("(t p) d -> t p d", p=P)
    NB = 4
    with ExitStack() as s:
        cs = s.enter_context(nc.sbuf_tensor("rope_cs", [P, 2 * NT * 32], F32))
        rot = s.enter_context(nc.sbuf_tensor("rope_rot", [P, 2, BANK], F32))
        rb = s.enter_context(nc.sbuf_tensor("rope_b", [P, BANK], F32))
        cw = s.enter_context(nc.sbuf_tensor("conv_taps", [P, 3, CW // P], F32))
        cz = s.enter_context(nc.sbuf_tensor("conv_z", [P, 4, S], F32))
        cu = s.enter_context(nc.sbuf_tensor("conv_u", [P, S + 2], F32))
        ps = s.enter_context(nc.psum_tensor("p1_ps", [P, NB, BANK], F32))
        pt = s.enter_context(nc.psum_tensor("p1_pt", [P, 2, BANK], F32))
        qk_sb = s.enter_context(nc.sbuf_tensor("p1_qk", [P, 2, BANK // P, P], F32))
        v_sb = s.enter_context(nc.sbuf_tensor("p1_v", [P, 2, BANK], F32))
        tables_in = c.sem("rope_tables_in")
        done, freed = weights.done, weights.freed
        qk_out, v_out = [c.sem(f"qk_out{b}") for b in range(2)], [c.sem(f"v_out{b}") for b in range(2)]
        rot_ready, rot_turned, rot_kept = c.sem("rot_ready"), c.sem("rot_turned"), c.sem("rot_kept")
        conv_done = c.sem("conv_done")
        cos = cs[:, 0:NT * 32].rearrange("p (t f) -> p t f", t=NT)
        sin = cs[:, NT * 32:2 * NT * 32].rearrange("p (t f) -> p t f", t=NT)
        NHB = BANK // HD
        with nc.Block() as block:
            @block.sync
            def _(sp):
                weights.load(sp, 2)

            @block.gpsimd
            def _(pool):
                a = CONST_AT["cos"]
                pool.dma_start(cs[:, :], io["consts"][:, a:a + 2 * NT * 32]).then_inc(tables_in, 16)
                for j in range(CW // P):
                    with nc.allow_non_contiguous_dma(reason="a few hundred taps, once"):
                        pool.dma_start(cw[:, :, j:j + 1],
                                       io["conv_w"][:, j * P:(j + 1) * P].rearrange("j (c o) -> c j o", o=1)
                                       ).then_inc(tables_in, 16)
                weights.take_los(pool)

            @block.tensor
            def _(pe):
                def turn(g):
                    pe.wait_ge(rot_ready, g + 1)
                    if g >= 2:
                        pe.wait_ge(rot_kept, g - 1)
                    for j in range(BANK // P):
                        ins = pe.transpose(pt[:, g % 2, j * P:(j + 1) * P], rot[:, g % 2, j * P:(j + 1) * P],
                                           c.const("ident"))
                    ins.then_inc(rot_turned, 1)

                for g in matmul_groups(pe, weights, hT, ps, NB):
                    if 1 <= g <= n_qk:
                        turn(g - 1)

            @block.vector
            def _(dve):
                dve.wait_ge(tables_in, 16 * (1 + CW // P))
                for g in range(n_qk):
                    t = g % NT
                    z = ps[:, g % NB, :].rearrange("p (h a f) -> p h a f", h=NHB, a=2)
                    r = rot[:, g % 2, :].rearrange("p (h a f) -> p h a f", h=NHB, a=2)
                    b = rb[:, :].rearrange("p (h a f) -> p h a f", h=NHB, a=2)
                    cb = cos[:, t, :].unsqueeze(1).to_broadcast([P, NHB, 32])
                    sb = sin[:, t, :].unsqueeze(1).to_broadcast([P, NHB, 32])
                    dve.wait_ge(done, g + 1)
                    if g >= 2:
                        dve.wait_ge(rot_turned, g - 1)
                    nc.vector.tensor_tensor(r[:, :, 0, :], z[:, :, 0, :], cb, ALU.mult)
                    nc.vector.tensor_tensor(r[:, :, 1, :], z[:, :, 1, :], cb, ALU.mult)
                    nc.vector.tensor_tensor(b[:, :, 0, :], z[:, :, 1, :], sb, ALU.mult)
                    nc.vector.tensor_tensor(b[:, :, 1, :], z[:, :, 0, :], sb, ALU.mult).then_inc(freed, 1)
                    dve.wait_ge(freed, g + 1)
                    nc.vector.tensor_tensor(r[:, :, 0, :], r[:, :, 0, :], b[:, :, 0, :], ALU.subtract)
                    ins = nc.vector.tensor_tensor(r[:, :, 1, :], r[:, :, 1, :], b[:, :, 1, :], ALU.add)
                    ins.then_inc(rot_ready, 1)
                    dve.wait_ge(rot_ready, g + 1)
                for j in range(CW // P):
                    dve.wait_ge(freed, n_g + 8 * (j + 1))
                    c.vstep(dve, nc.vector.memset(cu[:, 0:2], 0.0))
                    c.vstep(dve, nc.vector.tensor_tensor(cu[:, 2:S + 2], cz[:, 2, :], cz[:, 0, :], ALU.mult))
                    c.vstep(dve, nc.vector.tensor_scalar(cz[:, 0, :], cu[:, 0:S], cw[:, 0, j:j + 1], None, ALU.mult))
                    for tap in (1, 2):
                        c.vstep(dve, nc.vector.scalar_tensor_tensor(cz[:, 0, :], cu[:, tap:tap + S],
                                                                    cw[:, tap, j:j + 1], cz[:, 0, :],
                                                                    ALU.mult, ALU.add))
                    c.vstep(dve, nc.vector.tensor_tensor(cz[:, 0, :], cz[:, 0, :], cz[:, 1, :], ALU.mult))
                    nc.vector.tensor_tensor(mixT[:, AW // P + j, :], cz[:, 0, :], cz[:, 3, :],
                                            ALU.mult).then_inc(conv_done, 1)

            @block.scalar
            def _(act):
                def keep(g):
                    i, t = g // NT, g % NT
                    act.wait_ge(rot_turned, g + 1)
                    if g >= 2:
                        act.wait_ge(qk_out[g % 2], 16 * (g // 2))
                    nc.scalar.activation(qk_sb[:, g % 2, :, :], pt[:, g % 2, :].rearrange("p (j n) -> p j n", j=4),
                                         ACT.Copy).then_inc(rot_kept, 1)
                    act.wait_ge(rot_kept, g + 1)
                    act.dma_start(qk_dram[4 * i:4 * i + 4, :, t * P:(t + 1) * P].rearrange("j p n -> p j n"),
                                  qk_sb[:, g % 2, :, :]).then_inc(qk_out[g % 2], 16)

                weights.before(act, 0)
                for g in range(n_qk):
                    weights.before(act, g + 1)
                    keep(g)
                act.wait_ge(freed, n_qk)
                for g in range(n_qk, len(groups)):
                    i, kind, a, wd, t = groups[g]
                    if g > n_qk:
                        weights.before(act, g)
                    act.wait_ge(done, g + 1)
                    if g < n_v:
                        a, m = (0 if g - n_qk < NT else BANK), g - n_qk
                        if m >= 2:
                            act.wait_ge(v_out[m % 2], 16 * (m // 2))
                        ins = nc.scalar.activation(v_sb[:, m % 2, 0:wd], ps[:, g % NB, 0:wd], ACT.Copy)
                    elif g < n_g:
                        chunk, half = at[g]
                        ins = nc.scalar.activation(mixT[:, chunk, half * BANK:(half + 1) * BANK], ps[:, g % NB, :],
                                                   ACT.Silu)
                    else:
                        j, r = divmod(g - n_g, 8)
                        half, which = divmod(r, 4)
                        if r == 0 and j:
                            act.wait_ge(conv_done, j)
                        ins = nc.scalar.activation(cz[:, which, half * BANK:(half + 1) * BANK], ps[:, g % NB, :],
                                                   ACT.Silu if which == 3 else ACT.Copy)
                    ins.then_inc(freed, 1)
                    if g < n_v:
                        act.wait_ge(freed, g + 1)
                        act.dma_start(v_rows[t, :, a:a + wd], v_sb[:, m % 2, 0:wd]).then_inc(v_out[m % 2], 16)
                for b in range(2):
                    act.wait_ge(qk_out[b], 16 * n_qk // 2)
                    act.wait_ge(v_out[b], 16 * (n_v - n_qk) // 2)


def attention(c, qk_dram, v_dram, mixT, next_weights):
    nc, io = c.nc, c.io
    steps = [(hp * 2 + h, hp, a) for hp in range(NH // 2) for a in range(NT) for h in range(2)]
    N = len(steps)
    with ExitStack() as s:
        logc = s.enter_context(nc.sbuf_tensor("logc", [P, S], F32))
        qk = s.enter_context(nc.sbuf_tensor("att_qk", [P, 2, 2, S], F32))
        v = s.enter_context(nc.sbuf_tensor("att_v", [P, 2, NT, P], F32))
        sc = s.enter_context(nc.sbuf_tensor("att_scores", [P, 3, S], F32))
        pT = s.enter_context(nc.sbuf_tensor("att_pT", [P, 2, S], F32))
        mx = s.enter_context(nc.sbuf_tensor("att_max", [P, N], F32))
        nmx = s.enter_context(nc.sbuf_tensor("att_negmax", [P, N], F32))
        den = s.enter_context(nc.sbuf_tensor("att_den", [P, N], F32))
        rden = s.enter_context(nc.sbuf_tensor("att_rden", [P, N], F32))
        on = s.enter_context(nc.sbuf_tensor("att_out", [P, 2, P], F32))
        ps_s = s.enter_context(nc.psum_tensor("att_ps_s", [P, 2, S], F32))
        ps_t = s.enter_context(nc.psum_tensor("att_ps_t", [P, S], F32))
        ps_o = s.enter_context(nc.psum_tensor("att_ps_o", [P, BANK], F32))
        ps_m = s.enter_context(nc.psum_tensor("att_ps_m", [P, BANK], F32))
        logc_in, pair_in = c.sem("logc_in"), [c.sem(f"att_pair_in{b}") for b in range(2)]
        scored, maxed, expd = c.sem("att_scored"), c.sem("att_maxed"), c.sem("att_expd")
        turned, kept = c.sem("att_turned"), c.sem("att_kept")
        summed, normed = c.sem("att_summed"), c.sem("att_normed")
        pair_turned, pair_kept = c.sem("att_pair_turned"), c.sem("att_pair_kept")
        with nc.Block() as block:
            @block.sync
            def _(sp):
                sp.dma_start(logc[:, :], c.const_dram("logc")).then_inc(logc_in, 16)
                for hp in range(NH // 2):
                    if hp >= 2:
                        sp.wait_ge(summed, 2 * NT * (hp - 1))
                    for k in range(2):
                        sp.dma_start(qk[:, hp % 2, k, :], qk_dram[k * AW // P + hp]).then_inc(pair_in[hp % 2], 16)
                    sp.dma_start(v[:, hp % 2, :, :], v_dram[:, hp * P:(hp + 1) * P].rearrange("(t p) d -> p t d", p=P)
                                 ).then_inc(pair_in[hp % 2], 16)
                    if hp == 1:
                        next_weights.load(sp)

            @block.gpsimd
            def _(pool):
                next_weights.prepare(pool)

            @block.tensor
            def _(pe):
                def scores(i):
                    h, hp, a = steps[i]
                    lo, n = HD * (h % 2), (a + 1) * P
                    if i % (2 * NT) == 0:
                        pe.wait_ge(pair_in[hp % 2], 48 * (hp // 2 + 1))
                    if i >= 2:
                        pe.wait_ge(maxed, i - 1)
                    for u in range(0, n, BANK):
                        m = min(BANK, n - u)
                        ins = pe.matmul(ps_s[:, i % 2, u:u + m], qk[lo:lo + HD, hp % 2, 0, a * P:(a + 1) * P],
                                        qk[lo:lo + HD, hp % 2, 1, u:u + m], start=True, stop=True)
                    ins.then_inc(scored, 1)

                def turn(i):
                    a = steps[i][2]
                    pe.wait_ge(expd, i + 1)
                    if i >= 1:
                        pe.wait_ge(kept, i)
                    for j in range(a + 1):
                        ins = pe.transpose(ps_t[:, j * P:(j + 1) * P], sc[:, i % 3, j * P:(j + 1) * P],
                                           c.const("ident"))
                    ins.then_inc(turned, 1)

                def values(i):
                    h, hp, a = steps[i]
                    pe.wait_ge(kept, i + 1)
                    if i >= 1:
                        pe.wait_ge(normed, i)
                    at = (i % 2) * HD
                    for j in range(a + 1):
                        ins = pe.matmul(ps_o[:, at:at + HD], pT[:, i % 2, j * P:(j + 1) * P],
                                        v[:, hp % 2, j, HD * (h % 2):HD * (h % 2) + HD], start=(j == 0), stop=(j == a))
                    ins.then_inc(summed, 1)

                def pair(m):
                    pe.wait_ge(normed, 2 * m + 2)
                    if m >= 1:
                        pe.wait_ge(pair_kept, m)
                    pe.transpose(ps_m[:, 0:P], on[:, m % 2, :], c.const("ident")).then_inc(pair_turned, 1)

                for i in range(N + 4):
                    if i < N:
                        scores(i)
                    if 1 <= i <= N:
                        turn(i - 1)
                    if 2 <= i <= N + 1:
                        values(i - 2)
                    if i >= 4 and i % 2 == 0:
                        pair((i - 4) // 2)

            @block.vector
            def _(dve):
                dve.wait_ge(logc_in, 16)

                def maxes(i):
                    a = steps[i][2]
                    n = (a + 1) * P
                    dve.wait_ge(scored, i + 1)
                    if i >= 3:
                        dve.wait_ge(turned, i - 2)
                    c.vstep(dve, nc.vector.tensor_tensor_reduce(sc[:, i % 3, 0:n], ps_s[:, i % 2, 0:n], logc[:, S - n:S],
                                                                SCALE, NEG, ALU.add, ALU.max, mx[:, i:i + 1]))
                    nc.vector.tensor_scalar(nmx[:, i:i + 1], mx[:, i:i + 1], -1.0, None, ALU.mult).then_inc(maxed, 1)

                def norm(i):
                    h, hp, a = steps[i]
                    m, at = i // 2, (i % 2) * HD
                    dve.wait_ge(expd, i + 1)
                    c.vstep(dve, nc.vector.reciprocal(rden[:, i:i + 1], den[:, i:i + 1]))
                    dve.wait_ge(summed, i + 1)
                    if m >= 2:
                        dve.wait_ge(pair_turned, m - 1)
                    nc.vector.tensor_scalar(on[:, m % 2, at:at + HD], ps_o[:, at:at + HD], rden[:, i:i + 1], None,
                                            ALU.mult).then_inc(normed, 1)

                def gate(m):
                    h, hp, a = steps[2 * m]
                    dve.wait_ge(pair_turned, m + 1)
                    nc.vector.tensor_tensor(mixT[:, hp, a * P:(a + 1) * P], ps_m[:, 0:P], mixT[:, hp, a * P:(a + 1) * P],
                                            ALU.mult).then_inc(pair_kept, 1)

                for i in range(N + 4):
                    if i < N:
                        maxes(i)
                    if 2 <= i <= N + 1:
                        norm(i - 2)
                    if i >= 4 and i % 2 == 0:
                        gate((i - 4) // 2)

            @block.scalar
            def _(act):
                for i in range(N + 1):
                    if i < N:
                        n = (steps[i][2] + 1) * P
                        act.wait_ge(maxed, i + 1)
                        nc.scalar.activation(sc[:, i % 3, 0:n], sc[:, i % 3, 0:n], ACT.Exp, bias=nmx[:, i:i + 1],
                                             accum_out=den[:, i:i + 1]).then_inc(expd, 1)
                    if i >= 1:
                        n = (steps[i - 1][2] + 1) * P
                        act.wait_ge(turned, i)
                        if i >= 3:
                            act.wait_ge(summed, i - 2)
                        nc.scalar.activation(pT[:, (i - 1) % 2, 0:n], ps_t[:, 0:n], ACT.Copy).then_inc(kept, 1)


def out_weights(c, stack, tag, w, side=None):
    sources = [([by_chunks(w, n * BANK, (n + 1) * BANK)], BANK) for n in range(2)]
    return Weights(c, stack, tag, sources, [], R=2 * KC, pre=2 * KC, side=side)


def project_out(c, tag, weights, mT, src, dst, post_gain=None):
    nc = c.nc
    src_t, dst_t = src.rearrange("(t p) d -> t p d", p=P), dst.rearrange("(t p) d -> t p d", p=P)
    with ExitStack() as s:
        m = Split(nc, s, f"{tag}_m", [P, 2, KC, P])
        x = s.enter_context(nc.sbuf_tensor(f"{tag}_x", [P, 2, D], F32))
        y = s.enter_context(nc.sbuf_tensor(f"{tag}_y", [P, 2, D], F32))
        if post_gain is not None:
            sq = s.enter_context(nc.sbuf_tensor(f"{tag}_sq", [P, D], F32))
            g = s.enter_context(nc.sbuf_tensor(f"{tag}_g", [P, D], F32))
        ss = s.enter_context(nc.sbuf_tensor(f"{tag}_ss", [P, 3 * NT], F32))
        eps = s.enter_context(nc.sbuf_tensor(f"{tag}_eps", [P, 1], F32))
        ps = s.enter_context(nc.psum_tensor(f"{tag}_ps", [P, 3, D], F32))
        g_in, x_in = c.sem(f"{tag}_g_in"), [c.sem(f"{tag}_x_in{b}") for b in range(2)]
        y_out = [c.sem(f"{tag}_y_out{b}") for b in range(2)]
        done, rms_ready, y_ready = c.sem(f"{tag}_done"), c.sem(f"{tag}_rms"), c.sem(f"{tag}_y_ready")
        eps_ready, rounded, rest = c.sem(f"{tag}_eps_ready"), c.sem(f"{tag}_rounded"), c.sem(f"{tag}_rest")
        with nc.Block() as block:
            @block.sync
            def _(sp):
                if post_gain is not None:
                    sp.dma_start(g[:, :], post_gain.partition_broadcast(P)).then_inc(g_in, 16)
                for t in range(NT + 1):
                    if t < NT:
                        if t >= 2:
                            sp.wait_ge(y_ready, t - 1)
                        sp.dma_start(x[:, t % 2, :], src_t[t]).then_inc(x_in[t % 2], 16)
                    if t >= 1:
                        sp.wait_ge(y_ready, t)
                        sp.dma_start(dst_t[t - 1], y[:, (t - 1) % 2, :]).then_inc(y_out[(t - 1) % 2], 16)
                for b in range(2):
                    sp.wait_ge(y_out[b], 16 * NT // 2)

            @block.gpsimd
            def _(pool):
                for t in range(NT):
                    pool.wait_ge(rounded, t + 1)
                    nc.gpsimd.tensor_tensor(m.lo[:, t % 2, :, :], mT[:, :, t * P:(t + 1) * P],
                                            m.hi[:, t % 2, :, :].bitcast(F32), ALU.subtract).then_inc(rest, 1)

            @block.tensor
            def _(pe):
                pe.wait_ge(weights.lo_done, 2 * KC)
                for t in range(NT):
                    pe.wait_ge(rest, t + 1)
                    if t >= 3:
                        pe.wait_ge(y_ready, t - 2)
                    for n in range(2):
                        for k in range(KC):
                            slot = KC * n + k
                            ins = products(pe, ps[:, t % 3, n * BANK:(n + 1) * BANK],
                                           (m.hi[:, t % 2, k, :], m.lo[:, t % 2, k, :]),
                                           (weights.hi[:, slot, :], weights.lo[:, slot, :]), k == 0, k == KC - 1)
                    ins.then_inc(done, 1)

            @block.scalar
            def _(act):
                def round_hi(t):
                    if t >= 2:
                        act.wait_ge(done, t - 1)
                    nc.scalar.activation(m.hi[:, t % 2, :, :], mT[:, :, t * P:(t + 1) * P], ACT.Copy).then_inc(rounded, 1)

                act.wait_ge(eps_ready, 1)
                round_hi(0)
                round_hi(1)
                for t in range(NT):
                    act.wait_ge(done, t + 1)
                    if t + 2 < NT:
                        round_hi(t + 2)
                    if post_gain is not None:
                        c.astep(act, nc.scalar.activation(sq[:, :], ps[:, t % 3, :], ACT.Square,
                                                          accum_out=ss[:, t:t + 1]))
                        nc.scalar.activation(ss[:, NT + t:NT + t + 1], ss[:, t:t + 1], ACT.Sqrt, scale=1.0 / D,
                                             bias=eps[:, :]).then_inc(rms_ready, 1)

            @block.vector
            def _(dve):
                nc.vector.memset(eps[:, :], EPS).then_inc(eps_ready, 1)
                if post_gain is not None:
                    dve.wait_ge(g_in, 16)
                for t in range(NT):
                    dve.wait_ge(done, t + 1)
                    if t >= 2:
                        dve.wait_ge(y_out[t % 2], 16 * (t // 2))
                    dve.wait_ge(x_in[t % 2], 16 * (t // 2 + 1))
                    yt = y[:, t % 2, :]
                    if post_gain is None:
                        nc.vector.tensor_tensor(yt, ps[:, t % 3, :], x[:, t % 2, :], ALU.add).then_inc(y_ready, 1)
                    else:
                        dve.wait_ge(rms_ready, t + 1)
                        r = ss[:, 2 * NT + t:2 * NT + t + 1]
                        c.vstep(dve, nc.vector.reciprocal(r, ss[:, NT + t:NT + t + 1]))
                        c.vstep(dve, nc.vector.scalar_tensor_tensor(yt, ps[:, t % 3, :], r, g[:, :], ALU.mult, ALU.mult))
                        nc.vector.tensor_tensor(yt, yt, x[:, t % 2, :], ALU.add).then_inc(y_ready, 1)


def first_block(c, x, x1, qk_dram, v_dram):
    nc, io = c.nc, c.io
    with ExitStack() as s:
        mixT = s.enter_context(nc.sbuf_tensor("mixT", [P, KC, S], F32))
        with ExitStack() as s2:
            weights = first_weights(c, s2)
            hT = Split(nc, s2, "hT", [P, KC, S])
            norm_transposed(c, "n1", x, io["norm_pre_g"], hT, next_weights=weights)
            project_first(c, weights, hT, qk_dram, v_dram, mixT)
        weights = out_weights(c, s, "o1", io["w_out"])
        attention(c, qk_dram, v_dram, mixT, weights)
        project_out(c, "o1", weights, mixT, x, x1, post_gain=io["norm_post_g"])


IF_AT, U_AT, SV_AT, GA_AT, GB_AT = 4 * D, 4 * D + 8, 5 * D + 8, 6 * D + 8, 7 * D + 8
V_AT, O_AT = 2 * D, 3 * D


def row_panels(w, at, panel0):
    sources = [([by_rows(w, at + n * BANK, at + (n + 1) * BANK)], BANK) for n in range(D // BANK)]
    groups = [(panel0 + n, "rows", 0, BANK, t) for n in range(D // BANK) for t in range(NT)]
    return sources, groups


def mixer_weights(c, stack):
    w = c.io["w_in_2"]
    sources, groups = [], []
    for at in (SV_AT, U_AT, GB_AT):
        a, b = row_panels(w, at, len(sources))
        sources, groups = sources + a, groups + b
    for n in range(D // BANK):
        for at in (O_AT, GA_AT):
            groups += [(len(sources), "rows", 0, BANK, t) for t in range(NT)]
            sources.append(([by_rows(w, at + n * BANK, at + (n + 1) * BANK)], BANK))
    a, b = row_panels(w, V_AT, len(sources))
    sources, groups = sources + a, groups + b
    for n in range(2 * D // BANK):
        for sub in range(BANK // P):
            groups += [(len(sources), "cols", sub * P, BANK, half) for half in range(2)]
        sources.append(([by_rows(w, n * BANK, (n + 1) * BANK)], BANK))
    return Weights(c, stack, "p2", sources, groups)


SGU_PANELS, GATE_PANELS, QKV_PANELS = (0, 6), (6, 10), (10, 16)


def spatial_gate(c, weights, hT, yb_dram):
    nc, io = c.nc, c.io
    groups = weights.groups
    span, halves, chunks = weights.part(*SGU_PANELS)
    per = len(span) // 3
    NB = 4
    yb_t = yb_dram.rearrange("(t p) d -> t p d", p=P)
    with ExitStack() as s:
        sv = s.enter_context(nc.sbuf_tensor("sgu_v", [P, NT, D], F32))
        gb = s.enter_context(nc.sbuf_tensor("sgu_gate", [P, NB, BANK], F32))
        gbias = s.enter_context(nc.sbuf_tensor("sgu_gate_bias", [P, D], F32))
        gain = s.enter_context(nc.sbuf_tensor("sgu_gain", [P, D], F32))
        sq = s.enter_context(nc.sbuf_tensor("sgu_sq", [P, D], F32))
        ws = s.enter_context(nc.sbuf_tensor("sgu_ws", [P, 8, P], F32))
        bs = s.enter_context(nc.sbuf_tensor("sgu_bs", [P, 8], F32))
        ss = s.enter_context(nc.sbuf_tensor("sgu_ss", [P, 2 * NT], F32))
        eps = s.enter_context(nc.sbuf_tensor("sgu_eps", [P, 1], F32))
        ps = s.enter_context(nc.psum_tensor("sgu_ps", [P, NB, BANK], F32))
        pm = s.enter_context(nc.psum_tensor("sgu_pm", [P, 4, BANK], F32))
        done, freed = weights.done, weights.freed
        small_in = c.sem("sgu_small_in")
        eps_ready, ws_ready, v_ready = c.sem("sgu_eps_ready"), c.sem("sgu_ws_ready"), c.sem("sgu_v_ready")
        rms_ready, gated = c.sem("sgu_rms"), c.sem("sgu_gated")
        gate_ready, mixed, mix_kept = c.sem("sgu_gate_ready"), c.sem("sgu_mixed"), c.sem("sgu_mix_kept")
        y_out = c.sem("sgu_y_out")
        with nc.Block() as block:
            @block.sync
            def _(sp):
                weights.load(sp, *halves)
                for t in range(NT):
                    sp.wait_ge(gated, per + NT + t + 1)
                    sp.dma_start(yb_t[t], sv[:, t, :]).then_inc(y_out, 16)
                sp.wait_ge(y_out, 16 * NT)

            @block.gpsimd
            def _(pool):
                pool.dma_start(gain[:, :], io["sgu_norm_g_2"].partition_broadcast(P)).then_inc(small_in, 16)
                pool.dma_start(gbias[:, :], io["b_gate_2"][D:2 * D].partition_broadcast(P)).then_inc(small_in, 16)
                pool.dma_start(ws[:, :, :], io["w_s_T"].rearrange("g s t -> s g t")).then_inc(small_in, 16)
                with nc.allow_non_contiguous_dma(reason="1024 biases, once"):
                    pool.dma_start(bs[:, :].unsqueeze(2), io["b_s_2"].rearrange("g (t o) -> t g o", o=1)
                                   ).then_inc(small_in, 16)
                weights.take_los(pool, chunks)

            @block.tensor
            def _(pe):
                for g in matmul_groups(pe, weights, hT, ps, NB, span):
                    if g == per + NB - 1:
                        pe.wait_ge(ws_ready, 1)
                        pe.wait_ge(v_ready, NT)
                        for n in range(16):
                            sg, half = divmod(n, 2)
                            if n >= 4:
                                pe.wait_ge(mix_kept, n - 3)
                            pe.matmul(pm[:, n % 4, :].rearrange("p (c d) -> p c d", c=4), ws[:, sg, :],
                                      sv[:, 4 * half:4 * half + 4, sg * P:(sg + 1) * P], start=True, stop=True
                                      ).then_inc(mixed, 1)

            @block.scalar
            def _(act):
                act.wait_ge(eps_ready, 1)
                weights.before(act, 0)
                for g in span:
                    i, kind, a, wd, t = groups[g]
                    n = i % 2
                    if g + 1 < span.stop:
                        weights.before(act, g + 1)
                    if g >= per + NB and g < 2 * per:
                        act.wait_ge(gated, g - NB - per + 1)
                    if g < 2 * per:
                        act.wait_ge(done, g + 1)
                        dst = sv[:, t, n * BANK:(n + 1) * BANK] if g < per else gb[:, g % NB, :]
                        nc.scalar.activation(dst, ps[:, g % NB, :], ACT.Gelu_apprx_tanh).then_inc(freed, 1)
                    else:
                        act.wait_ge(freed, g + 1)
                        nc.scalar.activation(gb[:, g % NB, :], gb[:, g % NB, :], ACT.Sigmoid).then_inc(gate_ready, 1)
                    if g < per and n == 1:
                        act.wait_ge(freed, g + 1)
                        c.astep(act, nc.scalar.activation(sq[:, :], sv[:, t, :], ACT.Square,
                                                          accum_out=ss[:, t:t + 1]))
                    if g == per - 1:
                        nc.scalar.activation(ss[:, NT:], ss[:, 0:NT], ACT.Sqrt, scale=1.0 / D,
                                             bias=eps[:, :]).then_inc(rms_ready, 1)

            @block.vector
            def _(dve):
                nc.vector.memset(eps[:, :], EPS).then_inc(eps_ready, 1)
                dve.wait_ge(small_in, 64)
                nc.vector.tensor_tensor(ws[:, :, :], ws[:, :, :], c.const("causal").unsqueeze(1).to_broadcast([P, 8, P]),
                                        ALU.mult).then_inc(ws_ready, 1)
                dve.wait_ge(rms_ready, 1)
                c.vstep(dve, nc.vector.reciprocal(ss[:, 0:NT], ss[:, NT:]))
                for t in range(NT):
                    nc.vector.scalar_tensor_tensor(sv[:, t, :], sv[:, t, :], ss[:, t:t + 1], gain[:, :],
                                                   ALU.mult, ALU.mult).then_inc(v_ready, 1)
                for n in range(16):
                    sg, half = divmod(n, 2)
                    dve.wait_ge(mixed, n + 1)
                    nc.vector.tensor_scalar(sv[:, 4 * half:4 * half + 4, sg * P:(sg + 1) * P],
                                            pm[:, n % 4, :].rearrange("p (c d) -> p c d", c=4), bs[:, sg:sg + 1],
                                            None, ALU.add).then_inc(mix_kept, 1)
                dve.wait_ge(mix_kept, 16)
                for g in range(per, 3 * per + 1):
                    if 2 * per <= g < 3 * per:
                        n = groups[g][0] % 2
                        dve.wait_ge(done, g + 1)
                        dve.wait_ge(gated, g - per - NB + 1)
                        dve.wait_ge(freed, g)
                        nc.vector.tensor_tensor(gb[:, g % NB, :], ps[:, g % NB, :], gbias[:, n * BANK:(n + 1) * BANK],
                                                ALU.add).then_inc(freed, 1)
                    if g > per:
                        i, kind, a, wd, t = groups[g - 1]
                        n = i % 2
                        if g - 1 < 2 * per:
                            dve.wait_ge(freed, g)
                        else:
                            dve.wait_ge(gate_ready, g - 2 * per)
                        y = sv[:, t, n * BANK:(n + 1) * BANK]
                        if g > 2 * per:
                            dve.wait_ge(gated, g - 2 * per)
                        nc.vector.tensor_tensor(y, y, gb[:, (g - 1) % NB, :], ALU.mult).then_inc(gated, 1)


def output_gate(c, weights, hT, og_dram):
    nc, io = c.nc, c.io
    groups = weights.groups
    span, halves, chunks = weights.part(*GATE_PANELS)
    NB = 4
    og_t = og_dram.rearrange("(t p) d -> t p d", p=P)
    with ExitStack() as s:
        og = s.enter_context(nc.sbuf_tensor("og", [P, NT, D], F32))
        ga = s.enter_context(nc.sbuf_tensor("og_gate", [P, NB, BANK], F32))
        gbias = s.enter_context(nc.sbuf_tensor("og_bias", [P, D], F32))
        ps = s.enter_context(nc.psum_tensor("og_ps", [P, NB, BANK], F32))
        done, freed = weights.done, weights.freed
        bias_in, gate_ready, gated, out = c.sem("og_bias_in"), c.sem("og_gate_ready"), c.sem("og_gated"), c.sem("og_out")
        with nc.Block() as block:
            @block.sync
            def _(sp):
                sp.dma_start(gbias[:, :], io["b_gate_2"][0:D].partition_broadcast(P)).then_inc(bias_in, 16)
                weights.load(sp, *halves)
                for t in range(NT):
                    sp.wait_ge(gated, NT + t + 1)
                    sp.dma_start(og_t[t], og[:, t, :]).then_inc(out, 16)
                sp.wait_ge(out, 16 * NT)

            @block.gpsimd
            def _(pool):
                weights.take_los(pool, chunks)

            @block.tensor
            def _(pe):
                for g in matmul_groups(pe, weights, hT, ps, NB, span):
                    pass

            @block.scalar
            def _(act):
                gates = 0
                weights.before(act, span.start)
                for g in span:
                    i, kind, a, wd, t = groups[g]
                    if g + 1 < span.stop:
                        weights.before(act, g + 1)
                    if (i - GATE_PANELS[0]) % 2 == 0:
                        act.wait_ge(done, g + 1)
                        act.wait_ge(freed, g)
                        n = (i - GATE_PANELS[0]) // 2
                        nc.scalar.activation(og[:, t, n * BANK:(n + 1) * BANK], ps[:, g % NB, :],
                                             ACT.Sigmoid).then_inc(freed, 1)
                    else:
                        gates += 1
                        act.wait_ge(freed, g + 1)
                        nc.scalar.activation(ga[:, g % NB, :], ga[:, g % NB, :], ACT.Sigmoid).then_inc(gate_ready, 1)

            @block.vector
            def _(dve):
                dve.wait_ge(bias_in, 16)
                gates = 0
                for g in span:
                    i, kind, a, wd, t = groups[g]
                    if (i - GATE_PANELS[0]) % 2 == 0:
                        continue
                    n = (i - GATE_PANELS[0]) // 2
                    dve.wait_ge(done, g + 1)
                    dve.wait_ge(freed, g)
                    nc.vector.tensor_tensor(ga[:, g % NB, :], ps[:, g % NB, :], gbias[:, n * BANK:(n + 1) * BANK],
                                            ALU.add).then_inc(freed, 1)
                    gates += 1
                    dve.wait_ge(gate_ready, gates)
                    oo = og[:, t, n * BANK:(n + 1) * BANK]
                    nc.vector.tensor_tensor(oo, oo, ga[:, g % NB, :], ALU.mult).then_inc(gated, 1)


R_I, R_F, R_B, R_A = range(4)
R_WS, R_IW, R_T, R_FLOOR = R_I, R_F, R_A, R_B


def project_qkv(c, weights, hT, qk_dram, v_dram, maxima, cols, decay):
    nc, io = c.nc, c.io
    w = io["w_in_2"]
    groups = weights.groups
    span, halves, chunks_ = weights.part(*QKV_PANELS)
    g0 = span.start
    n_v = g0 + 2 * NT
    NB, NSUB, TAPS = 4, 2 * D // P, 4
    v_rows = v_dram.rearrange("(t p) d -> t p d", p=P)
    with ExitStack() as s:
        rows = s.enter_context(nc.sbuf_tensor("ml_rows", [MH, 4, S], F32))
        m = s.enter_context(nc.sbuf_tensor("ml_m", [MH, NT + 1], F32))
        dec = s.enter_context(nc.sbuf_tensor("ml_decay", [MH, NT], F32))
        v_sb = s.enter_context(nc.sbuf_tensor("qkv_v", [P, 2, BANK], F32))
        z = s.enter_context(nc.sbuf_tensor("qk_z", [P, 2, S + 3], F32))
        y = s.enter_context(nc.sbuf_tensor("qk_y", [P, 2, S], F32))
        cw = s.enter_context(nc.sbuf_tensor("qk_taps", [P, TAPS, NSUB], F32))
        cb = s.enter_context(nc.sbuf_tensor("qk_bias", [P, NSUB], F32))
        wif = s.enter_context(nc.sbuf_tensor("w_if", [P, KC, 36], F32))
        wif_split = Split(nc, s, "w_if", [P, KC, 36])
        bif = s.enter_context(nc.sbuf_tensor("b_if", [36, 1], F32))
        ps = s.enter_context(nc.psum_tensor("qkv_ps", [P, NB, BANK], F32))
        pif = s.enter_context(nc.psum_tensor("if_ps", [P, 2, BANK], F32))
        pc = s.enter_context(nc.psum_tensor("ml_pc", [P, NT, 4, MH], F32))
        pd = s.enter_context(nc.psum_tensor("ml_pd", [P, MH, NT], F32))
        small_in, if_in, wif_ready = c.sem("qkv_small_in"), c.sem("if_in"), c.sem("wif_ready")
        done, freed, if_done = weights.done, weights.freed, c.sem("if_done")
        pads, conv_ready, silu_done = c.sem("qk_pads"), c.sem("qk_conv_ready"), c.sem("qk_silu_done")
        qk_out, v_out = [c.sem(f"qk2_out{b}") for b in range(2)], [c.sem(f"v2_out{b}") for b in range(2)]
        absd, expd, lnd = c.sem("ml_absd"), c.sem("ml_expd"), c.sem("ml_lnd")
        diffs, row_weights, turned = c.sem("ml_diffs"), c.sem("ml_weights"), c.sem("ml_turned")

        def by_chunk(r):
            return r.rearrange("p (c n) -> p c n", c=NT)

        with nc.Block() as block:
            @block.sync
            def _(sp):
                weights.load(sp, *halves)

            @block.gpsimd
            def _(pool):
                nc.gpsimd.memset(wif[:, :, :], 0.0).then_inc(wif_ready, 1)
                pool.wait_ge(wif_ready, 1)
                for k in range(2):
                    at = IF_AT + 4 * k
                    with nc.allow_non_contiguous_dma(reason="8 columns, once"):
                        pool.dma_start(wif[:, :, 32 * k:32 * k + 4], by_rows(w, at, at + 4)).then_inc(if_in, 16)
                        pool.dma_start(bif[32 * k:32 * k + 4, :],
                                       io["b_if_2"][4 * k:4 * k + 4].rearrange("(h o) -> h o", o=1)).then_inc(if_in, 16)
                with nc.allow_non_contiguous_dma(reason="the taps, once"):
                    for j in range(TAPS):
                        pool.dma_start(cw[:, j, :].unsqueeze(2), io["conv_w_2"][j].rearrange("(k p o) -> p k o", p=P, o=1)
                                       ).then_inc(small_in, 16)
                    pool.dma_start(cb[:, :].unsqueeze(2), io["conv_b_2"].rearrange("(k p o) -> p k o", p=P, o=1)
                                   ).then_inc(small_in, 16)
                pool.wait_ge(if_in, 64)
                nc.gpsimd.tensor_copy(wif_split.hi[:, :, :], wif[:, :, :]).then_inc(wif_ready, 1)
                pool.wait_ge(wif_ready, 2)
                nc.gpsimd.tensor_tensor(wif_split.lo[:, :, :], wif[:, :, :], wif_split.hi[:, :, :].bitcast(F32),
                                        ALU.subtract).then_inc(wif_ready, 1)
                weights.take_los(pool, chunks_)

            @block.tensor
            def _(pe):
                for g in matmul_groups(pe, weights, hT, ps, NB, span):
                    if g == g0:
                        pe.wait_ge(wif_ready, 3)
                        for half in range(2):
                            sl = slice(half * BANK, (half + 1) * BANK)
                            for k in range(KC):
                                ins = products(pe, pif[0:36, half, :], (wif_split.hi[:, k, :], wif_split.lo[:, k, :]),
                                               (hT.hi[:, k, sl], hT.lo[:, k, sl]), k == 0, k == KC - 1)
                        ins.then_inc(if_done, 1)
                    if g == n_v:
                        pe.wait_ge(row_weights, 1)
                        for t in range(NT):
                            for n, r in enumerate((R_A, R_IW, R_FLOOR, R_WS)):
                                pe.transpose(pc[:, t, n, :], rows[:, r, t * P:(t + 1) * P],
                                             c.const("ident")[0:MH, 0:MH])
                        for h in range(MH):
                            ins = pe.matmul(pd[:, h, :], c.const("sel")[0:MH, h * P:(h + 1) * P], dec[:, :],
                                            start=True, stop=True)
                        ins.then_inc(turned, 1)

            @block.scalar
            def _(act):
                def silu(j):
                    act.wait_ge(conv_ready, j + 1)
                    nc.scalar.activation(y[:, j % 2, :], y[:, j % 2, :], ACT.Silu, bias=cb[:, j:j + 1]
                                         ).then_inc(silu_done, 1)
                    act.wait_ge(silu_done, j + 1)
                    act.dma_start(qk_dram[j], y[:, j % 2, :]).then_inc(qk_out[j % 2], 16)

                def row_step(g):
                    if g == g0 + 2:
                        act.wait_ge(absd, 1)
                        nc.scalar.activation(rows[:, R_T, :], rows[:, R_T, :], ACT.Exp, scale=-1.0).then_inc(expd, 1)
                    if g == g0 + 3:
                        act.wait_ge(absd, 2)
                        nc.scalar.activation(rows[:, R_T, :], rows[:, R_T, :], ACT.Ln).then_inc(lnd, 1)
                    if g == g0 + 10:
                        act.wait_ge(diffs, 1)
                        for r in (R_IW, R_FLOOR, R_WS):
                            nc.scalar.activation(rows[:, r, :], rows[:, r, :], ACT.Exp)
                        nc.scalar.activation(dec[:, :], dec[:, :], ACT.Exp).then_inc(row_weights, 1)

                weights.before(act, g0)
                for g in span:
                    i, kind, a, wd, t = groups[g]
                    if g + 1 < span.stop:
                        weights.before(act, g + 1)
                    act.wait_ge(done, g + 1)
                    if g < n_v:
                        n, slot = i % 2, g % 2
                        if g >= g0 + 2:
                            act.wait_ge(v_out[slot], 16 * ((g - g0) // 2))
                        nc.scalar.activation(v_sb[:, slot, :], ps[:, g % NB, :], ACT.Copy).then_inc(freed, 1)
                        act.wait_ge(freed, g + 1)
                        act.dma_start(v_rows[t, :, n * BANK:(n + 1) * BANK], v_sb[:, slot, :]).then_inc(v_out[slot], 16)
                        row_step(g)
                    else:
                        j, half = divmod(g - n_v, 2)
                        if g == n_v:
                            act.wait_ge(small_in, 16 * (TAPS + 1))
                            act.wait_ge(pads, 1)
                        if j >= 2:
                            act.wait_ge(conv_ready, j - 1)
                        nc.scalar.activation(z[:, j % 2, 3 + half * BANK:3 + (half + 1) * BANK], ps[:, g % NB, :],
                                             ACT.Copy).then_inc(freed, 1)
                        if half == 1 and j >= 1:
                            silu(j - 1)
                silu(NSUB - 1)
                for b in range(2):
                    act.wait_ge(v_out[b], 16 * NT)
                    act.wait_ge(qk_out[b], 16 * NSUB // 2)

            @block.vector
            def _(dve):
                nc.vector.memset(z[:, :, 0:3], 0.0).then_inc(pads, 1)
                dve.wait_ge(small_in, 16 * (TAPS + 1))
                dve.wait_ge(if_done, 1)
                nc.vector.tensor_scalar(rows[:, R_I, :], pif[0:MH, :, :].rearrange("p a n -> p (a n)"), bif[0:MH, :],
                                        None, ALU.add)
                c.vstep(dve, nc.vector.tensor_scalar(rows[:, R_F, :], pif[32:32 + MH, :, :].rearrange("p a n -> p (a n)"),
                                                     bif[32:32 + MH, :], None, ALU.add))
                nc.vector.scalar_tensor_tensor(rows[:, R_T, :], rows[:, R_F, :], -1.0, rows[:, R_F, :],
                                               ALU.mult, ALU.max).then_inc(absd, 1)
                dve.wait_ge(expd, 1)
                nc.vector.tensor_scalar(rows[:, R_T, :], rows[:, R_T, :], 1.0, None, ALU.add).then_inc(absd, 1)
                dve.wait_ge(lnd, 1)
                c.vstep(dve, nc.vector.scalar_tensor_tensor(rows[:, R_F, :], rows[:, R_F, :], 0.0, rows[:, R_T, :],
                                                            ALU.min, ALU.subtract))
                one = c.const("ones")[0:MH, :]
                for t in range(NT):
                    sl = slice(t * P, (t + 1) * P)
                    ins = nc.vector.tensor_tensor_scan(rows[:, R_B, sl], one, rows[:, R_F, sl], 0.0, ALU.mult, ALU.add)
                c.vstep(dve, ins)
                nc.vector.memset(m[:, 0:1], 0.0)
                c.vstep(dve, nc.vector.tensor_tensor(rows[:, R_A, :], rows[:, R_I, :], rows[:, R_B, :], ALU.subtract))
                for t in range(NT):
                    sl = slice(t * P, (t + 1) * P)
                    last = slice((t + 1) * P - 1, (t + 1) * P)
                    c.vstep(dve, nc.vector.tensor_tensor_scan(maxima[:, sl], one, rows[:, R_A, sl], m[:, t:t + 1],
                                                              ALU.mult, ALU.max))
                    c.vstep(dve, nc.vector.tensor_tensor(m[:, t + 1:t + 2], rows[:, R_B, last], maxima[:, last],
                                                         ALU.add))
                before = m[:, 0:NT]
                final = by_chunk(maxima[:, :])[:, :, P - 1]
                nc.vector.tensor_tensor(by_chunk(rows[:, R_IW, :]), before.unsqueeze(2).to_broadcast([MH, NT, P]),
                                        by_chunk(maxima[:, :]), ALU.subtract)
                nc.vector.tensor_tensor(by_chunk(rows[:, R_WS, :]), by_chunk(rows[:, R_A, :]),
                                        final.unsqueeze(2).to_broadcast([MH, NT, P]), ALU.subtract)
                nc.vector.tensor_tensor(dec[:, :], before, final, ALU.subtract)
                c.vstep(dve, nc.vector.tensor_tensor(rows[:, R_FLOOR, :], rows[:, R_B, :], maxima[:, :], ALU.add))
                nc.vector.tensor_scalar(rows[:, R_FLOOR, :], rows[:, R_FLOOR, :], -1.0, None, ALU.mult).then_inc(diffs, 1)
                for j in range(NSUB):
                    dve.wait_ge(freed, n_v + 2 * (j + 1))
                    if j >= 2:
                        dve.wait_ge(qk_out[j % 2], 16 * (j // 2))
                    zz, yy = z[:, j % 2, :], y[:, j % 2, :]
                    c.vstep(dve, nc.vector.tensor_scalar(yy, zz[:, 0:S], cw[:, 0, j:j + 1], None, ALU.mult))
                    for tap in range(1, TAPS):
                        ins = nc.vector.scalar_tensor_tensor(yy, zz[:, tap:tap + S], cw[:, tap, j:j + 1], yy,
                                                             ALU.mult, ALU.add)
                        if tap < TAPS - 1:
                            c.vstep(dve, ins)
                    ins.then_inc(conv_ready, 1)
                dve.wait_ge(turned, 1)
                nc.vector.tensor_copy(cols[:, :, :, :], pc[:, :, :, :])
                c.vstep(dve, nc.vector.tensor_copy(decay[:, :, :], pd[:, :, :]))


def mlstm(c, qk_dram, v_dram, maxima, cols, decay, og_dram, yb_dram, mT, next_weights):
    nc, io = c.nc, c.io
    og_t, yb_t = og_dram.rearrange("(t p) d -> t p d", p=P), yb_dram.rearrange("(t p) d -> t p d", p=P)
    R = MD ** -0.5
    with ExitStack() as s:
        e = s.enter_context(nc.sbuf_tensor("ml_e", [P, MH, P], F32))
        se = s.enter_context(nc.sbuf_tensor("ml_se", [P, 2, MH, P], F32))
        nsb = s.enter_context(nc.sbuf_tensor("ml_num", [P, 2, MV], F32))
        st = s.enter_context(nc.sbuf_tensor("ml_state", [P, MH, 2, MV], F32))
        qk = s.enter_context(nc.sbuf_tensor("ml_qk", [P, 3, 2 * KC, P], F32))
        v = s.enter_context(nc.sbuf_tensor("ml_v", [P, 3, MH, MV], F32))
        hh = s.enter_context(nc.sbuf_tensor("ml_hh", [P, 2, D], F32))
        gain = s.enter_context(nc.sbuf_tensor("ml_gain", [P, D], F32))
        kn = s.enter_context(nc.sbuf_tensor("ml_kn", [P, D], F32))
        sq = s.enter_context(nc.sbuf_tensor("ml_sq", [P, MD], F32))
        den = s.enter_context(nc.sbuf_tensor("ml_den", [P, 2], F32))
        ss = s.enter_context(nc.sbuf_tensor("ml_ss", [P, 3, MH], F32))
        eps = s.enter_context(nc.sbuf_tensor("ml_eps", [P, 1], F32))
        og = s.enter_context(nc.sbuf_tensor("ml_og", [P, 2, D], F32))
        yb = s.enter_context(nc.sbuf_tensor("ml_yb", [P, 2, D], F32))
        p_a = s.enter_context(nc.psum_tensor("ml_p_a", [P, MH, P], F32))
        p_s = s.enter_context(nc.psum_tensor("ml_p_s", [P, MH, P], F32))
        p_n = s.enter_context(nc.psum_tensor("ml_p_n", [P, BANK], F32))
        p_i = s.enter_context(nc.psum_tensor("ml_p_i", [P, BANK], F32))
        p_t = s.enter_context(nc.psum_tensor("ml_p_t", [P, D], F32))
        p_c = s.enter_context(nc.psum_tensor("ml_p_c", [P, 2, BANK], F32))
        gain_in, tile_in = c.sem("ml_gain_in"), [c.sem("ml_tile_in0"), c.sem("ml_tile_in1")]
        start, chunk_in = c.sem("ml_start"), [c.sem(f"ml_chunk_in{b}") for b in range(3)]
        a_bc, s_done, k_turned = c.sem("ml_a_bc"), c.sem("ml_s_done"), c.sem("ml_k_turned")
        n_done, c_done, m_turned = c.sem("ml_n_done"), c.sem("ml_c_done"), c.sem("ml_m_turned")
        e_pre, e_exp, se_ready = c.sem("ml_e_pre"), c.sem("ml_e_exp"), c.sem("ml_se_ready")
        kn_ready, nsb_ready = c.sem("ml_kn_ready"), c.sem("ml_nsb_ready")
        t_ready, h_ready, c_ready = c.sem("ml_t_ready"), c.sem("ml_h_ready"), c.sem("ml_c_ready")
        rms_ready, m_ready, m_kept = c.sem("ml_rms"), c.sem("ml_m_ready"), c.sem("ml_m_kept")
        with nc.Block() as block:
            @block.sync
            def _(sp):
                sp.dma_start(gain[:, :], io["mh_norm_g_2"].partition_broadcast(P)).then_inc(gain_in, 16)
                for t in range(NT):
                    if t >= 3:
                        sp.wait_ge(c_done, MH * (t - 2))
                    sp.dma_start(qk[:, t % 3, :, :], qk_dram[:, :, t * P:(t + 1) * P].rearrange("j p n -> p j n")
                                 ).then_inc(chunk_in[t % 3], 16)
                    sp.dma_start(v[:, t % 3, :, 0:MD], v_dram[t * P:(t + 1) * P, :].rearrange("p (h d) -> p h d", h=MH)
                                 ).then_inc(chunk_in[t % 3], 16)
                    if t == 2:
                        next_weights.load(sp, 0, 2)
                    if t >= 2:
                        sp.wait_ge(m_ready, t - 1)
                    sp.dma_start(og[:, t % 2, :], og_t[t]).then_inc(tile_in[t % 2], 16)
                    sp.dma_start(yb[:, t % 2, :], yb_t[t]).then_inc(tile_in[t % 2], 16)
                next_weights.load(sp, 2)

            @block.gpsimd
            def _(pool):
                next_weights.prepare(pool)

            @block.tensor
            def _(pe):
                def scores(t):
                    pe.wait_ge(e_pre, t)
                    for h in range(MH):
                        ins = pe.matmul(p_a[:, h, :], c.const("sel")[0:MH, h * P:(h + 1) * P],
                                        maxima[:, t * P:(t + 1) * P], start=True, stop=True)
                    ins.then_inc(a_bc, 1)
                    pe.wait_ge(se_ready, t)
                    pe.wait_ge(chunk_in[t % 3], 32 * (t // 3 + 1))
                    for h in range(MH):
                        for k in range(2):
                            ins = pe.matmul(p_s[:, h, :], qk[:, t % 3, KC + 2 * h + k, :], qk[:, t % 3, 2 * h + k, :],
                                            start=(k == 0), stop=(k == 1))
                    ins.then_inc(s_done, 1)

                def turn_keys(t):
                    if t >= 2:
                        pe.wait_ge(m_kept, t - 1)
                    for j in range(KC):
                        ins = pe.transpose(p_t[:, j * P:(j + 1) * P], qk[:, t % 3, KC + j, :], c.const("ident"))
                    ins.then_inc(k_turned, 1)

                def turn_mixed(t, keys):
                    pe.wait_ge(m_ready, t + 1)
                    pe.wait_ge(kn_ready, keys)
                    for j in range(KC):
                        ins = pe.transpose(p_t[:, j * P:(j + 1) * P], hh[:, t % 2, j * P:(j + 1) * P], c.const("ident"))
                    ins.then_inc(m_turned, 1)

                pe.wait_ge(start, 1)
                scores(0)
                turn_keys(0)
                for t in range(NT):
                    if t + 1 < NT:
                        scores(t + 1)
                    pe.wait_ge(se_ready, t + 1)
                    pe.wait_ge(kn_ready, t + 1)
                    for h in range(MH):
                        u = MH * t + h
                        pe.wait_ge(nsb_ready, u)
                        pe.wait_ge(t_ready, u)
                        pe.matmul(p_n[:, 0:MV], se[:, t % 2, h, :], v[:, t % 3, h, :], start=True, stop=True)
                        if t >= 1:
                            pe.wait_ge(c_ready, u - MH + 1)
                        for k in range(2):
                            ins = pe.matmul(p_i[:, 0:MV], qk[:, t % 3, 2 * h + k, :], st[:, h, k, :],
                                            start=(k == 0), stop=(k == 1))
                        ins.then_inc(n_done, 1)
                        pe.wait_ge(c_ready, u)
                        for k in range(2):
                            ins = pe.matmul(p_c[:, k, 0:MV], kn[:, (2 * h + k) * P:(2 * h + k + 1) * P], v[:, t % 3, h, :],
                                            start=True, stop=True)
                        ins.then_inc(c_done, 1)
                    if t >= 1:
                        turn_mixed(t - 1, t + 1)
                    if t + 1 < NT:
                        turn_keys(t + 1)
                pe.wait_ge(m_kept, NT - 1)
                turn_mixed(NT - 1, NT)

            @block.vector
            def _(dve):
                def gaps(t):
                    dve.wait_ge(a_bc, t + 1)
                    for h in range(MH):
                        ins = nc.vector.tensor_scalar(e[:, h, :], p_a[:, h, :], cols[:, t, 0, h:h + 1], 0.0,
                                                      ALU.subtract, ALU.max)
                    ins.then_inc(e_pre, 1)

                def weigh(t):
                    dve.wait_ge(e_exp, t + 1)
                    c.vstep(dve, nc.vector.scalar_tensor_tensor(
                        e[:, :, :], e[:, :, :], R, c.const("causal").unsqueeze(1).to_broadcast([P, MH, P]),
                        ALU.mult, ALU.mult))
                    dve.wait_ge(s_done, t + 1)
                    if t >= 2:
                        dve.wait_ge(n_done, MH * (t - 1))
                    nc.vector.tensor_tensor(se[:, t % 2, :, :], e[:, :, :], p_s[:, :, :], ALU.mult).then_inc(se_ready, 1)
                    dve.wait_ge(se_ready, t + 1)

                def head(t, h):
                    u = MH * t + h
                    dve.wait_ge(nsb_ready, u + 1)
                    n = nsb[:, u % 2, :]
                    nc.vector.scalar_tensor_tensor(n, p_i[:, 0:MV], cols[:, t, 1, h:h + 1], n, ALU.mult, ALU.add
                                                   ).then_inc(t_ready, 1)
                    dve.wait_ge(t_ready, u + 1)
                    c.vstep(dve, nc.vector.scalar_tensor_tensor(den[:, 0:1], n[:, MD:MV], -1.0, n[:, MD:MV],
                                                                ALU.mult, ALU.max))
                    c.vstep(dve, nc.vector.tensor_scalar(den[:, 0:1], den[:, 0:1], cols[:, t, 2, h:h + 1], None, ALU.max))
                    c.vstep(dve, nc.vector.reciprocal(den[:, 1:2], den[:, 0:1]))
                    if t >= 2 and h == 0:
                        dve.wait_ge(m_turned, t - 1)
                    nc.vector.tensor_scalar(hh[:, t % 2, h * MD:(h + 1) * MD], n[:, 0:MD], den[:, 1:2], None, ALU.mult
                                            ).then_inc(h_ready, 1)
                    dve.wait_ge(c_done, u + 1)
                    sh = st[:, h, :, :]
                    nc.vector.scalar_tensor_tensor(sh, sh, decay[:, h, t:t + 1], p_c[:, :, 0:MV], ALU.mult, ALU.add
                                                   ).then_inc(c_ready, 1)

                def mix(t):
                    m = hh[:, t % 2, :]
                    dve.wait_ge(rms_ready, t + 1)
                    c.vstep(dve, nc.vector.reciprocal(ss[:, 2, :], ss[:, 1, :]))
                    heads = m.rearrange("p (h d) -> p h d", h=MH)
                    c.vstep(dve, nc.vector.tensor_tensor(heads, heads, ss[:, 2, :].unsqueeze(2).to_broadcast([P, MH, MD]),
                                                         ALU.mult))
                    c.vstep(dve, nc.vector.tensor_tensor(m, m, gain[:, :], ALU.mult))
                    dve.wait_ge(tile_in[t % 2], 32 * (t // 2 + 1))
                    c.vstep(dve, nc.vector.tensor_tensor(m, m, og[:, t % 2, :], ALU.mult))
                    nc.vector.tensor_tensor(m, m, yb[:, t % 2, :], ALU.add).then_inc(m_ready, 1)

                nc.vector.memset(eps[:, :], EPS)
                nc.vector.memset(v[:, :, :, MD:MV], 1.0)
                nc.vector.memset(st[:, :, :, :], 0.0).then_inc(start, 1)
                dve.wait_ge(start, 1)
                dve.wait_ge(gain_in, 16)
                gaps(0)
                weigh(0)
                for t in range(NT):
                    if t + 1 < NT:
                        gaps(t + 1)
                    head(t, 0)
                    head(t, 1)
                    if t + 1 < NT:
                        weigh(t + 1)
                    head(t, 2)
                    head(t, 3)
                    mix(t)

            @block.scalar
            def _(act):
                def exps(t):
                    act.wait_ge(e_pre, t + 1)
                    nc.scalar.activation(e[:, :, :], e[:, :, :], ACT.Exp, scale=-1.0).then_inc(e_exp, 1)

                def keys(t):
                    act.wait_ge(k_turned, t + 1)
                    act.wait_ge(c_done, MH * t)
                    for h in range(MH):
                        c.astep(act, nc.scalar.activation(kn[:, h * MD:(h + 1) * MD], p_t[:, h * MD:(h + 1) * MD],
                                                          ACT.Copy, scale=cols[:, t, 3, h:h + 1]))
                    nc.scalar.activation(kn[:, :], kn[:, :], ACT.Copy, scale=R).then_inc(kn_ready, 1)

                def keep_mixed(t):
                    act.wait_ge(m_turned, t + 1)
                    nc.scalar.activation(mT[:, :, t * P:(t + 1) * P], p_t[:, :].rearrange("p (k n) -> p k n", k=KC),
                                         ACT.Copy).then_inc(m_kept, 1)

                act.wait_ge(start, 1)
                exps(0)
                keys(0)
                for t in range(NT):
                    if t + 1 < NT:
                        exps(t + 1)
                    for h in range(MH):
                        u = MH * t + h
                        act.wait_ge(n_done, u + 1)
                        if u >= 2:
                            act.wait_ge(h_ready, u - 1)
                        nc.scalar.activation(nsb[:, u % 2, :], p_n[:, 0:MV], ACT.Copy).then_inc(nsb_ready, 1)
                    for h in range(MH):
                        act.wait_ge(h_ready, MH * t + h + 1)
                        c.astep(act, nc.scalar.activation(sq[:, :], hh[:, t % 2, h * MD:(h + 1) * MD], ACT.Square,
                                                          accum_out=ss[:, 0, h:h + 1]))
                    act.wait_ge(m_ready, t)
                    nc.scalar.activation(ss[:, 1, :], ss[:, 0, :], ACT.Sqrt, scale=1.0 / MD, bias=eps[:, :]
                                         ).then_inc(rms_ready, 1)
                    if t >= 1:
                        keep_mixed(t - 1)
                    if t + 1 < NT:
                        keys(t + 1)
                keep_mixed(NT - 1)


def second_mixer(c, x1, x2, og, yb, qk_dram, v_dram):
    nc, io = c.nc, c.io
    with ExitStack() as s:
        maxima = s.enter_context(nc.sbuf_tensor("ml_maxima", [MH, S], F32))
        cols = s.enter_context(nc.sbuf_tensor("ml_cols", [P, NT, 4, MH], F32))
        decay = s.enter_context(nc.sbuf_tensor("ml_decays", [P, MH, NT], F32))
        with ExitStack() as s2:
            weights = mixer_weights(c, s2)
            hT = Split(nc, s2, "h2T", [P, KC, S])
            norm_transposed(c, "n2", x1, io["norm_mix_g_2"], hT, next_weights=weights)
            spatial_gate(c, weights, hT, yb)
            output_gate(c, weights, hT, og)
            project_qkv(c, weights, hT, qk_dram, v_dram, maxima, cols, decay)
        mT = s.enter_context(nc.sbuf_tensor("m2T", [P, KC, S], F32))
        weights = out_weights(c, s, "o2", io["w_out_2"])
        mlstm(c, qk_dram, v_dram, maxima, cols, decay, og, yb, mT, weights)
        project_out(c, "o2", weights, mT, x1, x2)


def memory_weights(c, stack):
    wq, wkv = c.io["w_xq_2"], c.io["w_xkv_2"]
    sources, groups = [], []
    for n in range(D // BANK):
        groups += [(len(sources), "cols", sub * P, NMEM, 0) for sub in range(BANK // P)]
        sources.append(([by_rows(wkv, n * BANK, (n + 1) * BANK)], BANK))
    for n in range(D // BANK):
        groups += [(len(sources), "rows", 0, BANK, t) for t in range(NMEM // P)]
        sources.append(([by_rows(wkv, D + n * BANK, D + (n + 1) * BANK)], BANK))
    for n in range(D // BANK):
        groups += [(len(sources), "cols", sub * P, BANK, half) for sub in range(BANK // P) for half in range(2)]
        sources.append(([by_rows(wq, n * BANK, (n + 1) * BANK)], BANK))
    return Weights(c, stack, "p3", sources, groups, side="right")


def memory_projections(c, weights, xT, mnT, qT, kT, v, y_slots=None):
    nc = c.nc
    keep = []
    for i, kind, a, wd, t in weights.groups:
        panel_of = i % 2
        if i < 2:
            keep.append((kT[:, 4 * panel_of + a // P, :], NMEM))
        elif i < 4:
            keep.append((v[:, t, panel_of * BANK:(panel_of + 1) * BANK], BANK))
        else:
            keep.append((qT[:, 4 * panel_of + a // P, t * BANK:(t + 1) * BANK], BANK))
    of_memory = 4
    NB = 4
    with ExitStack() as s:
        zero = s.enter_context(nc.sbuf_tensor("xp_zero", [P, D], F32))
        ps = s.enter_context(nc.psum_tensor("xp_ps", [P, NB, BANK], F32))
        done, freed = weights.done, weights.freed
        zero_ready, cleared = c.sem("xp_zero_ready"), c.sem("xp_cleared")
        with nc.Block() as block:
            @block.gpsimd
            def _(pool):
                weights.take_los(pool)
                nc.gpsimd.memset(zero[:, :], 0.0).then_inc(zero_ready, 1)
                pool.wait_ge(zero_ready, 1)
                if y_slots is not None:
                    for b in range(2 * S // P, NBLK):
                        pool.dma_start(y_slots[b * P:(b + 1) * P, :], zero[:, :]).then_inc(cleared, 16)
                    pool.wait_ge(cleared, 16 * NE)

            @block.sync
            def _(sp):
                weights.load(sp, 2)

            @block.tensor
            def _(pe):
                for g in matmul_groups(pe, weights, lambda i: mnT if i < of_memory else xT, ps, NB):
                    pass

            @block.scalar
            def _(act):
                weights.before(act, 0)
                for g, (dst, n) in enumerate(keep):
                    weights.before(act, g + 1)
                    act.wait_ge(done, g + 1)
                    nc.scalar.activation(dst, ps[:, g % NB, 0:n], ACT.Copy).then_inc(freed, 1)


def memory_attention(c, qT, kT, v, oT, next_weights):
    nc = c.nc
    steps = [(h, half, t) for h in range(4) for half in range(2) for t in range(4)]
    N, R = len(steps), MD ** -0.5
    with ExitStack() as s:
        pr = s.enter_context(nc.sbuf_tensor("xa_p", [P, 2, NMEM], F32))
        pT = s.enter_context(nc.sbuf_tensor("xa_pT", [P, 2, 2, BANK], F32))
        mx = s.enter_context(nc.sbuf_tensor("xa_max", [P, 4, N], F32))
        ps = s.enter_context(nc.psum_tensor("xa_ps", [P, 2, BANK], F32))
        pt = s.enter_context(nc.psum_tensor("xa_pt", [P, 2, BANK], F32))
        po = s.enter_context(nc.psum_tensor("xa_po", [P, 2, BANK], F32))
        scored, maxed, expd, normed = (c.sem(f"xa_{n}") for n in ("scored", "maxed", "expd", "normed"))
        turned, kept, summed, out_kept = (c.sem(f"xa_{n}") for n in ("turned", "kept", "summed", "out_kept"))
        with nc.Block() as block:
            @block.sync
            def _(sp):
                next_weights.load(sp)

            @block.gpsimd
            def _(pool):
                next_weights.prepare(pool)

            @block.tensor
            def _(pe):
                def scores(i):
                    h, half, t = steps[i]
                    if i >= 2:
                        pe.wait_ge(expd, i - 1)
                    at = (4 * half + t) * P
                    for k in range(2):
                        ins = pe.matmul(ps[:, i % 2, 0:NMEM], qT[:, 2 * h + k, at:at + P], kT[:, 2 * h + k, :],
                                        start=(k == 0), stop=(k == 1))
                    ins.then_inc(scored, 1)

                def turn(i):
                    pe.wait_ge(normed, i + 1)
                    if i >= 2:
                        pe.wait_ge(kept, i - 1)
                    for m in range(2):
                        ins = pe.transpose(pt[:, i % 2, m * P:(m + 1) * P], pr[:, i % 2, m * P:(m + 1) * P], c.const("ident"))
                    ins.then_inc(turned, 1)

                def values(q):
                    pe.wait_ge(kept, 4 * (q + 1))
                    h = q // 2
                    for e in range(2):
                        n = 2 * q + e
                        if n >= 2:
                            pe.wait_ge(out_kept, n - 1)
                        for m in range(2):
                            ins = pe.matmul(po[:, n % 2, :], v[:, m, (2 * h + e) * P:(2 * h + e + 1) * P],
                                            pT[:, q % 2, m, :], start=(m == 0), stop=(m == 1))
                        ins.then_inc(summed, 1)

                for i in range(N + 3):
                    if i < N:
                        scores(i)
                    if 1 <= i <= N:
                        turn(i - 1)
                    if i >= 6 and (i - 2) % 4 == 0:
                        values((i - 6) // 4)

            @block.vector
            def _(dve):
                for i in range(N + 1):
                    if i < N:
                        dve.wait_ge(scored, i + 1)
                        c.vstep(dve, nc.vector.tensor_reduce(mx[:, 0, i:i + 1], ps[:, i % 2, 0:NMEM], AX, ALU.max))
                        nc.vector.tensor_scalar(mx[:, 1, i:i + 1], mx[:, 0, i:i + 1], -R, None, ALU.mult
                                                ).then_inc(maxed, 1)
                    if i >= 1:
                        n = i - 1
                        dve.wait_ge(expd, n + 1)
                        c.vstep(dve, nc.vector.reciprocal(mx[:, 3, n:n + 1], mx[:, 2, n:n + 1]))
                        nc.vector.tensor_scalar(pr[:, n % 2, :], pr[:, n % 2, :], mx[:, 3, n:n + 1], None, ALU.mult
                                                ).then_inc(normed, 1)

            @block.scalar
            def _(act):
                def keep_out(n):
                    act.wait_ge(summed, n + 1)
                    q, e = divmod(n, 2)
                    h, half = divmod(q, 2)
                    nc.scalar.activation(oT[:, 2 * h + e, half * BANK:(half + 1) * BANK], po[:, n % 2, :], ACT.Copy
                                         ).then_inc(out_kept, 1)

                for i in range(N + 3):
                    if i < N:
                        act.wait_ge(maxed, i + 1)
                        if i >= 2:
                            act.wait_ge(turned, i - 1)
                        nc.scalar.activation(pr[:, i % 2, :], ps[:, i % 2, 0:NMEM], ACT.Exp, bias=mx[:, 1, i:i + 1],
                                             scale=R, accum_out=mx[:, 2, i:i + 1]).then_inc(expd, 1)
                    if 1 <= i <= N:
                        n = i - 1
                        q, t = divmod(n, 4)
                        act.wait_ge(turned, n + 1)
                        if q >= 2:
                            act.wait_ge(summed, 2 * (q - 1))
                        nc.scalar.activation(pT[:, q % 2, :, t * P:(t + 1) * P],
                                             pt[:, n % 2, 0:2 * P].rearrange("p (m n) -> p m n", m=2), ACT.Copy
                                             ).then_inc(kept, 1)
                    if i >= 6 and (i - 2) % 4 == 0:
                        keep_out((i - 6) // 4 * 2)
                        keep_out((i - 6) // 4 * 2 + 1)


def cross_attention(c, x2, x3, y_slots=None):
    nc, io = c.nc, c.io
    with ExitStack() as s:
        with ExitStack() as s2:
            weights = memory_weights(c, s2)
            hT = Split(nc, s2, "h3T", [P, KC, S], side="right")
            mnT = Split(nc, s2, "mnT", [P, KC, NMEM], side="right")
            norm_transposed(c, "nm", io["mem_2"], io["norm_mem_g_2"], mnT, n_tiles=NMEM // P)
            norm_transposed(c, "n3", x2, io["norm_x_g_2"], hT, next_weights=weights)
            qT = s.enter_context(nc.sbuf_tensor("q3T", [P, KC, S], F32))
            kT = s.enter_context(nc.sbuf_tensor("k3T", [P, KC, NMEM], F32))
            v = s.enter_context(nc.sbuf_tensor("v3", [P, NMEM // P, D], F32))
            memory_projections(c, weights, hT, mnT, qT, kT, v, y_slots)
        weights = out_weights(c, s, "o3", io["w_xo_2"])
        oT = qT
        memory_attention(c, qT, kT, v, oT, weights)
        project_out(c, "o3", weights, oT, x2, x3)


def route(c, hT, gates, dest, slot_token, block_expert, n_blocks):
    nc, io = c.nc, c.io
    NR = NG + NE
    with ExitStack() as s:
        def sb(name, shape, dt=F32):
            return s.enter_context(nc.sbuf_tensor(f"rt_{name}", shape, dt))

        wr, bias, lg = sb("w", [P, KC, NR]), sb("bias", [P, NR]), sb("logits", [P, NT, NR])
        el, e4, e32 = sb("el", [P, NT, NE]), sb("e4", [P, NT, NG]), sb("e32", [P, NT, NE])
        oh1, oh2, oh = sb("oh1", [P, NT, NE]), sb("oh2", [P, NT, NE]), sb("oh", [P, NT, NE])
        gm, pg, idx = sb("gmax", [P, NT]), sb("pgroup", [P, NT]), sb("idx", [P, NT])
        v1, v2, r = sb("v1", [P, NT]), sb("v2", [P, NT]), sb("r", [P, NT])
        cnt_i, padded, pend, start = sb("cnt_i", [P, NE], I32), sb("padded", [P, NE]), sb("pend", [P, NE]), sb("start", [P, NE])
        cmp = sb("cmp", [P, NBLK, NE])
        be, nb = sb("be", [P, NBLK]), sb("nb", [P, 1])
        dest_f, lo_i, lo, hi = sb("dest_f", [P, 2, NT]), sb("lo_i", [P, 2, NT], I32), sb("lo", [P, 2, NT]), sb("hi", [P, 2, NT])
        d1, d2 = sb("d1", [P, 2 * NT, P]), sb("d2", [P, 2 * NT, NBLK])
        pl = s.enter_context(nc.psum_tensor("rt_pl", [P, NT, 64], F32))
        pk = s.enter_context(nc.psum_tensor("rt_pk", [P, NT, 64], F32))
        pn = s.enter_context(nc.psum_tensor("rt_pn", [P, BANK], F32))
        pt = s.enter_context(nc.psum_tensor("rt_pt", [P, BANK], F32))
        w_in, scored = c.sem("rt_w_in"), c.sem("rt_scored")
        pre, expd, chosen = c.sem("rt_pre"), c.sem("rt_expd"), c.sem("rt_chosen")
        ranked, placed, tabled = c.sem("rt_ranked"), c.sem("rt_placed"), c.sem("rt_tabled")
        iota32 = c.const("iota32").rearrange("p (t e) -> p t e", t=NT)
        iota4 = iota32[:, :, 0:NG]

        def bc(x, n):
            return x.unsqueeze(2).to_broadcast([P, NT, n])

        with nc.Block() as block:
            @block.sync
            def _(sp):
                with nc.allow_non_contiguous_dma(reason="36 columns, once"):
                    sp.dma_start(wr[:, :, 0:NG], by_rows(io["w_rg_2"], 0, NG)).then_inc(w_in, 16)
                    sp.dma_start(wr[:, :, NG:], by_rows(io["w_re_2"], 0, NE)).then_inc(w_in, 16)
                sp.dma_start(bias[:, 0:NG], io["b_rg_2"].partition_broadcast(P)).then_inc(w_in, 16)
                sp.dma_start(bias[:, NG:], io["b_re_2"].partition_broadcast(P)).then_inc(w_in, 16)

            @block.tensor
            def _(pe):
                pe.wait_ge(w_in, 64)
                for t in range(NT):
                    for k in range(KC):
                        ins = pe.matmul(pl[:, t, 0:NR], hT[:, k, t * P:(t + 1) * P], wr[:, k, :],
                                        start=(k == 0), stop=(k == KC - 1))
                ins.then_inc(scored, 1)
                pe.wait_ge(chosen, 1)
                for t in range(NT):
                    for j in range(t):
                        pe.matmul(pk[:, t, 0:NE], c.const("ones"), oh[:, j, :], start=(j == 0), stop=False)
                    pe.matmul(pk[:, t, 0:NE], c.const("before"), oh[:, t, :], start=(t == 0), stop=True)
                for j in range(NT):
                    ins = pe.matmul(pn[:, 0:NE], c.const("ones"), oh[:, j, :], start=(j == 0), stop=(j == NT - 1))
                ins.then_inc(ranked, 1)
                pe.wait_ge(placed, 1)
                for n in range(2 * NT):
                    ins = pe.matmul(pt[:, 0:NBLK], d1[:, n, :], d2[:, n, :], start=(n == 0), stop=(n == 2 * NT - 1))
                ins.then_inc(tabled, 1)

            @block.scalar
            def _(act):
                act.wait_ge(pre, 1)
                nc.scalar.activation(e4[:, :, :], e4[:, :, :], ACT.Exp).then_inc(expd, 1)
                act.wait_ge(pre, 2)
                nc.scalar.activation(v2[:, :], v2[:, :], ACT.Exp).then_inc(expd, 1)

            @block.vector
            def _(dve):
                V = nc.vector

                def step(ins):
                    c.vstep(dve, ins)

                def first_of_max(values, n, top, onehot, iota, spare):
                    step(V.tensor_reduce(top[:, :], values, AX, ALU.max))
                    step(V.tensor_tensor(spare, values, bc(top[:, :], n), ALU.is_equal))
                    step(V.scalar_tensor_tensor(spare, spare, -64.0, iota, ALU.mult, ALU.add))
                    step(V.tensor_reduce(idx[:, :], spare, AX, ALU.min))
                    step(V.tensor_scalar(idx[:, :], idx[:, :], 64.0, None, ALU.add))
                    step(V.tensor_tensor(onehot, iota, bc(idx[:, :], n), ALU.is_equal))

                dve.wait_ge(scored, 1)
                step(V.tensor_tensor(lg[:, :, :], pl[:, :, 0:NR], bias[:, :].unsqueeze(1).to_broadcast([P, NT, NR]), ALU.add))
                first_of_max(lg[:, :, 0:NG], NG, gm, oh1[:, :, 0:NG], iota4, e32[:, :, 0:NG])
                V.tensor_tensor(e4[:, :, :], lg[:, :, 0:NG], bc(gm[:, :], NG), ALU.subtract).then_inc(pre, 1)
                step(V.tensor_scalar(oh1[:, :, 0:NG], oh1[:, :, 0:NG], -NEG, NEG, ALU.mult, ALU.add))
                for g in range(NG):
                    ins = V.tensor_tensor(el[:, :, g * EPG:(g + 1) * EPG], lg[:, :, NG + g * EPG:NG + (g + 1) * EPG],
                                          oh1[:, :, g:g + 1].to_broadcast([P, NT, EPG]), ALU.add)
                step(ins)
                first_of_max(el[:, :, :], NE, v1, oh1[:, :, :], iota32, e32[:, :, :])
                step(V.scalar_tensor_tensor(el[:, :, :], oh1[:, :, :], 3 * NEG, el[:, :, :], ALU.mult, ALU.add))
                first_of_max(el[:, :, :], NE, v2, oh2[:, :, :], iota32, e32[:, :, :])
                V.tensor_tensor(oh[:, :, :], oh1[:, :, :], oh2[:, :, :], ALU.add).then_inc(chosen, 1)
                V.tensor_tensor(v2[:, :], v2[:, :], v1[:, :], ALU.subtract).then_inc(pre, 1)
                dve.wait_ge(expd, 1)
                step(V.tensor_reduce(pg[:, :], e4[:, :, :], AX, ALU.add))
                step(V.reciprocal(pg[:, :], pg[:, :]))
                dve.wait_ge(expd, 2)
                step(V.tensor_scalar(r[:, :], v2[:, :], 1.0, None, ALU.add))
                step(V.reciprocal(r[:, :], r[:, :]))
                step(V.tensor_tensor(gates[:, 0, :], pg[:, :], r[:, :], ALU.mult))
                step(V.tensor_tensor(gates[:, 1, :], gates[:, 0, :], v2[:, :], ALU.mult))
                dve.wait_ge(ranked, 1)
                step(V.tensor_scalar(cnt_i[:, :], pn[:, 0:NE], float(P - 1), None, ALU.add))
                step(V.tensor_scalar(cnt_i[:, :], cnt_i[:, :], 7, 7, ALU.arith_shift_right, ALU.logical_shift_left))
                step(V.tensor_copy(padded[:, :], cnt_i[:, :]))
                step(V.tensor_tensor_scan(pend[:, :], c.const("ones")[:, 0:NE], padded[:, :], 0.0, ALU.mult, ALU.add))
                step(V.tensor_tensor(start[:, :], pend[:, :], padded[:, :], ALU.subtract))
                step(V.tensor_tensor(el[:, :, :], pk[:, :, 0:NE], start[:, :].unsqueeze(1).to_broadcast([P, NT, NE]), ALU.add))
                for k, o in enumerate((oh1, oh2)):
                    step(V.tensor_tensor(e32[:, :, :], o[:, :, :], el[:, :, :], ALU.mult))
                    step(V.tensor_reduce(dest_f[:, k, :], e32[:, :, :], AX, ALU.add))
                step(V.tensor_copy(dest[:, :, :], dest_f[:, :, :]))
                step(V.tensor_copy(lo_i[:, :, :], dest_f[:, :, :]))
                step(V.tensor_scalar(lo_i[:, :, :], lo_i[:, :, :], P - 1, None, ALU.bitwise_and))
                step(V.tensor_copy(lo[:, :, :], lo_i[:, :, :]))
                step(V.tensor_tensor(hi[:, :, :], dest_f[:, :, :], lo[:, :, :], ALU.subtract))
                for n in range(2 * NT):
                    k, t = divmod(n, NT)
                    V.tensor_scalar(d1[:, n, :], c.const("iota"), lo[:, k, t:t + 1], None, ALU.is_equal)
                    ins = V.tensor_scalar(d2[:, n, :], c.const("blk"), hi[:, k, t:t + 1], c.const("tokid")[:, t:t + 1],
                                          ALU.is_equal, ALU.mult)
                ins.then_inc(placed, 1)
                step(V.tensor_tensor(cmp[:, :, :], pend[:, :].unsqueeze(1).to_broadcast([P, NBLK, NE]),
                                     c.const("blk").unsqueeze(2).to_broadcast([P, NBLK, NE]), ALU.is_le))
                step(V.tensor_reduce(be[:, :], cmp[:, :, :], AX, ALU.add))
                step(V.tensor_scalar(block_expert[:, :], be[:, :], float(NE - 1), None, ALU.min))
                step(V.tensor_scalar(nb[:, :], pend[:, NE - 1:NE], 1.0 / P, None, ALU.mult))
                V.tensor_copy(n_blocks[:, 0:1], nb[:, :])
                step(V.tensor_scalar(n_blocks[:, 1:2], nb[:, :], -1.0, None, ALU.add))
                step(V.tensor_scalar(n_blocks[:, 2:3], n_blocks[:, 1:2], 1, None, ALU.bitwise_and))
                step(V.tensor_scalar(n_blocks[:, 1:2], n_blocks[:, 1:2], 1, None, ALU.arith_shift_right))
                dve.wait_ge(tabled, 1)
                V.memset(slot_token[:, NBLK:], 0)
                step(V.tensor_copy(slot_token[:, 0:NBLK], pt[:, 0:NBLK]))


def experts(c, xn, y_slots, slot_token, block_expert, n_blocks):
    nc, io = c.nc, c.io
    KF = FF // P
    w1 = io["w1_2"].rearrange("e (p k) f -> e p (k f)", k=KC)
    w3 = io["w3_2"].rearrange("e (p k) f -> e p (k f)", k=KC)
    w2 = io["w2_2"].rearrange("e (p k) d -> e p (k d)", k=KF)
    y_b = y_slots.rearrange("(b p) d -> b p d", p=P)
    with ExitStack() as s:
        def sb(name, shape, dt=F32):
            return s.enter_context(nc.sbuf_tensor(f"ex_{name}", shape, dt))

        w1s, w3s, w2s = sb("w1", [P, 2, KC * FF]), sb("w3", [P, 2, KC * FF]), sb("w2", [P, 2, KF * D])
        idx, xg, xT = sb("idx", [P, 2], I32), sb("x", [P, 2, D]), sb("xT", [P, 2, D])
        a, h, hT, y = sb("a", [P, 2, FF]), sb("h", [P, 2, FF]), sb("hT", [P, 2, FF]), sb("y", [P, 2, D])
        p_x = s.enter_context(nc.psum_tensor("ex_px", [P, D], F32))
        p_a = s.enter_context(nc.psum_tensor("ex_pa", [P, FF], F32))
        p_b = s.enter_context(nc.psum_tensor("ex_pb", [P, FF], F32))
        p_h = s.enter_context(nc.psum_tensor("ex_ph", [P, FF], F32))
        p_y = s.enter_context(nc.psum_tensor("ex_py", [P, D], F32))

        def pair(name):
            return [c.sem(f"ex_{name}{j}") for j in range(2)]

        w1_in, w3_in, w2_in = pair("w1_in"), pair("w3_in"), pair("w2_in")
        idx_ready, x_in, x_turned, x_kept = pair("idx"), pair("x_in"), pair("x_turned"), pair("x_kept")
        a_done, b_done, a_ready, h_ready = pair("a_done"), pair("b_done"), pair("a_ready"), pair("h_ready")
        h_turned, h_kept, y_done, y_ready, y_out = (pair("h_turned"), pair("h_kept"), pair("y_done"), pair("y_ready"),
                                                    pair("y_out"))
        gathers = c.sem("ex_gathers")
        stored = c.sem("ex_stored")

        def wait(eng, sem, value):
            if not isinstance(value, int) or value > 0:
                eng.wait_ge(sem, value)

        def last(i, j):
            return (i - 1, 1) if j == 0 else (i, 0)

        def next_(i, j):
            return (i, 1) if j == 0 else (i + 1, 0)

        def upto_last(i, j):
            return i if j == 0 else i + 1

        def over_blocks(eng, body, tail=None):
            n = eng.value_load(n_blocks[0:1, 0:1], min_val=2 * S // P, max_val=NBLK)
            for j in range(2):
                body(0, j)
            with eng.Fori(1, NBLK // 2) as i:
                for j in range(2):
                    with eng.If(2 * i + j < n):
                        body(i, j)
            if tail:
                end = eng.value_load(n_blocks[0:1, 1:2], min_val=S // P - 1, max_val=NBLK // 2 - 1)
                odd = eng.value_load(n_blocks[0:1, 2:3], min_val=0, max_val=1)
                for j in range(2):
                    with eng.If(odd == j):
                        tail(end, j)
            return n

        with nc.Block() as block:
            @block.sync
            def _(sp):
                def load(i, j):
                    b = 2 * i + j
                    at = slice(b, b + 1) if isinstance(b, int) else bass.ds(b, 1)
                    e = sp.value_load(block_expert[0:1, at], min_val=0, max_val=NE - 1)
                    wait(sp, a_done[j], i)
                    sp.dma_start(w1s[:, j, :], w1[bass.ds(e, 1)].rearrange("e p n -> (e p) n")).then_inc(w1_in[j], 16)
                    wait(sp, b_done[j], i)
                    sp.dma_start(w3s[:, j, :], w3[bass.ds(e, 1)].rearrange("e p n -> (e p) n")).then_inc(w3_in[j], 16)
                    wait(sp, y_done[j], i)
                    sp.dma_start(w2s[:, j, :], w2[bass.ds(e, 1)].rearrange("e p n -> (e p) n")).then_inc(w2_in[j], 16)

                over_blocks(sp, load)

            @block.gpsimd
            def _(pool):
                def gather(i, j):
                    b = 2 * i + j
                    at = slice(b, b + 1) if isinstance(b, int) else bass.ds(b, 1)
                    wait(pool, x_turned[j], i)
                    nc.gpsimd.tensor_copy(idx[:, j:j + 1], slot_token[:, at]).then_inc(idx_ready[j], 1)
                    pool.wait_ge(idx_ready[j], i + 1)
                    pool.sem_inc(gathers, 1)
                    nc.gpsimd.indirect_dma_start(xg[:, j, :], None, xn,
                                                 bass.IndirectOffsetOnAxis(idx[:, j:j + 1].bitcast(U32), 0)
                                                 ).then_inc(x_in[j], 16)

                gather(0, 0)
                over_blocks(pool, lambda i, j: gather(*next_(i, j)))

            @block.tensor
            def _(pe):
                def turn_x(i, j):
                    pe.wait_ge(x_in[j], 16 * i + 16)
                    wait(pe, x_kept[1 - j], upto_last(i, j))
                    for k in range(KC):
                        ins = pe.transpose(p_x[:, k * P:(k + 1) * P], xg[:, j, k::KC], c.const("ident"))
                    ins.then_inc(x_turned[j], 1)

                def up(i, j, ps, w, w_in, freed, done):
                    pe.wait_ge(w_in[j], 16 * i + 16)
                    wait(pe, freed[1 - j], upto_last(i, j))
                    for k in range(KC):
                        ins = pe.matmul(ps[:, :], xT[:, j, k * P:(k + 1) * P], w[:, j, k * FF:(k + 1) * FF],
                                        start=(k == 0), stop=(k == KC - 1))
                    ins.then_inc(done[j], 1)

                def turn_h(i, j):
                    pe.wait_ge(h_ready[j], i + 1)
                    wait(pe, h_kept[1 - j], upto_last(i, j))
                    for k in range(KF):
                        ins = pe.transpose(p_h[:, k * P:(k + 1) * P], h[:, j, k::KF], c.const("ident"))
                    ins.then_inc(h_turned[j], 1)

                def down(i, j):
                    pe.wait_ge(h_kept[j], i + 1)
                    pe.wait_ge(w2_in[j], 16 * i + 16)
                    wait(pe, y_ready[1 - j], upto_last(i, j))
                    for n in range(2):
                        for k in range(KF):
                            ins = pe.matmul(p_y[:, n * BANK:(n + 1) * BANK], hT[:, j, k * P:(k + 1) * P],
                                            w2s[:, j, k * D + n * BANK:k * D + (n + 1) * BANK],
                                            start=(k == 0), stop=(k == KF - 1))
                    ins.then_inc(y_done[j], 1)

                def body(i, j):
                    first = isinstance(i, int) and i == 0 and j == 0
                    pe.wait_ge(x_kept[j], i + 1)
                    up(i, j, p_a, w1s, w1_in, a_ready, a_done)
                    if not first:
                        turn_h(*last(i, j))
                    up(i, j, p_b, w3s, w3_in, h_ready, b_done)
                    turn_x(*next_(i, j))
                    if not first:
                        down(*last(i, j))

                def tail(i, j):
                    turn_h(i, j)
                    down(i, j)

                turn_x(0, 0)
                over_blocks(pe, body, tail)

            @block.scalar
            def _(act):
                def silu(i, j):
                    act.wait_ge(a_done[j], i + 1)
                    wait(act, h_ready[j], i)
                    nc.scalar.activation(a[:, j, :], p_a[:, :], ACT.Silu).then_inc(a_ready[j], 1)

                def store(i, j):
                    b = 2 * i + j
                    at = slice(b, b + 1) if isinstance(b, int) else bass.ds(b, 1)
                    act.wait_ge(y_done[j], i + 1)
                    wait(act, y_out[j], 16 * i)
                    nc.scalar.activation(y[:, j, :], p_y[:, :], ACT.Copy).then_inc(y_ready[j], 1)
                    act.wait_ge(y_ready[j], i + 1)
                    act.dma_start(y_b[at].rearrange("e p n -> (e p) n"), y[:, j, :]).then_inc(y_out[j], 16)

                def body(i, j):
                    silu(i, j)
                    if not (isinstance(i, int) and i == 0 and j == 0):
                        store(*last(i, j))

                n = over_blocks(act, body, store)
                act.wait_ge(y_out[0], ((n + 1) >> 1) * 16)
                act.wait_ge(y_out[1], (n >> 1) * 16)
                act.sem_inc(stored, 1)

            @block.vector
            def _(dve):
                def keep_x(i, j):
                    dve.wait_ge(x_turned[j], i + 1)
                    wait(dve, b_done[j], i)
                    nc.vector.tensor_copy(xT[:, j, :], p_x[:, :]).then_inc(x_kept[j], 1)

                def keep_h(i, j):
                    dve.wait_ge(h_turned[j], i + 1)
                    wait(dve, y_done[j], i)
                    nc.vector.tensor_copy(hT[:, j, :], p_h[:, :]).then_inc(h_kept[j], 1)

                def body(i, j):
                    if not (isinstance(i, int) and i == 0 and j == 0):
                        keep_h(*last(i, j))
                    dve.wait_ge(b_done[j], i + 1)
                    dve.wait_ge(a_ready[j], i + 1)
                    wait(dve, h_turned[j], i)
                    nc.vector.tensor_tensor(h[:, j, :], a[:, j, :], p_b[:, :], ALU.mult).then_inc(h_ready[j], 1)
                    keep_x(*next_(i, j))

                keep_x(0, 0)
                over_blocks(dve, body, keep_h)


def combine(c, x3, y_slots, dest, gates, out):
    nc, io = c.nc, c.io
    x_t, out_t = x3.rearrange("(t p) d -> t p d", p=P), out.rearrange("(t p) d -> t p d", p=P)
    with ExitStack() as s:
        def sb(name, shape, dt=F32):
            return s.enter_context(nc.sbuf_tensor(f"cb_{name}", shape, dt))

        x, y = sb("x", [P, 4, D]), sb("y", [P, 4, 2, D])
        sq, gain, ss, eps = sb("sq", [P, D]), sb("gain", [P, D]), sb("ss", [P, 3, NT]), sb("eps", [P, 1])
        gain_in, eps_ready, added, rms_ready, ready = (c.sem(f"cb_{n}") for n in ("gain_in", "eps", "added", "rms", "ready"))
        x_in, y_in, out_done = ([c.sem(f"cb_{n}{b}") for b in range(4)] for n in ("x_in", "y_in", "out"))
        with nc.Block() as block:
            @block.sync
            def _(sp):
                sp.dma_start(gain[:, :], io["norm_f_g_2"].partition_broadcast(P)).then_inc(gain_in, 16)
                for t in range(NT + 1):
                    if t < NT:
                        if t >= 4:
                            sp.wait_ge(out_done[t % 4], 16)
                        sp.dma_start(x[:, t % 4, :], x_t[t]).then_inc(x_in[t % 4], 16)
                    if t >= 1:
                        sp.wait_ge(ready, t)
                        sp.dma_start(out_t[t - 1], x[:, (t - 1) % 4, :]).then_inc(out_done[(t - 1) % 4], 16)
                for b in range(4):
                    sp.wait_ge(out_done[b], 32)

            @block.gpsimd
            def _(pool):
                for t in range(NT):
                    if t >= 4:
                        pool.wait_ge(added, t - 3)
                    for k in range(2):
                        nc.gpsimd.indirect_dma_start(y[:, t % 4, k, :], None, y_slots,
                                                     bass.IndirectOffsetOnAxis(dest[:, k, t:t + 1].bitcast(U32), 0)
                                                     ).then_inc(y_in[t % 4], 16)

            @block.scalar
            def _(act):
                act.wait_ge(eps_ready, 1)
                for t in range(NT):
                    act.wait_ge(added, t + 1)
                    c.astep(act, nc.scalar.activation(sq[:, :], x[:, t % 4, :], ACT.Square, accum_out=ss[:, 0, t:t + 1]))
                    nc.scalar.activation(ss[:, 1, t:t + 1], ss[:, 0, t:t + 1], ACT.Sqrt, scale=1.0 / D, bias=eps[:, :]
                                         ).then_inc(rms_ready, 1)

            @block.vector
            def _(dve):
                nc.vector.memset(eps[:, :], EPS).then_inc(eps_ready, 1)
                dve.wait_ge(gain_in, 16)
                for t in range(NT):
                    xx = x[:, t % 4, :]
                    dve.wait_ge(x_in[t % 4], 16 * (t // 4 + 1))
                    dve.wait_ge(y_in[t % 4], 32 * (t // 4 + 1))
                    c.vstep(dve, nc.vector.scalar_tensor_tensor(xx, y[:, t % 4, 0, :], gates[:, 0, t:t + 1], xx,
                                                                ALU.mult, ALU.add))
                    nc.vector.scalar_tensor_tensor(xx, y[:, t % 4, 1, :], gates[:, 1, t:t + 1], xx, ALU.mult, ALU.add
                                                   ).then_inc(added, 1)
                    dve.wait_ge(rms_ready, t + 1)
                    c.vstep(dve, nc.vector.reciprocal(ss[:, 2, t:t + 1], ss[:, 1, t:t + 1]))
                    nc.vector.scalar_tensor_tensor(xx, xx, ss[:, 2, t:t + 1], gain[:, :], ALU.mult, ALU.mult
                                                   ).then_inc(ready, 1)


def mixture(c, x3, xn, y_slots, out):
    nc, io = c.nc, c.io
    with ExitStack() as s:
        gates = s.enter_context(nc.sbuf_tensor("gates", [P, 2, NT], F32))
        dest = s.enter_context(nc.sbuf_tensor("dest", [P, 2, NT], I32))
        slot_token = s.enter_context(nc.sbuf_tensor("slot_token", [P, NBLK + 1], I32))
        block_expert = s.enter_context(nc.sbuf_tensor("block_expert", [P, NBLK], I32))
        n_blocks = s.enter_context(nc.sbuf_tensor("n_blocks", [P, 3], I32))
        with ExitStack() as s2:
            hT = s2.enter_context(nc.sbuf_tensor("h4T", [P, KC, S], F32))
            norm_transposed(c, "n4", x3, io["norm_moe_g_2"], None, plain=hT, keep=xn, gain_row=io["norm_moe_g_2"])
            route(c, hT, gates, dest, slot_token, block_expert, n_blocks)
        experts(c, xn, y_slots, slot_token, block_expert, n_blocks)
        combine(c, x3, y_slots, dest, gates, out)


INS = ["x", "norm_pre_g", "w_in", "conv_w", "w_out", "norm_post_g", "mem_2", "norm_mix_g_2", "w_in_2", "b_gate_2",
       "b_if_2", "conv_w_2", "conv_b_2", "mh_norm_g_2", "sgu_norm_g_2", "b_s_2", "w_out_2", "norm_x_g_2",
       "norm_mem_g_2", "w_xq_2", "w_xkv_2", "w_xo_2", "norm_moe_g_2", "w_rg_2", "b_rg_2", "w_re_2", "b_re_2", "w1_2",
       "w3_2", "w2_2", "norm_f_g_2"]
WHOLE = {"norm_pre_g", "w_in", "conv_w", "w_out", "norm_post_g", "norm_f_g_2"}


def build(nc, io):
    def scratch(name, rows):
        return nc.dram_tensor(name, (rows, D), F32, kind="Internal").ap()

    x1, x2, x3, xn = (scratch(f"{n}_rows", S) for n in ("x1", "x2", "x3", "xn"))
    og, yb, y_slots = scratch("og_rows", S), scratch("yb_rows", S), scratch("y_slots", NBLK * P)
    qk1, v1 = (nc.dram_tensor(n, shape, F32, kind="Internal").ap()
               for n, shape in (("qk1_columns", (2 * AW // P, P, S)), ("v1_rows", (S, AW))))
    qk2, v2 = (nc.dram_tensor(n, shape, F32, kind="Internal").ap()
               for n, shape in (("qk2_columns", (2 * D // P, P, S)), ("v2_rows", (S, D))))
    with ExitStack() as ctx:
        c = Core(nc, io, ctx)
        load_constants(c)
        first_block(c, io["x"], x1, qk1, v1)
        c.retire_semaphores()
        second_mixer(c, x1, x2, og, yb, qk2, v2)
        c.retire_semaphores()
        cross_attention(c, x2, x3, y_slots)
        c.retire_semaphores()
        mixture(c, x3, xn, y_slots, io["out"])


def kernel(**inputs):
    import concourse.bacc as bacc
    from concourse.bass_utils import run_bass_kernel_spmd as run

    nc = bacc.Bacc("TRN2", target_bir_lowering=False, num_devices=1)
    arrays = {}
    for name in INS:
        a = np.asarray(inputs[name])
        arrays[name] = np.ascontiguousarray(a if name in WHOLE else a[0])
    arrays["w_s_T"] = np.ascontiguousarray(np.asarray(inputs["w_s_2"])[0].transpose(0, 2, 1))
    arrays["consts"] = shape_constants()
    io = {n: nc.dram_tensor(n, a.shape, mybir.dt.from_np(a.dtype), kind="ExternalInput").ap() for n, a in arrays.items()}
    io["out"] = nc.dram_tensor("out", (S, D), F32, kind="ExternalOutput").ap()
    build(nc, io)
    r = run(nc, [arrays], core_ids=[0])
    return r.results[0]["out"].reshape(1, S, D)
```

```python
from contextlib import ExitStack

import numpy as np

import concourse.bass as bass
from concourse import mybir

F32 = mybir.dt.float32
F32R = mybir.dt.float32r
I32 = mybir.dt.int32
U32 = mybir.dt.uint32
ALU = mybir.AluOpType
ACT = mybir.ActivationFunctionType
AX = mybir.AxisListType.X

P = 128
D = 1024
S = 1024
KC = D // P
NT = S // P
BANK = 512
EPS = 1e-6
NEG = -1e30

HD = 64
AW = 768
NH = AW // HD
CW = 256
SCALE = HD ** -0.5
MH, MD, MV = 4, 256, 257
NMEM = 256
NE, NG, EPG, FF = 32, 4, 8, 512
NBLK = 2 * S // P + NE

CONST_COLS = dict(ident=P, ones=P, causal=P, before=P, iota=P, tokid=NT, blk=NBLK, sel=MH * P, iota32=NT * NE,
                  cos=NT * 32, sin=NT * 32, logc=S)
CONST_AT = {}
_at = 0
for _n, _w in CONST_COLS.items():
    CONST_AT[_n] = _at
    _at += _w
CONST_W = _at


def shape_constants():
    c = {n: np.zeros((P, w), np.float32) for n, w in CONST_COLS.items()}
    p = np.arange(P)
    c["ident"][p, p] = 1
    c["ones"][:] = 1
    c["causal"][:] = p[:, None] <= p[None, :]
    c["before"][:] = p[:, None] < p[None, :]
    c["iota"][:] = p[None, :]
    c["tokid"][:] = p[:, None] + P * np.arange(NT)[None, :]
    c["blk"][:] = P * np.arange(NBLK)[None, :]
    for h in range(MH):
        c["sel"][h, h * P:(h + 1) * P] = 1
    c["iota32"][:] = np.tile(np.arange(NE), NT)[None, :]
    inv = np.float32(10000.0) ** (-np.arange(32, dtype=np.float32) * np.float32(2.0) / np.float32(64))
    ang = np.arange(S, dtype=np.float32)[:, None] * inv[None, :].astype(np.float32)
    c["cos"][:] = np.cos(ang).reshape(NT, P, 32).transpose(1, 0, 2).reshape(P, -1)
    c["sin"][:] = np.sin(ang).reshape(NT, P, 32).transpose(1, 0, 2).reshape(P, -1)
    d = p[:, None] + (S - P) - np.arange(S)[None, :]
    n = sum(((d >= 0) & (d <= w) & (d % r == 0)).astype(np.float32) for w, r in ((128, 1), (512, 4), (2048, 16)))
    c["logc"][:] = np.where(n > 0, np.log(np.maximum(n, 1)) / np.float32(SCALE), NEG)
    return np.ascontiguousarray(np.concatenate([c[n] for n in CONST_COLS], axis=1).astype(np.float32))


class Tally:

    def __init__(self, nc, ctx, name):
        self.sem, self.n = ctx.enter_context(nc.semaphore(name)), 0

    def inc(self, ins, by=1):
        ins.then_inc(self.sem, by)
        self.n += by
        return self.n


class Core:

    def __init__(self, nc, io, ctx):
        self.nc, self.io, self.ctx, self.in_use = nc, io, ctx, []
        self.small = ctx.enter_context(nc.sbuf_tensor("const_small", [P, CONST_AT["cos"]], F32))
        self.const_in = ctx.enter_context(nc.semaphore("const_in"))
        self.dve_chain = Tally(nc, ctx, "dve_chain")
        self.act_chain = Tally(nc, ctx, "act_chain")
        self.pool_chain = Tally(nc, ctx, "pool_chain")
    def sem(self, name):
        self.in_use.append(self.nc.alloc_semaphore(name=name))
        return self.in_use[-1]

    def retire_semaphores(self):
        self.nc.clear_and_free_semaphores(self.in_use)
        self.in_use = []
        self.nc.all_engine_barrier()

    def const(self, name):
        return self.small[:, CONST_AT[name]:CONST_AT[name] + CONST_COLS[name]]

    def const_dram(self, name):
        return self.io["consts"][:, CONST_AT[name]:CONST_AT[name] + CONST_COLS[name]]

    def vstep(self, dve, ins):
        dve.wait_ge(self.dve_chain.sem, self.dve_chain.inc(ins))

    def astep(self, act, ins):
        act.wait_ge(self.act_chain.sem, self.act_chain.inc(ins))

    def gstep(self, pool, ins):
        pool.wait_ge(self.pool_chain.sem, self.pool_chain.inc(ins))


def load_constants(c):
    nc = c.nc
    with nc.Block() as block:
        @block.sync
        def _(sp):
            sp.dma_start(c.small[:, :], c.io["consts"][:, 0:CONST_AT["cos"]]).then_inc(c.const_in, 16)
            sp.wait_ge(c.const_in, 16)


def column_of(gain):
    return gain.rearrange("(p k) -> p k", k=KC)


class Split:

    def __init__(self, nc, stack, name, shape, side=None):
        self.hi = stack.enter_context(nc.sbuf_tensor(f"{name}_hi", shape, F32R, side=side))
        self.lo = stack.enter_context(nc.sbuf_tensor(f"{name}_lo", shape, F32R, side=side))


class Weights:

    def __init__(self, c, stack, tag, sources, groups, R=12, pre=KC, side=None):
        nc, tag = c.nc, f"{tag}_w"
        self.c, self.sources, self.groups, self.R, self.pre = c, sources, groups, R, pre
        self.raw = stack.enter_context(nc.sbuf_tensor(f"{tag}_raw", [P, 2, KC // 2 * BANK], F32, side=side))
        self.hi = stack.enter_context(nc.sbuf_tensor(f"{tag}_hi", [P, R, BANK], F32R, side=side))
        self.lo = stack.enter_context(nc.sbuf_tensor(f"{tag}_lo", [P, R, BANK], F32R, side=side))
        self.raw_in = [c.sem(f"{tag}_raw_in{b}") for b in range(2)]
        self.hi_done, self.lo_done = c.sem(f"{tag}_hi_done"), c.sem(f"{tag}_lo_done")
        self.chunk_used = c.sem(f"{tag}_chunk_used")
        self.done, self.freed = c.sem(f"{tag}_done"), c.sem(f"{tag}_freed")
        self.landed, total = [], [0, 0]
        for q in range(2 * len(sources)):
            total[q % 2] += 16 * len(sources[q // 2][0])
            self.landed.append(total[q % 2])
        self.first = {i: min((g for g, x in enumerate(groups) if x[0] == i), default=0) for i in range(len(sources))}
        self.last = {i: max((g for g, x in enumerate(groups) if x[0] == i), default=0) for i in range(len(sources))}
        self.n_chunks = KC * len(sources)

    def part(self, i0, i1):
        end = min(i1 + 1, len(self.sources))
        g0 = self.first[i0]
        g1 = self.last[i1 - 1] + 1
        return range(g0, g1), (2 * (i0 + 1), 2 * end), (self.pre if i0 == 0 else KC * (i0 + 1), KC * end)

    def half(self, q, w):
        return self.raw[:, q % 2, 0:KC // 2 * w].rearrange("p (k n) -> p k n", n=w)

    def load(self, sp, q0=0, q1=None):
        for q in range(q0, 2 * len(self.sources) if q1 is None else q1):
            pieces, w = self.sources[q // 2]
            if q >= 2:
                sp.wait_ge(self.lo_done, 4 * (q - 1))
            at, k0 = 0, KC // 2 * (q % 2)
            for src in pieces:
                wide = src.shape[-1]
                sp.dma_start(self.half(q, w)[:, :, at:at + wide], src[:, k0:k0 + KC // 2, :]
                             ).then_inc(self.raw_in[q % 2], 16)
                at += wide

    def round_hi(self, engine, emit, n):
        w = self.sources[n // KC][1]
        q = n // (KC // 2)
        engine.wait_ge(self.raw_in[q % 2], self.landed[q])
        if n >= self.R:
            i, k = divmod(n - self.R, KC)
            if k == KC - 1:
                engine.wait_ge(self.done, self.last[i] + 1)
            else:
                engine.wait_ge(self.chunk_used, (KC - 1) * i + k + 1)
        emit(self.hi[:, n % self.R, 0:w], self.half(q, w)[:, n % (KC // 2), :]).then_inc(self.hi_done, 1)

    def take_lo(self, engine, emit, n):
        w = self.sources[n // KC][1]
        engine.wait_ge(self.hi_done, n + 1)
        emit(self.lo[:, n % self.R, 0:w], self.half(n // (KC // 2), w)[:, n % (KC // 2), :],
             self.hi[:, n % self.R, 0:w].bitcast(F32), ALU.subtract).then_inc(self.lo_done, 1)

    def prepare(self, pool, n0=0, n1=None):
        for n in range(n0, self.pre if n1 is None else n1):
            self.round_hi(pool, self.c.nc.gpsimd.tensor_copy, n)
            self.take_lo(pool, self.c.nc.gpsimd.tensor_tensor, n)

    def take_los(self, pool, chunks=None):
        for n in range(*(chunks or (self.pre, self.n_chunks))):
            self.take_lo(pool, self.c.nc.gpsimd.tensor_tensor, n)

    def before(self, act, g):
        if g >= len(self.groups):
            return
        i = self.groups[g][0]
        spare = min(KC, self.R - KC)
        copy = lambda out, in_: self.c.nc.scalar.activation(out, in_, ACT.Copy)
        if g == 0:
            for n in range(self.pre, KC):
                self.round_hi(act, copy, n)
        if i + 1 < len(self.sources):
            for first, lo, hi in ((self.first[i] == g, 0, spare), (self.last[i] == g, spare, KC)):
                if first:
                    for n in range(KC * (i + 1) + lo, KC * (i + 1) + hi):
                        if n >= self.pre:
                            self.round_hi(act, copy, n)


def norm_transposed(c, tag, src, gain, hT, n_tiles=NT, keep=None, gain_row=None, plain=None, next_weights=None,
                    router=None):
    nc = c.nc
    SLOTS = min(4, n_tiles)
    src_t = src.rearrange("(t p) d -> t p d", p=P)
    with ExitStack() as s:
        x = s.enter_context(nc.sbuf_tensor(f"{tag}_x", [P, SLOTS, D], F32))
        sq = s.enter_context(nc.sbuf_tensor(f"{tag}_sq", [P, D], F32))
        diag = s.enter_context(nc.sbuf_tensor(f"{tag}_diag", [P, 2, P], F32))
        g = s.enter_context(nc.sbuf_tensor(f"{tag}_g", [P, KC], F32))
        ss = s.enter_context(nc.sbuf_tensor(f"{tag}_ss", [P, n_tiles], F32))
        rms = s.enter_context(nc.sbuf_tensor(f"{tag}_rms", [P, n_tiles], F32))
        rstd = s.enter_context(nc.sbuf_tensor(f"{tag}_rstd", [P, n_tiles], F32))
        eps = s.enter_context(nc.sbuf_tensor(f"{tag}_eps", [P, 1], F32))
        ps = s.enter_context(nc.psum_tensor(f"{tag}_ps", [P, 2, D], F32))
        g_in, x_in = c.sem(f"{tag}_g_in"), [c.sem(f"{tag}_x_in{b}") for b in range(SLOTS)]
        rms_ready, diag_ready = c.sem(f"{tag}_rms"), c.sem(f"{tag}_diag")
        turned, taken = c.sem(f"{tag}_turned"), c.sem(f"{tag}_taken")
        eps_ready = c.sem(f"{tag}_eps")
        if plain is None:
            full = s.enter_context(nc.sbuf_tensor(f"{tag}_full", [P, 2, KC, P], F32))
            rounded, rest = c.sem(f"{tag}_rounded"), c.sem(f"{tag}_rest")
        if keep is not None:
            keep_t = keep.rearrange("(t p) d -> t p d", p=P)
            grow = s.enter_context(nc.sbuf_tensor(f"{tag}_grow", [P, D], F32))
            xg = s.enter_context(nc.sbuf_tensor(f"{tag}_xg", [P, 2, D], F32))
            xg_ready, xg_out = c.sem(f"{tag}_xg_ready"), [c.sem(f"{tag}_xg_out0"), c.sem(f"{tag}_xg_out1")]
        if router:
            w_in = c.sem(f"{tag}_w_in")
        with nc.Block() as block:
            @block.sync
            def _(sp):
                for t in range(n_tiles):
                    if t >= SLOTS:
                        sp.wait_ge(turned, t - SLOTS + 1)
                        if keep is not None:
                            sp.wait_ge(xg_ready, t - SLOTS + 1)
                    sp.dma_start(x[:, t % SLOTS, :], src_t[t]).then_inc(x_in[t % SLOTS], 16)
                    if t == 0:
                        sp.dma_start(g[:, :], column_of(gain)).then_inc(g_in, 16)
                        if keep is not None:
                            sp.dma_start(grow[:, :], gain_row.partition_broadcast(P)).then_inc(g_in, 16)
                        if router:
                            load_router(c, sp, router[0], router[1], w_in)
                    if t in (1, 3) and next_weights:
                        next_weights.load(sp, t // 2, t // 2 + 1)
                    if keep is not None and t >= 1:
                        sp.wait_ge(xg_ready, t)
                        sp.dma_start(keep_t[t - 1], xg[:, (t - 1) % 2, :]).then_inc(xg_out[(t - 1) % 2], 16)
                if keep is not None:
                    t = n_tiles
                    sp.wait_ge(xg_ready, t)
                    sp.dma_start(keep_t[t - 1], xg[:, (t - 1) % 2, :]).then_inc(xg_out[(t - 1) % 2], 16)
                    sp.wait_ge(xg_out[0], 16 * (n_tiles // 2))
                    sp.wait_ge(xg_out[1], 16 * (n_tiles // 2))

            @block.scalar
            def _(act):
                def round_hi(t):
                    act.wait_ge(taken, t + 1)
                    nc.scalar.activation(hT.hi[:, :, t * P:(t + 1) * P], full[:, t % 2, :, :], ACT.Copy
                                         ).then_inc(rounded, 1)

                act.wait_ge(eps_ready, 1)
                c.astep(act, nc.scalar.activation(rms[:, 0:1], eps[:, :], ACT.Sqrt))
                for t in range(n_tiles):
                    act.wait_ge(x_in[t % SLOTS], 16 * (t // SLOTS + 1))
                    c.astep(act, nc.scalar.activation(sq[:, :], x[:, t % SLOTS, :], ACT.Square, accum_out=ss[:, t:t + 1]))
                    nc.scalar.activation(rms[:, t:t + 1], ss[:, t:t + 1], ACT.Sqrt, scale=1.0 / D,
                                         bias=eps[:, :]).then_inc(rms_ready, 1)
                    if plain is None and t >= 2:
                        round_hi(t - 2)
                if plain is None:
                    round_hi(n_tiles - 2)
                    round_hi(n_tiles - 1)

            @block.vector
            def _(dve):
                nc.vector.memset(eps[:, :], EPS).then_inc(eps_ready, 1)

                def evacuate(t):
                    dve.wait_ge(turned, t + 1)
                    if plain is None and t >= 2:
                        dve.wait_ge(rest, t - 1)
                    out = plain[:, :, t * P:(t + 1) * P] if plain is not None else full[:, t % 2, :, :]
                    nc.vector.tensor_tensor(out, ps[:, t % 2, :].rearrange("p (k n) -> p k n", k=KC),
                                            g[:, :].unsqueeze(2).to_broadcast([P, KC, P]), ALU.mult).then_inc(taken, 1)

                def take_rest(t):
                    sl = slice(t * P, (t + 1) * P)
                    dve.wait_ge(rounded, t + 1)
                    nc.vector.tensor_tensor(hT.lo[:, :, sl], full[:, t % 2, :, :], hT.hi[:, :, sl].bitcast(F32),
                                            ALU.subtract).then_inc(rest, 1)

                for t in range(n_tiles):
                    dve.wait_ge(rms_ready, t + 1)
                    c.vstep(dve, nc.vector.reciprocal(rstd[:, t:t + 1], rms[:, t:t + 1]))
                    if t >= 2:
                        dve.wait_ge(turned, t - 1)
                    nc.vector.tensor_scalar(diag[:, t % 2, :], c.const("ident"), rstd[:, t:t + 1], None, ALU.mult
                                            ).then_inc(diag_ready, 1)
                    if t == 0:
                        dve.wait_ge(g_in, 16 if keep is None else 32)
                    if keep is not None:
                        if t >= 2:
                            dve.wait_ge(xg_out[t % 2], 16 * (t // 2))
                        nc.vector.scalar_tensor_tensor(xg[:, t % 2, :], x[:, t % SLOTS, :], rstd[:, t:t + 1], grow[:, :],
                                                       ALU.mult, ALU.mult).then_inc(xg_ready, 1)
                    if plain is None and t >= 3:
                        take_rest(t - 3)
                    if t >= 1:
                        evacuate(t - 1)
                if plain is None and n_tiles >= 3:
                    take_rest(n_tiles - 3)
                evacuate(n_tiles - 1)
                if plain is None:
                    for t in range(max(0, n_tiles - 2), n_tiles):
                        take_rest(t)

            @block.tensor
            def _(pe):
                def score(t):
                    wr, _, logits = router
                    if t == 0:
                        pe.wait_ge(w_in, 64)
                    pe.wait_ge(taken, t + 1)
                    for k in range(KC):
                        pe.matmul(logits[:, t, 0:NG + NE], plain[:, k, t * P:(t + 1) * P], wr[:, k, :],
                                  start=(k == 0), stop=(k == KC - 1))

                for t in range(n_tiles):
                    pe.wait_ge(diag_ready, t + 1)
                    if t >= 2:
                        pe.wait_ge(taken, t - 1)
                    for k in range(KC):
                        ins = pe.matmul(ps[:, t % 2, k * P:(k + 1) * P], x[:, t % SLOTS, k::KC], diag[:, t % 2, :],
                                        start=True, stop=True)
                    ins.then_inc(turned, 1)
                    if router and t >= 1:
                        score(t - 1)
                if router:
                    score(n_tiles - 1)

            @block.gpsimd
            def _(pool):
                if next_weights:
                    next_weights.prepare(pool)


def by_rows(w, a, b):
    return w.rearrange("(p k) n -> p k n", k=KC)[:, :, a:b]


def by_chunks(w, a, b):
    return w.rearrange("(k p) n -> p k n", p=P)[:, :, a:b]


def products(pe, out, stationary, moving, start, stop):
    (a, b), (x, y) = stationary, moving
    pe.matmul(out, a, x, start=start, stop=False)
    pe.matmul(out, a, y, start=False, stop=False)
    return pe.matmul(out, b, x, start=False, stop=stop)


def matmul_groups(pe, weights, hT, ps, n_banks, span=None):
    for g in span or range(len(weights.groups)):
        i, kind, a, w, t = weights.groups[g]
        if g >= n_banks:
            pe.wait_ge(weights.freed, g - n_banks + 1)
        x = hT(i) if callable(hT) else hT
        for k in range(KC):
            n = KC * i + k
            if g == weights.first[i]:
                pe.wait_ge(weights.lo_done, n + 1)
            slot = n % weights.R
            if kind == "rows":
                tok, col = slice(t * P, (t + 1) * P), slice(a, a + w)
                acts = (x.hi[:, k, tok], x.lo[:, k, tok])
                ins = products(pe, ps[:, g % n_banks, 0:w], acts, (weights.hi[:, slot, col], weights.lo[:, slot, col]),
                               k == 0, k == KC - 1)
            else:
                tok, col = slice(t * w, (t + 1) * w), slice(a, a + P)
                acts = (x.hi[:, k, tok], x.lo[:, k, tok])
                ins = products(pe, ps[:, g % n_banks, 0:w], (weights.hi[:, slot, col], weights.lo[:, slot, col]), acts,
                               k == 0, k == KC - 1)
            if g == weights.last[i] and k < KC - 1:
                ins.then_inc(weights.chunk_used, 1)
        ins.then_inc(weights.done, 1)
        yield g


def first_weights(c, stack):
    w = c.io["w_in"]
    qk_cols, v_at, g_at, c_at = 2 * AW, 2 * AW, 3 * AW, 4 * AW
    sources, groups, at = [], [], {}
    for i in range(qk_cols // BANK):
        sources.append(([by_rows(w, i * BANK, (i + 1) * BANK)], BANK))
        groups += [(i, "rows", 0, BANK, t) for t in range(NT)]
    at["v"] = len(groups)
    for a, wd in ((0, BANK), (BANK, AW - BANK)):
        groups += [(len(sources), "rows", 0, wd, t) for t in range(NT)]
        sources.append(([by_rows(w, v_at + a, v_at + a + wd)], wd))
    at["gate"] = len(groups)
    for a, wd in ((0, BANK), (BANK, AW - BANK)):
        for sub in range(wd // P):
            for half in range(2):
                at[len(groups)] = (a // P + sub, half)
                groups.append((len(sources), "cols", sub * P, BANK, half))
        sources.append(([by_rows(w, g_at + a, g_at + a + wd)], wd))
    at["conv"] = len(groups)
    for j in range(CW // P):
        for half in range(2):
            for kind in range(4):
                groups.append((len(sources), "cols", kind * P, BANK, half))
        sources.append(([by_rows(w, c_at + kind * CW + j * P, c_at + kind * CW + (j + 1) * P)
                         for kind in range(4)], BANK))
    weights = Weights(c, stack, "p1", sources, groups, R=11)
    weights.at = at
    return weights


def project_first(c, weights, hT, qk_dram, v_dram, mixT):
    nc, io = c.nc, c.io
    groups, at = weights.groups, weights.at
    n_qk, n_v, n_g = at["v"], at["gate"], at["conv"]
    v_rows = v_dram.rearrange("(t p) d -> t p d", p=P)
    NB = 4
    with ExitStack() as s:
        cs = s.enter_context(nc.sbuf_tensor("rope_cs", [P, 2 * NT * 32], F32))
        rot = s.enter_context(nc.sbuf_tensor("rope_rot", [P, 2, BANK], F32))
        rb = s.enter_context(nc.sbuf_tensor("rope_b", [P, BANK], F32))
        cw = s.enter_context(nc.sbuf_tensor("conv_taps", [P, 3, CW // P], F32))
        cz = s.enter_context(nc.sbuf_tensor("conv_z", [P, 4, S], F32))
        cu = s.enter_context(nc.sbuf_tensor("conv_u", [P, S + 2], F32))
        ps = s.enter_context(nc.psum_tensor("p1_ps", [P, NB, BANK], F32))
        pt = s.enter_context(nc.psum_tensor("p1_pt", [P, 2, BANK], F32))
        qk_sb = s.enter_context(nc.sbuf_tensor("p1_qk", [P, 2, BANK // P, P], F32))
        v_sb = s.enter_context(nc.sbuf_tensor("p1_v", [P, 2, BANK], F32))
        tables_in = c.sem("rope_tables_in")
        done, freed = weights.done, weights.freed
        qk_out, v_out = [c.sem(f"qk_out{b}") for b in range(2)], [c.sem(f"v_out{b}") for b in range(2)]
        rot_ready, rot_turned, rot_kept = c.sem("rot_ready"), c.sem("rot_turned"), c.sem("rot_kept")
        conv_done = c.sem("conv_done")
        cos = cs[:, 0:NT * 32].rearrange("p (t f) -> p t f", t=NT)
        sin = cs[:, NT * 32:2 * NT * 32].rearrange("p (t f) -> p t f", t=NT)
        NHB = BANK // HD
        with nc.Block() as block:
            @block.sync
            def _(sp):
                weights.load(sp, 2)

            @block.gpsimd
            def _(pool):
                a = CONST_AT["cos"]
                pool.dma_start(cs[:, :], io["consts"][:, a:a + 2 * NT * 32]).then_inc(tables_in, 16)
                for j in range(CW // P):
                    with nc.allow_non_contiguous_dma(reason="a few hundred taps, once"):
                        pool.dma_start(cw[:, :, j:j + 1],
                                       io["conv_w"][:, j * P:(j + 1) * P].rearrange("j (c o) -> c j o", o=1)
                                       ).then_inc(tables_in, 16)
                weights.take_los(pool)

            @block.tensor
            def _(pe):
                def turn(g):
                    pe.wait_ge(rot_ready, g + 1)
                    if g >= 2:
                        pe.wait_ge(rot_kept, g - 1)
                    for j in range(BANK // P):
                        ins = pe.transpose(pt[:, g % 2, j * P:(j + 1) * P], rot[:, g % 2, j * P:(j + 1) * P],
                                           c.const("ident"))
                    ins.then_inc(rot_turned, 1)

                for g in matmul_groups(pe, weights, hT, ps, NB):
                    if 1 <= g <= n_qk:
                        turn(g - 1)

            @block.vector
            def _(dve):
                dve.wait_ge(tables_in, 16 * (1 + CW // P))
                for g in range(n_qk):
                    t = g % NT
                    z = ps[:, g % NB, :].rearrange("p (h a f) -> p h a f", h=NHB, a=2)
                    r = rot[:, g % 2, :].rearrange("p (h a f) -> p h a f", h=NHB, a=2)
                    b = rb[:, :].rearrange("p (h a f) -> p h a f", h=NHB, a=2)
                    cb = cos[:, t, :].unsqueeze(1).to_broadcast([P, NHB, 32])
                    sb = sin[:, t, :].unsqueeze(1).to_broadcast([P, NHB, 32])
                    dve.wait_ge(done, g + 1)
                    if g >= 2:
                        dve.wait_ge(rot_turned, g - 1)
                    nc.vector.tensor_tensor(r[:, :, 0, :], z[:, :, 0, :], cb, ALU.mult)
                    nc.vector.tensor_tensor(r[:, :, 1, :], z[:, :, 1, :], cb, ALU.mult)
                    nc.vector.tensor_tensor(b[:, :, 0, :], z[:, :, 1, :], sb, ALU.mult)
                    nc.vector.tensor_tensor(b[:, :, 1, :], z[:, :, 0, :], sb, ALU.mult).then_inc(freed, 1)
                    dve.wait_ge(freed, g + 1)
                    nc.vector.tensor_tensor(r[:, :, 0, :], r[:, :, 0, :], b[:, :, 0, :], ALU.subtract)
                    ins = nc.vector.tensor_tensor(r[:, :, 1, :], r[:, :, 1, :], b[:, :, 1, :], ALU.add)
                    ins.then_inc(rot_ready, 1)
                    dve.wait_ge(rot_ready, g + 1)
                for j in range(CW // P):
                    dve.wait_ge(freed, n_g + 8 * (j + 1))
                    c.vstep(dve, nc.vector.memset(cu[:, 0:2], 0.0))
                    c.vstep(dve, nc.vector.tensor_tensor(cu[:, 2:S + 2], cz[:, 2, :], cz[:, 0, :], ALU.mult))
                    c.vstep(dve, nc.vector.tensor_scalar(cz[:, 0, :], cu[:, 0:S], cw[:, 0, j:j + 1], None, ALU.mult))
                    for tap in (1, 2):
                        c.vstep(dve, nc.vector.scalar_tensor_tensor(cz[:, 0, :], cu[:, tap:tap + S],
                                                                    cw[:, tap, j:j + 1], cz[:, 0, :],
                                                                    ALU.mult, ALU.add))
                    c.vstep(dve, nc.vector.tensor_tensor(cz[:, 0, :], cz[:, 0, :], cz[:, 1, :], ALU.mult))
                    nc.vector.tensor_tensor(mixT[:, AW // P + j, :], cz[:, 0, :], cz[:, 3, :],
                                            ALU.mult).then_inc(conv_done, 1)

            @block.scalar
            def _(act):
                def keep(g):
                    i, t = g // NT, g % NT
                    act.wait_ge(rot_turned, g + 1)
                    if g >= 2:
                        act.wait_ge(qk_out[g % 2], 16 * (g // 2))
                    nc.scalar.activation(qk_sb[:, g % 2, :, :], pt[:, g % 2, :].rearrange("p (j n) -> p j n", j=4),
                                         ACT.Copy).then_inc(rot_kept, 1)
                    act.wait_ge(rot_kept, g + 1)
                    act.dma_start(qk_dram[4 * i:4 * i + 4, :, t * P:(t + 1) * P].rearrange("j p n -> p j n"),
                                  qk_sb[:, g % 2, :, :]).then_inc(qk_out[g % 2], 16)

                weights.before(act, 0)
                for g in range(n_qk):
                    weights.before(act, g + 1)
                    keep(g)
                act.wait_ge(freed, n_qk)
                for g in range(n_qk, len(groups)):
                    i, kind, a, wd, t = groups[g]
                    if g > n_qk:
                        weights.before(act, g)
                    act.wait_ge(done, g + 1)
                    if g < n_v:
                        a, m = (0 if g - n_qk < NT else BANK), g - n_qk
                        if m >= 2:
                            act.wait_ge(v_out[m % 2], 16 * (m // 2))
                        ins = nc.scalar.activation(v_sb[:, m % 2, 0:wd], ps[:, g % NB, 0:wd], ACT.Copy)
                    elif g < n_g:
                        chunk, half = at[g]
                        ins = nc.scalar.activation(mixT[:, chunk, half * BANK:(half + 1) * BANK], ps[:, g % NB, :],
                                                   ACT.Silu)
                    else:
                        j, r = divmod(g - n_g, 8)
                        half, which = divmod(r, 4)
                        if r == 0 and j:
                            act.wait_ge(conv_done, j)
                        ins = nc.scalar.activation(cz[:, which, half * BANK:(half + 1) * BANK], ps[:, g % NB, :],
                                                   ACT.Silu if which == 3 else ACT.Copy)
                    ins.then_inc(freed, 1)
                    if g < n_v:
                        act.wait_ge(freed, g + 1)
                        act.dma_start(v_rows[t, :, a:a + wd], v_sb[:, m % 2, 0:wd]).then_inc(v_out[m % 2], 16)
                for b in range(2):
                    act.wait_ge(qk_out[b], 16 * n_qk // 2)
                    act.wait_ge(v_out[b], 16 * (n_v - n_qk) // 2)


def attention(c, qk_dram, v_dram, mixT, next_weights):
    nc, io = c.nc, c.io
    steps = [(hp * 2 + h, hp, a) for hp in range(NH // 2) for q in range(NT // 2) for h in range(2)
             for a in (q, NT - 1 - q)]
    N = len(steps)

    def bank(i):
        return BANK * (i % 2)

    def pair_after(i):
        q, r = divmod(i - 6, 4)
        return 2 * q + r if i >= 6 and r < 2 and 2 * q + r < N // 2 else None
    with ExitStack() as s:
        logc = s.enter_context(nc.sbuf_tensor("logc", [P, S], F32))
        qk = s.enter_context(nc.sbuf_tensor("att_qk", [P, 2, 2, S], F32))
        v = s.enter_context(nc.sbuf_tensor("att_v", [P, 2, NT, P], F32))
        sc = s.enter_context(nc.sbuf_tensor("att_scores", [P, 4, S], F32))
        pT = s.enter_context(nc.sbuf_tensor("att_pT", [P, 2, S], F32))
        mx = s.enter_context(nc.sbuf_tensor("att_max", [P, N], F32))
        nmx = s.enter_context(nc.sbuf_tensor("att_negmax", [P, N], F32))
        den = s.enter_context(nc.sbuf_tensor("att_den", [P, N], F32))
        rden = s.enter_context(nc.sbuf_tensor("att_rden", [P, N], F32))
        on = s.enter_context(nc.sbuf_tensor("att_out", [P, 4, P], F32))
        ps_s = s.enter_context(nc.psum_tensor("att_ps_s", [P, 3 * BANK], F32))
        ps_t = s.enter_context(nc.psum_tensor("att_ps_t", [P, 3 * BANK], F32))
        ps_o = s.enter_context(nc.psum_tensor("att_ps_o", [P, BANK], F32))
        ps_m = s.enter_context(nc.psum_tensor("att_ps_m", [P, BANK], F32))
        logc_in, pair_in = c.sem("logc_in"), [c.sem(f"att_pair_in{b}") for b in range(2)]
        scored, maxed, expd = c.sem("att_scored"), c.sem("att_maxed"), c.sem("att_expd")
        turned, kept = c.sem("att_turned"), c.sem("att_kept")
        summed, normed = c.sem("att_summed"), c.sem("att_normed")
        pair_turned, pair_kept = c.sem("att_pair_turned"), c.sem("att_pair_kept")
        with nc.Block() as block:
            @block.sync
            def _(sp):
                sp.dma_start(logc[:, :], c.const_dram("logc")).then_inc(logc_in, 16)
                for hp in range(NH // 2):
                    if hp >= 2:
                        sp.wait_ge(summed, 2 * NT * (hp - 1))
                    for k in range(2):
                        sp.dma_start(qk[:, hp % 2, k, :], qk_dram[k * AW // P + hp]).then_inc(pair_in[hp % 2], 16)
                    sp.dma_start(v[:, hp % 2, :, :], v_dram[:, hp * P:(hp + 1) * P].rearrange("(t p) d -> p t d", p=P)
                                 ).then_inc(pair_in[hp % 2], 16)
                    if hp == 1:
                        next_weights.load(sp)

            @block.gpsimd
            def _(pool):
                next_weights.prepare(pool)

            @block.tensor
            def _(pe):
                def scores(i):
                    h, hp, a = steps[i]
                    lo, n = HD * (h % 2), (a + 1) * P
                    if i % (2 * NT) == 0:
                        pe.wait_ge(pair_in[hp % 2], 48 * (hp // 2 + 1))
                    if i >= 2:
                        pe.wait_ge(maxed, i - 1)
                    for u in range(0, n, BANK):
                        m = min(BANK, n - u)
                        ins = pe.matmul(ps_s[:, bank(i) + u:bank(i) + u + m], qk[lo:lo + HD, hp % 2, 0, a * P:(a + 1) * P],
                                        qk[lo:lo + HD, hp % 2, 1, u:u + m], start=True, stop=True)
                    ins.then_inc(scored, 1)

                def turn(i):
                    a = steps[i][2]
                    pe.wait_ge(expd, i + 1)
                    if i >= 2:
                        pe.wait_ge(kept, i - 1)
                    for j in range(a + 1):
                        ins = pe.transpose(ps_t[:, bank(i) + j * P:bank(i) + (j + 1) * P], sc[:, i % 4, j * P:(j + 1) * P],
                                           c.const("ident"))
                    ins.then_inc(turned, 1)

                def values(i):
                    h, hp, a = steps[i]
                    pe.wait_ge(kept, i + 1)
                    if i >= 1:
                        pe.wait_ge(normed, i)
                    at = (i % 2) * HD
                    for j in range(a + 1):
                        ins = pe.matmul(ps_o[:, at:at + HD], pT[:, i % 2, j * P:(j + 1) * P],
                                        v[:, hp % 2, j, HD * (h % 2):HD * (h % 2) + HD], start=(j == 0), stop=(j == a))
                    ins.then_inc(summed, 1)

                def pair(m):
                    pe.wait_ge(normed, 4 * (m // 2) + 3 + m % 2)
                    if m >= 1:
                        pe.wait_ge(pair_kept, m)
                    pe.transpose(ps_m[:, 0:P], on[:, m % 4, :], c.const("ident")).then_inc(pair_turned, 1)

                for i in range(N + 4):
                    if i < N:
                        scores(i)
                    if 2 <= i <= N + 1:
                        turn(i - 2)
                    if 3 <= i <= N + 2:
                        values(i - 3)
                    if pair_after(i) is not None:
                        pair(pair_after(i))

            @block.vector
            def _(dve):
                dve.wait_ge(logc_in, 16)

                def maxes(i):
                    a = steps[i][2]
                    n = (a + 1) * P
                    dve.wait_ge(scored, i + 1)
                    if i >= 4:
                        dve.wait_ge(turned, i - 3)
                    c.vstep(dve, nc.vector.tensor_tensor_reduce(sc[:, i % 4, 0:n], ps_s[:, bank(i):bank(i) + n], logc[:, S - n:S],
                                                                SCALE, NEG, ALU.add, ALU.max, mx[:, i:i + 1]))
                    nc.vector.tensor_scalar(nmx[:, i:i + 1], mx[:, i:i + 1], -1.0, None, ALU.mult).then_inc(maxed, 1)

                def norm(i):
                    h, hp, a = steps[i]
                    m, at = 2 * (i // 4) + i % 2, (i % 2) * HD
                    dve.wait_ge(expd, i + 1)
                    c.vstep(dve, nc.vector.reciprocal(rden[:, i:i + 1], den[:, i:i + 1]))
                    dve.wait_ge(summed, i + 1)
                    if m >= 4:
                        dve.wait_ge(pair_turned, m - 3)
                    nc.vector.tensor_scalar(on[:, m % 4, HD * (h % 2):HD * (h % 2) + HD], ps_o[:, at:at + HD], rden[:, i:i + 1], None,
                                            ALU.mult).then_inc(normed, 1)

                def gate(m):
                    h, hp, a = steps[4 * (m // 2) + m % 2]
                    dve.wait_ge(pair_turned, m + 1)
                    nc.vector.tensor_tensor(mixT[:, hp, a * P:(a + 1) * P], ps_m[:, 0:P], mixT[:, hp, a * P:(a + 1) * P],
                                            ALU.mult).then_inc(pair_kept, 1)

                for i in range(N + 4):
                    if i < N:
                        maxes(i)
                    if 3 <= i <= N + 2:
                        norm(i - 3)
                    if pair_after(i) is not None:
                        gate(pair_after(i))

            @block.scalar
            def _(act):
                for i in range(N + 2):
                    if i >= 2:
                        m = i - 2
                        n = (steps[m][2] + 1) * P
                        act.wait_ge(turned, m + 1)
                        if m >= 2:
                            act.wait_ge(summed, m - 1)
                        nc.scalar.activation(pT[:, m % 2, 0:n], ps_t[:, bank(m):bank(m) + n], ACT.Copy).then_inc(kept, 1)
                    if i < N:
                        n = (steps[i][2] + 1) * P
                        act.wait_ge(maxed, i + 1)
                        nc.scalar.activation(sc[:, i % 4, 0:n], sc[:, i % 4, 0:n], ACT.Exp, bias=nmx[:, i:i + 1],
                                             accum_out=den[:, i:i + 1]).then_inc(expd, 1)


def out_weights(c, stack, tag, w, side=None):
    sources = [([by_chunks(w, n * BANK, (n + 1) * BANK)], BANK) for n in range(2)]
    return Weights(c, stack, tag, sources, [], R=2 * KC, pre=2 * KC, side=side)


def project_out(c, tag, weights, mT, src, dst, post_gain=None):
    nc = c.nc
    src_t, dst_t = src.rearrange("(t p) d -> t p d", p=P), dst.rearrange("(t p) d -> t p d", p=P)
    with ExitStack() as s:
        m = Split(nc, s, f"{tag}_m", [P, 2, KC, P])
        x = s.enter_context(nc.sbuf_tensor(f"{tag}_x", [P, 2, D], F32))
        y = s.enter_context(nc.sbuf_tensor(f"{tag}_y", [P, 2, D], F32))
        if post_gain is not None:
            sq = s.enter_context(nc.sbuf_tensor(f"{tag}_sq", [P, D], F32))
            g = s.enter_context(nc.sbuf_tensor(f"{tag}_g", [P, D], F32))
        ss = s.enter_context(nc.sbuf_tensor(f"{tag}_ss", [P, 3 * NT], F32))
        eps = s.enter_context(nc.sbuf_tensor(f"{tag}_eps", [P, 1], F32))
        ps = s.enter_context(nc.psum_tensor(f"{tag}_ps", [P, 3, D], F32))
        g_in, x_in = c.sem(f"{tag}_g_in"), [c.sem(f"{tag}_x_in{b}") for b in range(2)]
        y_out = [c.sem(f"{tag}_y_out{b}") for b in range(2)]
        done, rms_ready, y_ready = c.sem(f"{tag}_done"), c.sem(f"{tag}_rms"), c.sem(f"{tag}_y_ready")
        eps_ready, rounded, rest = c.sem(f"{tag}_eps_ready"), c.sem(f"{tag}_rounded"), c.sem(f"{tag}_rest")
        with nc.Block() as block:
            @block.sync
            def _(sp):
                if post_gain is not None:
                    sp.dma_start(g[:, :], post_gain.partition_broadcast(P)).then_inc(g_in, 16)
                for t in range(NT + 1):
                    if t < NT:
                        if t >= 2:
                            sp.wait_ge(y_ready, t - 1)
                        sp.dma_start(x[:, t % 2, :], src_t[t]).then_inc(x_in[t % 2], 16)
                    if t >= 1:
                        sp.wait_ge(y_ready, t)
                        sp.dma_start(dst_t[t - 1], y[:, (t - 1) % 2, :]).then_inc(y_out[(t - 1) % 2], 16)
                for b in range(2):
                    sp.wait_ge(y_out[b], 16 * NT // 2)

            @block.gpsimd
            def _(pool):
                for t in range(NT):
                    pool.wait_ge(rounded, t + 1)
                    nc.gpsimd.tensor_tensor(m.lo[:, t % 2, :, :], mT[:, :, t * P:(t + 1) * P],
                                            m.hi[:, t % 2, :, :].bitcast(F32), ALU.subtract).then_inc(rest, 1)

            @block.tensor
            def _(pe):
                pe.wait_ge(weights.lo_done, 2 * KC)
                for t in range(NT):
                    pe.wait_ge(rest, t + 1)
                    if t >= 3:
                        pe.wait_ge(y_ready, t - 2)
                    for n in range(2):
                        for k in range(KC):
                            slot = KC * n + k
                            ins = products(pe, ps[:, t % 3, n * BANK:(n + 1) * BANK],
                                           (m.hi[:, t % 2, k, :], m.lo[:, t % 2, k, :]),
                                           (weights.hi[:, slot, :], weights.lo[:, slot, :]), k == 0, k == KC - 1)
                    ins.then_inc(done, 1)

            @block.scalar
            def _(act):
                def round_hi(t):
                    if t >= 2:
                        act.wait_ge(done, t - 1)
                    nc.scalar.activation(m.hi[:, t % 2, :, :], mT[:, :, t * P:(t + 1) * P], ACT.Copy).then_inc(rounded, 1)

                act.wait_ge(eps_ready, 1)
                round_hi(0)
                round_hi(1)
                for t in range(NT):
                    act.wait_ge(done, t + 1)
                    if t + 2 < NT:
                        round_hi(t + 2)
                    if post_gain is not None:
                        c.astep(act, nc.scalar.activation(sq[:, :], ps[:, t % 3, :], ACT.Square,
                                                          accum_out=ss[:, t:t + 1]))
                        nc.scalar.activation(ss[:, NT + t:NT + t + 1], ss[:, t:t + 1], ACT.Sqrt, scale=1.0 / D,
                                             bias=eps[:, :]).then_inc(rms_ready, 1)

            @block.vector
            def _(dve):
                nc.vector.memset(eps[:, :], EPS).then_inc(eps_ready, 1)
                if post_gain is not None:
                    dve.wait_ge(g_in, 16)
                for t in range(NT):
                    dve.wait_ge(done, t + 1)
                    if t >= 2:
                        dve.wait_ge(y_out[t % 2], 16 * (t // 2))
                    dve.wait_ge(x_in[t % 2], 16 * (t // 2 + 1))
                    yt = y[:, t % 2, :]
                    if post_gain is None:
                        nc.vector.tensor_tensor(yt, ps[:, t % 3, :], x[:, t % 2, :], ALU.add).then_inc(y_ready, 1)
                    else:
                        dve.wait_ge(rms_ready, t + 1)
                        r = ss[:, 2 * NT + t:2 * NT + t + 1]
                        c.vstep(dve, nc.vector.reciprocal(r, ss[:, NT + t:NT + t + 1]))
                        c.vstep(dve, nc.vector.scalar_tensor_tensor(yt, ps[:, t % 3, :], r, g[:, :], ALU.mult, ALU.mult))
                        nc.vector.tensor_tensor(yt, yt, x[:, t % 2, :], ALU.add).then_inc(y_ready, 1)


def first_block(c, x, x1, qk_dram, v_dram):
    nc, io = c.nc, c.io
    with ExitStack() as s:
        mixT = s.enter_context(nc.sbuf_tensor("mixT", [P, KC, S], F32))
        with ExitStack() as s2:
            weights = first_weights(c, s2)
            hT = Split(nc, s2, "hT", [P, KC, S])
            norm_transposed(c, "n1", x, io["norm_pre_g"], hT, next_weights=weights)
            project_first(c, weights, hT, qk_dram, v_dram, mixT)
        weights = out_weights(c, s, "o1", io["w_out"])
        attention(c, qk_dram, v_dram, mixT, weights)
        project_out(c, "o1", weights, mixT, x, x1, post_gain=io["norm_post_g"])


IF_AT, U_AT, SV_AT, GA_AT, GB_AT = 4 * D, 4 * D + 8, 5 * D + 8, 6 * D + 8, 7 * D + 8
V_AT, O_AT = 2 * D, 3 * D


def row_panels(w, at, panel0):
    sources = [([by_rows(w, at + n * BANK, at + (n + 1) * BANK)], BANK) for n in range(D // BANK)]
    groups = [(panel0 + n, "rows", 0, BANK, t) for n in range(D // BANK) for t in range(NT)]
    return sources, groups


def mixer_weights(c, stack):
    w = c.io["w_in_2"]
    sources, groups = [], []
    for at in (SV_AT, U_AT, GB_AT):
        a, b = row_panels(w, at, len(sources))
        sources, groups = sources + a, groups + b
    for n in range(D // BANK):
        for at in (O_AT, GA_AT):
            groups += [(len(sources), "rows", 0, BANK, t) for t in range(NT)]
            sources.append(([by_rows(w, at + n * BANK, at + (n + 1) * BANK)], BANK))
    a, b = row_panels(w, V_AT, len(sources))
    sources, groups = sources + a, groups + b
    for n in range(2 * D // BANK):
        for sub in range(BANK // P):
            groups += [(len(sources), "cols", sub * P, BANK, half) for half in range(2)]
        sources.append(([by_rows(w, n * BANK, (n + 1) * BANK)], BANK))
    return Weights(c, stack, "p2", sources, groups)


SGU_PANELS, GATE_PANELS, QKV_PANELS = (0, 6), (6, 10), (10, 16)


def spatial_gate(c, weights, hT, yb_dram):
    nc, io = c.nc, c.io
    groups = weights.groups
    span, halves, chunks = weights.part(*SGU_PANELS)
    per = len(span) // 3
    NB = 4
    yb_t = yb_dram.rearrange("(t p) d -> t p d", p=P)
    with ExitStack() as s:
        sv = s.enter_context(nc.sbuf_tensor("sgu_v", [P, NT, D], F32))
        gb = s.enter_context(nc.sbuf_tensor("sgu_gate", [P, NB, BANK], F32))
        gbias = s.enter_context(nc.sbuf_tensor("sgu_gate_bias", [P, D], F32))
        gain = s.enter_context(nc.sbuf_tensor("sgu_gain", [P, D], F32))
        sq = s.enter_context(nc.sbuf_tensor("sgu_sq", [P, D], F32))
        ws = s.enter_context(nc.sbuf_tensor("sgu_ws", [P, 8, P], F32))
        bs = s.enter_context(nc.sbuf_tensor("sgu_bs", [P, 8], F32))
        ss = s.enter_context(nc.sbuf_tensor("sgu_ss", [P, 2 * NT], F32))
        eps = s.enter_context(nc.sbuf_tensor("sgu_eps", [P, 1], F32))
        ps = s.enter_context(nc.psum_tensor("sgu_ps", [P, NB, BANK], F32))
        pm = s.enter_context(nc.psum_tensor("sgu_pm", [P, 4, BANK], F32))
        done, freed = weights.done, weights.freed
        small_in = c.sem("sgu_small_in")
        eps_ready, ws_ready, v_ready = c.sem("sgu_eps_ready"), c.sem("sgu_ws_ready"), c.sem("sgu_v_ready")
        rms_ready, gated = c.sem("sgu_rms"), c.sem("sgu_gated")
        gate_ready, mixed, mix_kept = c.sem("sgu_gate_ready"), c.sem("sgu_mixed"), c.sem("sgu_mix_kept")
        y_out = c.sem("sgu_y_out")
        with nc.Block() as block:
            @block.sync
            def _(sp):
                weights.load(sp, *halves)
                for t in range(NT):
                    sp.wait_ge(gated, per + NT + t + 1)
                    sp.dma_start(yb_t[t], sv[:, t, :]).then_inc(y_out, 16)
                sp.wait_ge(y_out, 16 * NT)

            @block.gpsimd
            def _(pool):
                pool.dma_start(gain[:, :], io["sgu_norm_g_2"].partition_broadcast(P)).then_inc(small_in, 16)
                pool.dma_start(gbias[:, :], io["b_gate_2"][D:2 * D].partition_broadcast(P)).then_inc(small_in, 16)
                pool.dma_start(ws[:, :, :], io["w_s_T"].rearrange("g s t -> s g t")).then_inc(small_in, 16)
                with nc.allow_non_contiguous_dma(reason="1024 biases, once"):
                    pool.dma_start(bs[:, :].unsqueeze(2), io["b_s_2"].rearrange("g (t o) -> t g o", o=1)
                                   ).then_inc(small_in, 16)
                weights.take_los(pool, chunks)

            @block.tensor
            def _(pe):
                for g in matmul_groups(pe, weights, hT, ps, NB, span):
                    if g == per + NB - 1:
                        pe.wait_ge(ws_ready, 1)
                        pe.wait_ge(v_ready, NT)
                        for n in range(16):
                            sg, half = divmod(n, 2)
                            if n >= 4:
                                pe.wait_ge(mix_kept, n - 3)
                            pe.matmul(pm[:, n % 4, :].rearrange("p (c d) -> p c d", c=4), ws[:, sg, :],
                                      sv[:, 4 * half:4 * half + 4, sg * P:(sg + 1) * P], start=True, stop=True
                                      ).then_inc(mixed, 1)

            @block.scalar
            def _(act):
                act.wait_ge(eps_ready, 1)
                weights.before(act, 0)
                for g in span:
                    i, kind, a, wd, t = groups[g]
                    n = i % 2
                    if g + 1 < span.stop:
                        weights.before(act, g + 1)
                    if g >= per + NB and g < 2 * per:
                        act.wait_ge(gated, g - NB - per + 1)
                    if g < 2 * per:
                        act.wait_ge(done, g + 1)
                        dst = sv[:, t, n * BANK:(n + 1) * BANK] if g < per else gb[:, g % NB, :]
                        nc.scalar.activation(dst, ps[:, g % NB, :], ACT.Gelu_apprx_tanh).then_inc(freed, 1)
                    else:
                        act.wait_ge(freed, g + 1)
                        nc.scalar.activation(gb[:, g % NB, :], gb[:, g % NB, :], ACT.Sigmoid).then_inc(gate_ready, 1)
                    if g < per and n == 1:
                        act.wait_ge(freed, g + 1)
                        c.astep(act, nc.scalar.activation(sq[:, :], sv[:, t, :], ACT.Square,
                                                          accum_out=ss[:, t:t + 1]))
                    if g == per - 1:
                        nc.scalar.activation(ss[:, NT:], ss[:, 0:NT], ACT.Sqrt, scale=1.0 / D,
                                             bias=eps[:, :]).then_inc(rms_ready, 1)

            @block.vector
            def _(dve):
                nc.vector.memset(eps[:, :], EPS).then_inc(eps_ready, 1)
                dve.wait_ge(small_in, 64)
                nc.vector.tensor_tensor(ws[:, :, :], ws[:, :, :], c.const("causal").unsqueeze(1).to_broadcast([P, 8, P]),
                                        ALU.mult).then_inc(ws_ready, 1)
                dve.wait_ge(rms_ready, 1)
                c.vstep(dve, nc.vector.reciprocal(ss[:, 0:NT], ss[:, NT:]))
                for t in range(NT):
                    nc.vector.scalar_tensor_tensor(sv[:, t, :], sv[:, t, :], ss[:, t:t + 1], gain[:, :],
                                                   ALU.mult, ALU.mult).then_inc(v_ready, 1)
                for n in range(16):
                    sg, half = divmod(n, 2)
                    dve.wait_ge(mixed, n + 1)
                    nc.vector.tensor_scalar(sv[:, 4 * half:4 * half + 4, sg * P:(sg + 1) * P],
                                            pm[:, n % 4, :].rearrange("p (c d) -> p c d", c=4), bs[:, sg:sg + 1],
                                            None, ALU.add).then_inc(mix_kept, 1)
                dve.wait_ge(mix_kept, 16)
                for g in range(per, 3 * per + 1):
                    if 2 * per <= g < 3 * per:
                        n = groups[g][0] % 2
                        dve.wait_ge(done, g + 1)
                        dve.wait_ge(gated, g - per - NB + 1)
                        dve.wait_ge(freed, g)
                        nc.vector.tensor_tensor(gb[:, g % NB, :], ps[:, g % NB, :], gbias[:, n * BANK:(n + 1) * BANK],
                                                ALU.add).then_inc(freed, 1)
                    if g > per:
                        i, kind, a, wd, t = groups[g - 1]
                        n = i % 2
                        if g - 1 < 2 * per:
                            dve.wait_ge(freed, g)
                        else:
                            dve.wait_ge(gate_ready, g - 2 * per)
                        y = sv[:, t, n * BANK:(n + 1) * BANK]
                        if g > 2 * per:
                            dve.wait_ge(gated, g - 2 * per)
                        nc.vector.tensor_tensor(y, y, gb[:, (g - 1) % NB, :], ALU.mult).then_inc(gated, 1)


def output_gate(c, weights, hT, og_dram):
    nc, io = c.nc, c.io
    groups = weights.groups
    span, halves, chunks = weights.part(*GATE_PANELS)
    NB = 4
    og_t = og_dram.rearrange("(t p) d -> t p d", p=P)
    with ExitStack() as s:
        og = s.enter_context(nc.sbuf_tensor("og", [P, NT, D], F32))
        ga = s.enter_context(nc.sbuf_tensor("og_gate", [P, NB, BANK], F32))
        gbias = s.enter_context(nc.sbuf_tensor("og_bias", [P, D], F32))
        gain = s.enter_context(nc.sbuf_tensor("og_gain", [P, D], F32))
        ps = s.enter_context(nc.psum_tensor("og_ps", [P, NB, BANK], F32))
        done, freed = weights.done, weights.freed
        bias_in, gate_ready, gated, out = c.sem("og_bias_in"), c.sem("og_gate_ready"), c.sem("og_gated"), c.sem("og_out")
        with nc.Block() as block:
            @block.sync
            def _(sp):
                sp.dma_start(gbias[:, :], io["b_gate_2"][0:D].partition_broadcast(P)).then_inc(bias_in, 16)
                sp.dma_start(gain[:, :], io["mh_norm_g_2"].partition_broadcast(P)).then_inc(bias_in, 16)
                weights.load(sp, *halves)
                for t in range(NT):
                    sp.wait_ge(gated, NT + t + 1)
                    sp.dma_start(og_t[t], og[:, t, :]).then_inc(out, 16)
                sp.wait_ge(out, 16 * NT)

            @block.gpsimd
            def _(pool):
                weights.take_los(pool, chunks)

            @block.tensor
            def _(pe):
                for g in matmul_groups(pe, weights, hT, ps, NB, span):
                    pass

            @block.scalar
            def _(act):
                gates = 0
                weights.before(act, span.start)
                for g in span:
                    i, kind, a, wd, t = groups[g]
                    if g + 1 < span.stop:
                        weights.before(act, g + 1)
                    if (i - GATE_PANELS[0]) % 2 == 0:
                        act.wait_ge(done, g + 1)
                        act.wait_ge(freed, g)
                        n = (i - GATE_PANELS[0]) // 2
                        nc.scalar.activation(og[:, t, n * BANK:(n + 1) * BANK], ps[:, g % NB, :],
                                             ACT.Sigmoid).then_inc(freed, 1)
                    else:
                        gates += 1
                        act.wait_ge(freed, g + 1)
                        nc.scalar.activation(ga[:, g % NB, :], ga[:, g % NB, :], ACT.Sigmoid).then_inc(gate_ready, 1)

            @block.vector
            def _(dve):
                dve.wait_ge(bias_in, 32)
                gates = 0
                for g in span:
                    i, kind, a, wd, t = groups[g]
                    if (i - GATE_PANELS[0]) % 2 == 0:
                        continue
                    n = (i - GATE_PANELS[0]) // 2
                    dve.wait_ge(done, g + 1)
                    dve.wait_ge(freed, g)
                    nc.vector.tensor_tensor(ga[:, g % NB, :], ps[:, g % NB, :], gbias[:, n * BANK:(n + 1) * BANK],
                                            ALU.add).then_inc(freed, 1)
                    gates += 1
                    dve.wait_ge(gate_ready, gates)
                    oo = og[:, t, n * BANK:(n + 1) * BANK]
                    c.vstep(dve, nc.vector.tensor_tensor(oo, oo, ga[:, g % NB, :], ALU.mult))
                    nc.vector.tensor_tensor(oo, oo, gain[:, n * BANK:(n + 1) * BANK], ALU.mult).then_inc(gated, 1)


R_I, R_F, R_B, R_A = range(4)
R_WS, R_T, R_FLOOR = R_I, R_A, R_B
C_A, C_FLOOR, C_WS = range(3)


def project_qkv(c, weights, hT, qk_dram, v_dram, maxima, carry, cols, decay):
    nc, io = c.nc, c.io
    w = io["w_in_2"]
    groups = weights.groups
    span, halves, chunks_ = weights.part(*QKV_PANELS)
    g0 = span.start
    n_v = g0 + 2 * NT
    NB, NSUB, TAPS = 4, 2 * D // P, 4
    v_rows = v_dram.rearrange("(t p) d -> t p d", p=P)
    with ExitStack() as s:
        rows = s.enter_context(nc.sbuf_tensor("ml_rows", [MH, 4, S], F32))
        m = s.enter_context(nc.sbuf_tensor("ml_m", [MH, NT + 1], F32))
        dec = s.enter_context(nc.sbuf_tensor("ml_decay", [MH, NT], F32))
        v_sb = s.enter_context(nc.sbuf_tensor("qkv_v", [P, 2, BANK], F32))
        z = s.enter_context(nc.sbuf_tensor("qk_z", [P, 2, S + 3], F32))
        y = s.enter_context(nc.sbuf_tensor("qk_y", [P, 2, S], F32))
        cw = s.enter_context(nc.sbuf_tensor("qk_taps", [P, TAPS, NSUB], F32))
        cb = s.enter_context(nc.sbuf_tensor("qk_bias", [P, NSUB], F32))
        wif = s.enter_context(nc.sbuf_tensor("w_if", [P, KC, 36], F32))
        wif_split = Split(nc, s, "w_if", [P, KC, 36])
        bif = s.enter_context(nc.sbuf_tensor("b_if", [36, 1], F32))
        ps = s.enter_context(nc.psum_tensor("qkv_ps", [P, NB, BANK], F32))
        pif = s.enter_context(nc.psum_tensor("if_ps", [P, 2, BANK], F32))
        pc = s.enter_context(nc.psum_tensor("ml_pc", [P, NT, 3, MH], F32))
        pd = s.enter_context(nc.psum_tensor("ml_pd", [P, MH, NT], F32))
        small_in, if_in, wif_ready = c.sem("qkv_small_in"), c.sem("if_in"), c.sem("wif_ready")
        done, freed, if_done = weights.done, weights.freed, c.sem("if_done")
        pads, conv_ready, silu_done = c.sem("qk_pads"), c.sem("qk_conv_ready"), c.sem("qk_silu_done")
        qk_out, v_out = [c.sem(f"qk2_out{b}") for b in range(2)], [c.sem(f"v2_out{b}") for b in range(2)]
        absd, expd, lnd = c.sem("ml_absd"), c.sem("ml_expd"), c.sem("ml_lnd")
        diffs, row_weights, turned = c.sem("ml_diffs"), c.sem("ml_weights"), c.sem("ml_turned")

        def by_chunk(r):
            return r.rearrange("p (c n) -> p c n", c=NT)

        with nc.Block() as block:
            @block.sync
            def _(sp):
                weights.load(sp, *halves)

            @block.gpsimd
            def _(pool):
                nc.gpsimd.memset(wif[:, :, :], 0.0).then_inc(wif_ready, 1)
                pool.wait_ge(wif_ready, 1)
                for k in range(2):
                    at = IF_AT + 4 * k
                    with nc.allow_non_contiguous_dma(reason="8 columns, once"):
                        pool.dma_start(wif[:, :, 32 * k:32 * k + 4], by_rows(w, at, at + 4)).then_inc(if_in, 16)
                        pool.dma_start(bif[32 * k:32 * k + 4, :],
                                       io["b_if_2"][4 * k:4 * k + 4].rearrange("(h o) -> h o", o=1)).then_inc(if_in, 16)
                with nc.allow_non_contiguous_dma(reason="the taps, once"):
                    for j in range(TAPS):
                        pool.dma_start(cw[:, j, :].unsqueeze(2), io["conv_w_2"][j].rearrange("(k p o) -> p k o", p=P, o=1)
                                       ).then_inc(small_in, 16)
                    pool.dma_start(cb[:, :].unsqueeze(2), io["conv_b_2"].rearrange("(k p o) -> p k o", p=P, o=1)
                                   ).then_inc(small_in, 16)
                pool.wait_ge(if_in, 64)
                nc.gpsimd.tensor_copy(wif_split.hi[:, :, :], wif[:, :, :]).then_inc(wif_ready, 1)
                pool.wait_ge(wif_ready, 2)
                nc.gpsimd.tensor_tensor(wif_split.lo[:, :, :], wif[:, :, :], wif_split.hi[:, :, :].bitcast(F32),
                                        ALU.subtract).then_inc(wif_ready, 1)
                weights.take_los(pool, chunks_)

            @block.tensor
            def _(pe):
                for g in matmul_groups(pe, weights, hT, ps, NB, span):
                    if g == g0:
                        pe.wait_ge(wif_ready, 3)
                        for half in range(2):
                            sl = slice(half * BANK, (half + 1) * BANK)
                            for k in range(KC):
                                ins = products(pe, pif[0:36, half, :], (wif_split.hi[:, k, :], wif_split.lo[:, k, :]),
                                               (hT.hi[:, k, sl], hT.lo[:, k, sl]), k == 0, k == KC - 1)
                        ins.then_inc(if_done, 1)
                    if g == n_v:
                        pe.wait_ge(row_weights, 1)
                        for t in range(NT):
                            for n, r in enumerate((R_A, R_FLOOR, R_WS)):
                                pe.transpose(pc[:, t, n, :], rows[:, r, t * P:(t + 1) * P],
                                             c.const("ident")[0:MH, 0:MH])
                        for h in range(MH):
                            ins = pe.matmul(pd[:, h, :], c.const("sel")[0:MH, h * P:(h + 1) * P], dec[:, :],
                                            start=True, stop=True)
                        ins.then_inc(turned, 1)

            @block.scalar
            def _(act):
                def silu(j):
                    act.wait_ge(conv_ready, j + 1)
                    nc.scalar.activation(y[:, j % 2, :], y[:, j % 2, :], ACT.Silu, bias=cb[:, j:j + 1]
                                         ).then_inc(silu_done, 1)
                    act.wait_ge(silu_done, j + 1)
                    act.dma_start(qk_dram[j], y[:, j % 2, :]).then_inc(qk_out[j % 2], 16)

                def row_step(g):
                    if g == g0 + 2:
                        act.wait_ge(absd, 1)
                        nc.scalar.activation(rows[:, R_T, :], rows[:, R_T, :], ACT.Exp, scale=-1.0).then_inc(expd, 1)
                    if g == g0 + 3:
                        act.wait_ge(absd, 2)
                        nc.scalar.activation(rows[:, R_T, :], rows[:, R_T, :], ACT.Ln).then_inc(lnd, 1)
                    if g == g0 + 10:
                        act.wait_ge(diffs, 1)
                        nc.scalar.activation(carry[:, :], carry[:, :], ACT.Exp)
                        for r in (R_FLOOR, R_WS):
                            nc.scalar.activation(rows[:, r, :], rows[:, r, :], ACT.Exp)
                        nc.scalar.activation(dec[:, :], dec[:, :], ACT.Exp).then_inc(row_weights, 1)

                weights.before(act, g0)
                for g in span:
                    i, kind, a, wd, t = groups[g]
                    if g + 1 < span.stop:
                        weights.before(act, g + 1)
                    act.wait_ge(done, g + 1)
                    if g < n_v:
                        n, slot = i % 2, g % 2
                        if g >= g0 + 2:
                            act.wait_ge(v_out[slot], 16 * ((g - g0) // 2))
                        nc.scalar.activation(v_sb[:, slot, :], ps[:, g % NB, :], ACT.Copy).then_inc(freed, 1)
                        act.wait_ge(freed, g + 1)
                        act.dma_start(v_rows[t, :, n * BANK:(n + 1) * BANK], v_sb[:, slot, :]).then_inc(v_out[slot], 16)
                        row_step(g)
                    else:
                        j, half = divmod(g - n_v, 2)
                        if g == n_v:
                            act.wait_ge(small_in, 16 * (TAPS + 1))
                            act.wait_ge(pads, 1)
                        if j >= 2:
                            act.wait_ge(conv_ready, j - 1)
                        nc.scalar.activation(z[:, j % 2, 3 + half * BANK:3 + (half + 1) * BANK], ps[:, g % NB, :],
                                             ACT.Copy).then_inc(freed, 1)
                        if half == 1 and j >= 1:
                            silu(j - 1)
                silu(NSUB - 1)
                for b in range(2):
                    act.wait_ge(v_out[b], 16 * NT)
                    act.wait_ge(qk_out[b], 16 * NSUB // 2)

            @block.vector
            def _(dve):
                nc.vector.memset(z[:, :, 0:3], 0.0).then_inc(pads, 1)
                dve.wait_ge(small_in, 16 * (TAPS + 1))
                dve.wait_ge(if_done, 1)
                nc.vector.tensor_scalar(rows[:, R_I, :], pif[0:MH, :, :].rearrange("p a n -> p (a n)"), bif[0:MH, :],
                                        None, ALU.add)
                c.vstep(dve, nc.vector.tensor_scalar(rows[:, R_F, :], pif[32:32 + MH, :, :].rearrange("p a n -> p (a n)"),
                                                     bif[32:32 + MH, :], None, ALU.add))
                nc.vector.scalar_tensor_tensor(rows[:, R_T, :], rows[:, R_F, :], -1.0, rows[:, R_F, :],
                                               ALU.mult, ALU.max).then_inc(absd, 1)
                dve.wait_ge(expd, 1)
                nc.vector.tensor_scalar(rows[:, R_T, :], rows[:, R_T, :], 1.0, None, ALU.add).then_inc(absd, 1)
                dve.wait_ge(lnd, 1)
                c.vstep(dve, nc.vector.scalar_tensor_tensor(rows[:, R_F, :], rows[:, R_F, :], 0.0, rows[:, R_T, :],
                                                            ALU.min, ALU.subtract))
                one = c.const("ones")[0:MH, :]
                for t in range(NT):
                    sl = slice(t * P, (t + 1) * P)
                    ins = nc.vector.tensor_tensor_scan(rows[:, R_B, sl], one, rows[:, R_F, sl], 0.0, ALU.mult, ALU.add)
                c.vstep(dve, ins)
                nc.vector.memset(m[:, 0:1], 0.0)
                c.vstep(dve, nc.vector.tensor_tensor(rows[:, R_A, :], rows[:, R_I, :], rows[:, R_B, :], ALU.subtract))
                for t in range(NT):
                    sl = slice(t * P, (t + 1) * P)
                    last = slice((t + 1) * P - 1, (t + 1) * P)
                    c.vstep(dve, nc.vector.tensor_tensor_scan(maxima[:, sl], one, rows[:, R_A, sl], m[:, t:t + 1],
                                                              ALU.mult, ALU.max))
                    c.vstep(dve, nc.vector.tensor_tensor(m[:, t + 1:t + 2], rows[:, R_B, last], maxima[:, last],
                                                         ALU.add))
                before = m[:, 0:NT]
                final = by_chunk(maxima[:, :])[:, :, P - 1]
                nc.vector.tensor_tensor(by_chunk(carry[:, :]), before.unsqueeze(2).to_broadcast([MH, NT, P]),
                                        by_chunk(maxima[:, :]), ALU.subtract)
                nc.vector.tensor_tensor(by_chunk(rows[:, R_WS, :]), by_chunk(rows[:, R_A, :]),
                                        final.unsqueeze(2).to_broadcast([MH, NT, P]), ALU.subtract)
                nc.vector.tensor_tensor(dec[:, :], before, final, ALU.subtract)
                c.vstep(dve, nc.vector.tensor_tensor(rows[:, R_FLOOR, :], rows[:, R_B, :], maxima[:, :], ALU.add))
                nc.vector.tensor_scalar(rows[:, R_FLOOR, :], rows[:, R_FLOOR, :], -1.0, None, ALU.mult).then_inc(diffs, 1)
                for j in range(NSUB):
                    dve.wait_ge(freed, n_v + 2 * (j + 1))
                    if j >= 2:
                        dve.wait_ge(qk_out[j % 2], 16 * (j // 2))
                    zz, yy = z[:, j % 2, :], y[:, j % 2, :]
                    c.vstep(dve, nc.vector.tensor_scalar(yy, zz[:, 0:S], cw[:, 0, j:j + 1], None, ALU.mult))
                    for tap in range(1, TAPS):
                        ins = nc.vector.scalar_tensor_tensor(yy, zz[:, tap:tap + S], cw[:, tap, j:j + 1], yy,
                                                             ALU.mult, ALU.add)
                        if tap < TAPS - 1:
                            c.vstep(dve, ins)
                    ins.then_inc(conv_ready, 1)
                dve.wait_ge(turned, 1)
                nc.vector.tensor_copy(cols[:, :, C_A:C_FLOOR + 1, :], pc[:, :, C_A:C_FLOOR + 1, :])
                nc.vector.tensor_scalar(cols[:, :, C_WS, :], pc[:, :, C_WS, :], MD ** -0.5, None, ALU.mult)
                c.vstep(dve, nc.vector.tensor_copy(decay[:, :, :], pd[:, :, :]))


def mlstm(c, qk_dram, v_dram, maxima, carry, cols, decay, og_dram, yb_dram, mT, next_weights):
    nc, io = c.nc, c.io
    og_t, yb_t = og_dram.rearrange("(t p) d -> t p d", p=P), yb_dram.rearrange("(t p) d -> t p d", p=P)
    R = MD ** -0.5
    with ExitStack() as s:
        e = s.enter_context(nc.sbuf_tensor("ml_e", [P, MH, P], F32))
        se = s.enter_context(nc.sbuf_tensor("ml_se", [P, 2, MH, P], F32))
        st = s.enter_context(nc.sbuf_tensor("ml_state", [P, MH, 2, MV], F32))
        qk = s.enter_context(nc.sbuf_tensor("ml_qk", [P, 3, 2 * KC, P], F32))
        qs = s.enter_context(nc.sbuf_tensor("ml_qs", [P, 2, KC, P], F32))
        v = s.enter_context(nc.sbuf_tensor("ml_v", [P, 2, MH, MV], F32))
        hh = s.enter_context(nc.sbuf_tensor("ml_hh", [P, 2, D], F32))
        kn = s.enter_context(nc.sbuf_tensor("ml_kn", [P, D], F32))
        sq = s.enter_context(nc.sbuf_tensor("ml_sq", [P, MD], F32))
        den = s.enter_context(nc.sbuf_tensor("ml_den", [P, 2], F32))
        ss = s.enter_context(nc.sbuf_tensor("ml_ss", [P, 3, MH], F32))
        eps = s.enter_context(nc.sbuf_tensor("ml_eps", [P, 1], F32))
        og = s.enter_context(nc.sbuf_tensor("ml_og", [P, 2, D], F32))
        yb = s.enter_context(nc.sbuf_tensor("ml_yb", [P, D], F32))
        p_a = s.enter_context(nc.psum_tensor("ml_p_a", [P, MH, P], F32))
        p_s = s.enter_context(nc.psum_tensor("ml_p_s", [P, MH, P], F32))
        p_n = s.enter_context(nc.psum_tensor("ml_p_n", [P, 2, BANK], F32))
        p_t = s.enter_context(nc.psum_tensor("ml_p_t", [P, D], F32))
        p_c = s.enter_context(nc.psum_tensor("ml_p_c", [P, 2, BANK], F32))
        qk_in, v_in = [c.sem(f"ml_qk_in{b}") for b in range(3)], [c.sem(f"ml_v_in{b}") for b in range(2)]
        og_in, yb_in = [c.sem(f"ml_og_in{b}") for b in range(2)], c.sem("ml_yb_in")
        start = c.sem("ml_start")
        max_bc, carry_bc, s_done, k_turned = c.sem("ml_max_bc"), c.sem("ml_carry_bc"), c.sem("ml_s_done"), c.sem("ml_k_turned")
        n_done, c_done, m_turned = c.sem("ml_n_done"), c.sem("ml_c_done"), c.sem("ml_m_turned")
        e_pre, e_exp, se_ready = c.sem("ml_e_pre"), c.sem("ml_e_exp"), c.sem("ml_se_ready")
        kn_ready, q_scaled = c.sem("ml_kn_ready"), c.sem("ml_q_scaled")
        h_ready, c_ready = c.sem("ml_h_ready"), c.sem("ml_c_ready")
        rstd_ready, rows_scaled = c.sem("ml_rstd_ready"), c.sem("ml_rows_scaled")
        rms_ready, m_ready, m_kept = c.sem("ml_rms"), c.sem("ml_m_ready"), c.sem("ml_m_kept")
        with nc.Block() as block:
            @block.sync
            def _(sp):
                for t in range(NT + 1):
                    if t < NT:
                        if t >= 3:
                            sp.wait_ge(c_done, MH * (t - 2))
                        sp.dma_start(qk[:, t % 3, :, :], qk_dram[:, :, t * P:(t + 1) * P].rearrange("j p n -> p j n")
                                     ).then_inc(qk_in[t % 3], 16)
                    if t == 2:
                        next_weights.load(sp, 0, 2)
                    if t == NT - 1:
                        next_weights.load(sp, 2)
                    u = t - 1
                    if u >= 0:
                        if u >= 2:
                            sp.wait_ge(c_done, MH * (u - 1))
                        sp.dma_start(v[:, u % 2, :, 0:MD], v_dram[u * P:(u + 1) * P, :].rearrange("p (h d) -> p h d", h=MH)
                                     ).then_inc(v_in[u % 2], 16)

            @block.gpsimd
            def _(pool):
                ready = 0
                for t in range(2):
                    pool.dma_start(og[:, t, :], og_t[t]).then_inc(og_in[t], 16)
                pool.dma_start(yb[:, :], yb_t[0]).then_inc(yb_in, 16)
                for t in range(NT):
                    m = hh[:, t % 2, :]
                    pool.wait_ge(rows_scaled, t + 1)
                    pool.wait_ge(og_in[t % 2], 16 * (t // 2 + 1))
                    c.gstep(pool, nc.gpsimd.tensor_tensor(m, m, og[:, t % 2, :], ALU.mult))
                    pool.wait_ge(yb_in, 16 * (t + 1))
                    nc.gpsimd.tensor_tensor(m, m, yb[:, :], ALU.add).then_inc(m_ready, 1)
                    if t + 1 < NT:
                        pool.wait_ge(m_ready, t + 1)
                        pool.dma_start(yb[:, :], yb_t[t + 1]).then_inc(yb_in, 16)
                    if t + 2 < NT:
                        pool.dma_start(og[:, t % 2, :], og_t[t + 2]).then_inc(og_in[t % 2], 16)
                    upto = next_weights.pre * (t + 1) // NT
                    next_weights.prepare(pool, ready, upto)
                    ready = upto

            @block.tensor
            def _(pe):
                def spread(rows, t):
                    for h in range(MH):
                        ins = pe.matmul(p_a[:, h, :], c.const("sel")[0:MH, h * P:(h + 1) * P],
                                        rows[:, t * P:(t + 1) * P], start=True, stop=True)
                    return ins

                def scores(t):
                    if t >= 1:
                        pe.wait_ge(q_scaled, t)
                    spread(maxima, t).then_inc(max_bc, 1)
                    if t >= 1:
                        pe.wait_ge(se_ready, t)
                    pe.wait_ge(qk_in[t % 3], 16 * (t // 3 + 1))
                    for h in range(MH):
                        for k in range(2):
                            ins = pe.matmul(p_s[:, h, :], qk[:, t % 3, KC + 2 * h + k, :], qk[:, t % 3, 2 * h + k, :],
                                            start=(k == 0), stop=(k == 1))
                    ins.then_inc(s_done, 1)

                def spread_carry(t):
                    pe.wait_ge(e_pre, t + 1)
                    spread(carry, t).then_inc(carry_bc, 1)

                def turn_keys(t):
                    if t >= 2:
                        pe.wait_ge(m_kept, t - 1)
                    for j in range(KC):
                        ins = pe.transpose(p_t[:, j * P:(j + 1) * P], qk[:, t % 3, KC + j, :], c.const("ident"))
                    ins.then_inc(k_turned, 1)

                def turn_mixed(t, keys):
                    pe.wait_ge(m_ready, t + 1)
                    pe.wait_ge(kn_ready, keys)
                    for j in range(KC):
                        ins = pe.transpose(p_t[:, j * P:(j + 1) * P], hh[:, t % 2, j * P:(j + 1) * P], c.const("ident"))
                    ins.then_inc(m_turned, 1)

                pe.wait_ge(start, 1)
                scores(0)
                spread_carry(0)
                turn_keys(0)
                for t in range(NT):
                    if t + 1 < NT:
                        scores(t + 1)
                    if t >= 1:
                        turn_keys(t)
                    pe.wait_ge(se_ready, t + 1)
                    pe.wait_ge(q_scaled, t + 1)
                    pe.wait_ge(v_in[t % 2], 16 * (t // 2 + 1))
                    for h in range(MH):
                        u = MH * t + h
                        if u >= 2:
                            pe.wait_ge(h_ready, u - 1)
                        pe.matmul(p_n[:, u % 2, 0:MV], se[:, t % 2, h, :], v[:, t % 2, h, :], start=True, stop=False)
                        if t >= 1:
                            pe.wait_ge(c_ready, u - MH + 1)
                        for k in range(2):
                            ins = pe.matmul(p_n[:, u % 2, 0:MV], qs[:, t % 2, 2 * h + k, :], st[:, h, k, :],
                                            start=False, stop=(k == 1))
                        ins.then_inc(n_done, 1)
                        pe.wait_ge(kn_ready, t + 1)
                        if u >= 1:
                            pe.wait_ge(c_ready, u)
                        for k in range(2):
                            ins = pe.matmul(p_c[:, k, 0:MV], kn[:, (2 * h + k) * P:(2 * h + k + 1) * P],
                                            v[:, t % 2, h, :], start=True, stop=True)
                        ins.then_inc(c_done, 1)
                        if h == 1 and t + 1 < NT:
                            spread_carry(t + 1)
                    if t >= 1:
                        turn_mixed(t - 1, t + 1)
                pe.wait_ge(m_kept, NT - 1)
                turn_mixed(NT - 1, NT)

            @block.vector
            def _(dve):
                def gaps(t):
                    dve.wait_ge(max_bc, t + 1)
                    for h in range(MH):
                        ins = nc.vector.tensor_scalar(e[:, h, :], p_a[:, h, :], cols[:, t, C_A, h:h + 1], 0.0,
                                                      ALU.subtract, ALU.max)
                    ins.then_inc(e_pre, 1)

                def weigh(t):
                    dve.wait_ge(e_exp, t + 1)
                    c.vstep(dve, nc.vector.scalar_tensor_tensor(
                        e[:, :, :], e[:, :, :], R, c.const("causal").unsqueeze(1).to_broadcast([P, MH, P]),
                        ALU.mult, ALU.mult))
                    dve.wait_ge(s_done, t + 1)
                    if t >= 2:
                        dve.wait_ge(n_done, MH * (t - 1))
                    nc.vector.tensor_tensor(se[:, t % 2, :, :], e[:, :, :], p_s[:, :, :], ALU.mult).then_inc(se_ready, 1)
                    dve.wait_ge(se_ready, t + 1)

                def scale_queries(t):
                    dve.wait_ge(carry_bc, t + 1)
                    if t >= 2:
                        dve.wait_ge(n_done, MH * (t - 1))
                    nc.vector.tensor_tensor(qs[:, t % 2, :, :].rearrange("p (h k) n -> p h k n", k=2),
                                            qk[:, t % 3, 0:KC, :].rearrange("p (h k) n -> p h k n", k=2),
                                            p_a[:, :, :].unsqueeze(2).to_broadcast([P, MH, 2, P]),
                                            ALU.mult).then_inc(q_scaled, 1)

                def head(t, h):
                    u = MH * t + h
                    dve.wait_ge(n_done, u + 1)
                    n = p_n[:, u % 2, :]
                    if u >= 1:
                        dve.wait_ge(h_ready, u)
                    c.vstep(dve, nc.vector.tensor_scalar(den[:, 0:1], n[:, MD:MV], -1.0, cols[:, t, C_FLOOR, h:h + 1],
                                                         ALU.mult, ALU.max))
                    c.vstep(dve, nc.vector.tensor_tensor(den[:, 0:1], n[:, MD:MV], den[:, 0:1], ALU.max))
                    c.vstep(dve, nc.vector.reciprocal(den[:, 1:2], den[:, 0:1]))
                    if t >= 2 and h == 0:
                        dve.wait_ge(m_turned, t - 1)
                    nc.vector.tensor_scalar(hh[:, t % 2, h * MD:(h + 1) * MD], n[:, 0:MD], den[:, 1:2], None, ALU.mult
                                            ).then_inc(h_ready, 1)
                    dve.wait_ge(c_done, u + 1)
                    sh = st[:, h, :, :]
                    nc.vector.scalar_tensor_tensor(sh, sh, decay[:, h, t:t + 1], p_c[:, :, 0:MV], ALU.mult, ALU.add
                                                   ).then_inc(c_ready, 1)

                def invert_rms(t):
                    dve.wait_ge(rms_ready, t + 1)
                    if t >= 1:
                        dve.wait_ge(rows_scaled, t)
                    nc.vector.reciprocal(ss[:, 2, :], ss[:, 1, :]).then_inc(rstd_ready, 1)

                nc.vector.memset(eps[:, :], EPS)
                nc.vector.memset(v[:, :, :, MD:MV], 1.0)
                nc.vector.memset(st[:, :, :, :], 0.0).then_inc(start, 1)
                dve.wait_ge(start, 1)
                gaps(0)
                weigh(0)
                scale_queries(0)
                for t in range(NT):
                    if t + 1 < NT:
                        gaps(t + 1)
                    if t >= 1:
                        invert_rms(t - 1)
                    head(t, 0)
                    head(t, 1)
                    if t + 1 < NT:
                        weigh(t + 1)
                    head(t, 2)
                    if t + 1 < NT:
                        scale_queries(t + 1)
                    head(t, 3)
                invert_rms(NT - 1)

            @block.scalar
            def _(act):
                def exps(t):
                    act.wait_ge(e_pre, t + 1)
                    nc.scalar.activation(e[:, :, :], e[:, :, :], ACT.Exp, scale=-1.0).then_inc(e_exp, 1)

                def keys(t):
                    act.wait_ge(k_turned, t + 1)
                    if t >= 1:
                        act.wait_ge(c_done, MH * t)
                    for h in range(MH):
                        ins = nc.scalar.activation(kn[:, h * MD:(h + 1) * MD], p_t[:, h * MD:(h + 1) * MD],
                                                   ACT.Copy, scale=cols[:, t, C_WS, h:h + 1])
                    ins.then_inc(kn_ready, 1)

                def scale_rows(t):
                    act.wait_ge(rstd_ready, t + 1)
                    for h in range(MH):
                        rows = hh[:, t % 2, h * MD:(h + 1) * MD]
                        ins = nc.scalar.activation(rows, rows, ACT.Copy, scale=ss[:, 2, h:h + 1])
                    ins.then_inc(rows_scaled, 1)

                def keep_mixed(t):
                    act.wait_ge(m_turned, t + 1)
                    nc.scalar.activation(mT[:, :, t * P:(t + 1) * P], p_t[:, :].rearrange("p (k n) -> p k n", k=KC),
                                         ACT.Copy).then_inc(m_kept, 1)

                act.wait_ge(start, 1)
                exps(0)
                keys(0)
                for t in range(NT):
                    if t + 1 < NT:
                        exps(t + 1)
                    if t >= 1:
                        keys(t)
                        scale_rows(t - 1)
                    for h in range(MH):
                        act.wait_ge(h_ready, MH * t + h + 1)
                        if h == 0 and t >= 1:
                            act.wait_ge(rms_ready, t)
                        c.astep(act, nc.scalar.activation(sq[:, :], hh[:, t % 2, h * MD:(h + 1) * MD], ACT.Square,
                                                          accum_out=ss[:, 0, h:h + 1]))
                    if t >= 1:
                        act.wait_ge(rstd_ready, t)
                    nc.scalar.activation(ss[:, 1, :], ss[:, 0, :], ACT.Sqrt, scale=1.0 / MD, bias=eps[:, :]
                                         ).then_inc(rms_ready, 1)
                    if t >= 1:
                        keep_mixed(t - 1)
                scale_rows(NT - 1)
                keep_mixed(NT - 1)


def second_mixer(c, x1, x2, og, yb, qk_dram, v_dram):
    nc, io = c.nc, c.io
    with ExitStack() as s:
        maxima = s.enter_context(nc.sbuf_tensor("ml_maxima", [MH, S], F32))
        carry = s.enter_context(nc.sbuf_tensor("ml_carry", [MH, S], F32))
        cols = s.enter_context(nc.sbuf_tensor("ml_cols", [P, NT, 3, MH], F32))
        decay = s.enter_context(nc.sbuf_tensor("ml_decays", [P, MH, NT], F32))
        with ExitStack() as s2:
            weights = mixer_weights(c, s2)
            hT = Split(nc, s2, "h2T", [P, KC, S])
            norm_transposed(c, "n2", x1, io["norm_mix_g_2"], hT, next_weights=weights)
            spatial_gate(c, weights, hT, yb)
            output_gate(c, weights, hT, og)
            project_qkv(c, weights, hT, qk_dram, v_dram, maxima, carry, cols, decay)
        mT = s.enter_context(nc.sbuf_tensor("m2T", [P, KC, S], F32))
        weights = out_weights(c, s, "o2", io["w_out_2"])
        mlstm(c, qk_dram, v_dram, maxima, carry, cols, decay, og, yb, mT, weights)
        project_out(c, "o2", weights, mT, x1, x2)


def memory_weights(c, stack):
    wq, wkv = c.io["w_xq_2"], c.io["w_xkv_2"]
    sources, groups = [], []
    for n in range(D // BANK):
        groups += [(len(sources), "cols", sub * P, NMEM, 0) for sub in range(BANK // P)]
        sources.append(([by_rows(wkv, n * BANK, (n + 1) * BANK)], BANK))
    for n in range(D // BANK):
        groups += [(len(sources), "rows", 0, BANK, t) for t in range(NMEM // P)]
        sources.append(([by_rows(wkv, D + n * BANK, D + (n + 1) * BANK)], BANK))
    for n in range(D // BANK):
        groups += [(len(sources), "cols", sub * P, BANK, half) for sub in range(BANK // P) for half in range(2)]
        sources.append(([by_rows(wq, n * BANK, (n + 1) * BANK)], BANK))
    return Weights(c, stack, "p3", sources, groups, side="right")


def memory_projections(c, weights, xT, mnT, qT, kT, v, y_slots=None):
    nc = c.nc
    keep = []
    for i, kind, a, wd, t in weights.groups:
        panel_of = i % 2
        if i < 2:
            keep.append((kT[:, 4 * panel_of + a // P, :], NMEM))
        elif i < 4:
            keep.append((v[:, t, panel_of * BANK:(panel_of + 1) * BANK], BANK))
        else:
            keep.append((qT[:, 4 * panel_of + a // P, t * BANK:(t + 1) * BANK], BANK))
    of_memory = 4
    NB = 4
    with ExitStack() as s:
        zero = s.enter_context(nc.sbuf_tensor("xp_zero", [P, D], F32))
        ps = s.enter_context(nc.psum_tensor("xp_ps", [P, NB, BANK], F32))
        done, freed = weights.done, weights.freed
        zero_ready, cleared = c.sem("xp_zero_ready"), c.sem("xp_cleared")
        with nc.Block() as block:
            @block.gpsimd
            def _(pool):
                weights.take_los(pool)
                nc.gpsimd.memset(zero[:, :], 0.0).then_inc(zero_ready, 1)
                pool.wait_ge(zero_ready, 1)
                if y_slots is not None:
                    for b in range(2 * S // P, NBLK):
                        pool.dma_start(y_slots[b * P:(b + 1) * P, :], zero[:, :]).then_inc(cleared, 16)
                    pool.wait_ge(cleared, 16 * NE)

            @block.sync
            def _(sp):
                weights.load(sp, 2)

            @block.tensor
            def _(pe):
                for g in matmul_groups(pe, weights, lambda i: mnT if i < of_memory else xT, ps, NB):
                    pass

            @block.scalar
            def _(act):
                weights.before(act, 0)
                for g, (dst, n) in enumerate(keep):
                    weights.before(act, g + 1)
                    act.wait_ge(done, g + 1)
                    nc.scalar.activation(dst, ps[:, g % NB, 0:n], ACT.Copy).then_inc(freed, 1)


def memory_attention(c, qT, kT, v, oT, next_weights):
    nc = c.nc
    steps = [(h, half, t) for h in range(4) for half in range(2) for t in range(4)]
    N, R = len(steps), MD ** -0.5
    with ExitStack() as s:
        pr = s.enter_context(nc.sbuf_tensor("xa_p", [P, 3, NMEM], F32))
        pT = s.enter_context(nc.sbuf_tensor("xa_pT", [P, 2, 2, BANK], F32))
        mx = s.enter_context(nc.sbuf_tensor("xa_max", [P, 4, N], F32))
        ps = s.enter_context(nc.psum_tensor("xa_ps", [P, 3, BANK], F32))
        pt = s.enter_context(nc.psum_tensor("xa_pt", [P, 2, BANK], F32))
        po = s.enter_context(nc.psum_tensor("xa_po", [P, 2, BANK], F32))
        scored, maxed, expd, normed = (c.sem(f"xa_{n}") for n in ("scored", "maxed", "expd", "normed"))
        turned, kept, summed, out_kept = (c.sem(f"xa_{n}") for n in ("turned", "kept", "summed", "out_kept"))
        with nc.Block() as block:
            @block.sync
            def _(sp):
                next_weights.load(sp)

            @block.gpsimd
            def _(pool):
                next_weights.prepare(pool)

            @block.tensor
            def _(pe):
                def scores(i):
                    h, half, t = steps[i]
                    if i >= 3:
                        pe.wait_ge(expd, i - 2)
                    at = (4 * half + t) * P
                    for k in range(2):
                        ins = pe.matmul(ps[:, i % 3, 0:NMEM], qT[:, 2 * h + k, at:at + P], kT[:, 2 * h + k, :],
                                        start=(k == 0), stop=(k == 1))
                    ins.then_inc(scored, 1)

                def turn(i):
                    pe.wait_ge(normed, i + 1)
                    if i >= 2:
                        pe.wait_ge(kept, i - 1)
                    for m in range(2):
                        ins = pe.transpose(pt[:, i % 2, m * P:(m + 1) * P], pr[:, i % 3, m * P:(m + 1) * P], c.const("ident"))
                    ins.then_inc(turned, 1)

                def values(q):
                    pe.wait_ge(kept, 4 * (q + 1))
                    h = q // 2
                    for e in range(2):
                        n = 2 * q + e
                        if n >= 2:
                            pe.wait_ge(out_kept, n - 1)
                        for m in range(2):
                            ins = pe.matmul(po[:, n % 2, :], v[:, m, (2 * h + e) * P:(2 * h + e + 1) * P],
                                            pT[:, q % 2, m, :], start=(m == 0), stop=(m == 1))
                        ins.then_inc(summed, 1)

                for i in range(N + 4):
                    if i < N:
                        scores(i)
                    if 2 <= i <= N + 1:
                        turn(i - 2)
                    if i >= 7 and i % 4 == 3:
                        values((i - 7) // 4)

            @block.vector
            def _(dve):
                for i in range(N + 1):
                    if i < N:
                        dve.wait_ge(scored, i + 1)
                        c.vstep(dve, nc.vector.tensor_reduce(mx[:, 0, i:i + 1], ps[:, i % 3, 0:NMEM], AX, ALU.max))
                        nc.vector.tensor_scalar(mx[:, 1, i:i + 1], mx[:, 0, i:i + 1], -R, None, ALU.mult
                                                ).then_inc(maxed, 1)
                    if i >= 1:
                        n = i - 1
                        dve.wait_ge(expd, n + 1)
                        c.vstep(dve, nc.vector.reciprocal(mx[:, 3, n:n + 1], mx[:, 2, n:n + 1]))
                        nc.vector.tensor_scalar(pr[:, n % 3, :], pr[:, n % 3, :], mx[:, 3, n:n + 1], None, ALU.mult
                                                ).then_inc(normed, 1)

            @block.scalar
            def _(act):
                def keep_out(n):
                    act.wait_ge(summed, n + 1)
                    q, e = divmod(n, 2)
                    h, half = divmod(q, 2)
                    nc.scalar.activation(oT[:, 2 * h + e, half * BANK:(half + 1) * BANK], po[:, n % 2, :], ACT.Copy
                                         ).then_inc(out_kept, 1)

                for i in range(N + 4):
                    if i < N:
                        act.wait_ge(maxed, i + 1)
                        if i >= 3:
                            act.wait_ge(turned, i - 2)
                        nc.scalar.activation(pr[:, i % 3, :], ps[:, i % 3, 0:NMEM], ACT.Exp, bias=mx[:, 1, i:i + 1],
                                             scale=R, accum_out=mx[:, 2, i:i + 1]).then_inc(expd, 1)
                    if 2 <= i <= N + 1:
                        n = i - 2
                        q, t = divmod(n, 4)
                        act.wait_ge(turned, n + 1)
                        if q >= 2:
                            act.wait_ge(summed, 2 * (q - 1))
                        nc.scalar.activation(pT[:, q % 2, :, t * P:(t + 1) * P],
                                             pt[:, n % 2, 0:2 * P].rearrange("p (m n) -> p m n", m=2), ACT.Copy
                                             ).then_inc(kept, 1)
                    if i >= 7 and i % 4 == 3:
                        keep_out((i - 7) // 4 * 2)
                        keep_out((i - 7) // 4 * 2 + 1)


def cross_attention(c, x2, x3, y_slots=None):
    nc, io = c.nc, c.io
    with ExitStack() as s:
        with ExitStack() as s2:
            weights = memory_weights(c, s2)
            hT = Split(nc, s2, "h3T", [P, KC, S], side="right")
            mnT = Split(nc, s2, "mnT", [P, KC, NMEM], side="right")
            norm_transposed(c, "nm", io["mem_2"], io["norm_mem_g_2"], mnT, n_tiles=NMEM // P)
            norm_transposed(c, "n3", x2, io["norm_x_g_2"], hT, next_weights=weights)
            qT = s.enter_context(nc.sbuf_tensor("q3T", [P, KC, S], F32))
            kT = s.enter_context(nc.sbuf_tensor("k3T", [P, KC, NMEM], F32))
            v = s.enter_context(nc.sbuf_tensor("v3", [P, NMEM // P, D], F32))
            memory_projections(c, weights, hT, mnT, qT, kT, v, y_slots)
        weights = out_weights(c, s, "o3", io["w_xo_2"])
        oT = qT
        memory_attention(c, qT, kT, v, oT, weights)
        project_out(c, "o3", weights, oT, x2, x3)


def load_router(c, sp, wr, bias, w_in):
    io = c.io
    with c.nc.allow_non_contiguous_dma(reason="36 columns, once"):
        sp.dma_start(wr[:, :, 0:NG], by_rows(io["w_rg_2"], 0, NG)).then_inc(w_in, 16)
        sp.dma_start(wr[:, :, NG:], by_rows(io["w_re_2"], 0, NE)).then_inc(w_in, 16)
    sp.dma_start(bias[:, 0:NG], io["b_rg_2"].partition_broadcast(P)).then_inc(w_in, 16)
    sp.dma_start(bias[:, NG:], io["b_re_2"].partition_broadcast(P)).then_inc(w_in, 16)


def route(c, pl, bias, expert_weights, gates, dest, slot_token, block_expert, n_blocks):
    nc = c.nc
    NR = NG + NE
    with ExitStack() as s:
        def sb(name, shape, dt=F32):
            return s.enter_context(nc.sbuf_tensor(f"rt_{name}", shape, dt))

        lg = sb("logits", [P, NT, NR])
        el, e4, e32 = sb("el", [P, NT, NE]), sb("e4", [P, NT, NG]), sb("e32", [P, NT, NE])
        oh1, oh2, oh = sb("oh1", [P, NT, NE]), sb("oh2", [P, NT, NE]), sb("oh", [P, NT, NE])
        gm, pg, idx = sb("gmax", [P, NT]), sb("pgroup", [P, NT]), sb("idx", [P, NT])
        v1, v2, r = sb("v1", [P, NT]), sb("v2", [P, NT]), sb("r", [P, NT])
        cnt_i, counts, padded, pend, start = sb("cnt_i", [P, NE], I32), sb("counts", [P, NT + 1, NE]), sb("padded", [P, NE]), sb("pend", [P, NE]), sb("start", [P, NE])
        cmp = sb("cmp", [P, NBLK, NE])
        be, nb = sb("be", [P, NBLK]), sb("nb", [P, 1])
        dest_f, lo_i, lo, hi = sb("dest_f", [P, 2, NT]), sb("lo_i", [P, 2, NT], I32), sb("lo", [P, 2, NT]), sb("hi", [P, 2, NT])
        d1, d2 = sb("d1", [P, 2 * NT, P]), sb("d2", [P, 2 * NT, NBLK])
        pk = s.enter_context(nc.psum_tensor("rt_pk", [P, 2, NT, NE], F32))
        pn = s.enter_context(nc.psum_tensor("rt_pn", [P, 2, NT, NE], F32))
        pt = s.enter_context(nc.psum_tensor("rt_pt", [P, BANK], F32))
        blocks_known = c.sem("rt_blocks_known")
        pre, expd, chosen = c.sem("rt_pre"), c.sem("rt_expd"), c.sem("rt_chosen")
        ranked, placed, tabled = c.sem("rt_ranked"), c.sem("rt_placed"), c.sem("rt_tabled")
        iota32 = c.const("iota32").rearrange("p (t e) -> p t e", t=NT)
        iota4 = iota32[:, :, 0:NG]

        def bc(x, n):
            return x.unsqueeze(2).to_broadcast([P, NT, n])

        with nc.Block() as block:
            @block.sync
            def _(sp):
                sp.wait_ge(blocks_known, 1)
                expert_weights.load(sp, 0, 0)

            @block.tensor
            def _(pe):
                pe.wait_ge(chosen, 1)
                pe.matmul(pk[:, 0, :, :], c.const("before"), oh[:, :, :], start=True, stop=True)
                pe.matmul(pn[:, 0, :, :], c.const("ones"), oh[:, :, :], start=True, stop=True).then_inc(ranked, 1)
                pe.wait_ge(placed, 1)
                for n in range(2 * NT):
                    ins = pe.matmul(pt[:, 0:NBLK], d1[:, n, :], d2[:, n, :], start=(n == 0), stop=(n == 2 * NT - 1))
                ins.then_inc(tabled, 1)

            @block.scalar
            def _(act):
                act.wait_ge(pre, 1)
                nc.scalar.activation(e4[:, :, :], e4[:, :, :], ACT.Exp).then_inc(expd, 1)
                act.wait_ge(pre, 2)
                nc.scalar.activation(v2[:, :], v2[:, :], ACT.Exp).then_inc(expd, 1)

            @block.vector
            def _(dve):
                V = nc.vector

                def step(ins):
                    c.vstep(dve, ins)

                def first_of_max(values, n, top, onehot, iota, spare):
                    step(V.tensor_reduce(top[:, :], values, AX, ALU.max))
                    step(V.tensor_tensor(spare, values, bc(top[:, :], n), ALU.is_equal))
                    step(V.scalar_tensor_tensor(spare, spare, -64.0, iota, ALU.mult, ALU.add))
                    step(V.tensor_reduce(idx[:, :], spare, AX, ALU.min))
                    step(V.tensor_scalar(idx[:, :], idx[:, :], 64.0, None, ALU.add))
                    step(V.tensor_tensor(onehot, iota, bc(idx[:, :], n), ALU.is_equal))

                step(V.tensor_tensor(lg[:, :, :], pl[:, :, 0:NR], bias[:, :].unsqueeze(1).to_broadcast([P, NT, NR]), ALU.add))
                first_of_max(lg[:, :, 0:NG], NG, gm, oh1[:, :, 0:NG], iota4, e32[:, :, 0:NG])
                V.tensor_tensor(e4[:, :, :], lg[:, :, 0:NG], bc(gm[:, :], NG), ALU.subtract).then_inc(pre, 1)
                step(V.tensor_scalar(oh1[:, :, 0:NG], oh1[:, :, 0:NG], -NEG, NEG, ALU.mult, ALU.add))
                for g in range(NG):
                    ins = V.tensor_tensor(el[:, :, g * EPG:(g + 1) * EPG], lg[:, :, NG + g * EPG:NG + (g + 1) * EPG],
                                          oh1[:, :, g:g + 1].to_broadcast([P, NT, EPG]), ALU.add)
                step(ins)
                first_of_max(el[:, :, :], NE, v1, oh1[:, :, :], iota32, e32[:, :, :])
                step(V.scalar_tensor_tensor(el[:, :, :], oh1[:, :, :], 3 * NEG, el[:, :, :], ALU.mult, ALU.add))
                first_of_max(el[:, :, :], NE, v2, oh2[:, :, :], iota32, e32[:, :, :])
                V.tensor_tensor(oh[:, :, :], oh1[:, :, :], oh2[:, :, :], ALU.add).then_inc(chosen, 1)
                V.tensor_tensor(v2[:, :], v2[:, :], v1[:, :], ALU.subtract).then_inc(pre, 1)
                dve.wait_ge(expd, 1)
                step(V.tensor_reduce(pg[:, :], e4[:, :, :], AX, ALU.add))
                step(V.reciprocal(pg[:, :], pg[:, :]))
                dve.wait_ge(expd, 2)
                step(V.tensor_scalar(r[:, :], v2[:, :], 1.0, None, ALU.add))
                step(V.reciprocal(r[:, :], r[:, :]))
                step(V.tensor_tensor(gates[:, 0, :], pg[:, :], r[:, :], ALU.mult))
                step(V.tensor_tensor(gates[:, 1, :], gates[:, 0, :], v2[:, :], ALU.mult))
                dve.wait_ge(ranked, 1)
                step(V.memset(counts[:, 0, :], 0.0))
                for t in range(NT):
                    step(V.tensor_tensor(counts[:, t + 1, :], counts[:, t, :], pn[:, 0, t, :], ALU.add))
                step(V.tensor_scalar(cnt_i[:, :], counts[:, NT, :], float(P - 1), None, ALU.add))
                step(V.tensor_scalar(cnt_i[:, :], cnt_i[:, :], 7, 7, ALU.arith_shift_right, ALU.logical_shift_left))
                step(V.tensor_copy(padded[:, :], cnt_i[:, :]))
                step(V.tensor_tensor_scan(pend[:, :], c.const("ones")[:, 0:NE], padded[:, :], 0.0, ALU.mult, ALU.add))
                step(V.tensor_tensor(start[:, :], pend[:, :], padded[:, :], ALU.subtract))
                step(V.tensor_tensor(cmp[:, :, :], pend[:, :].unsqueeze(1).to_broadcast([P, NBLK, NE]),
                                     c.const("blk").unsqueeze(2).to_broadcast([P, NBLK, NE]), ALU.is_le))
                step(V.tensor_reduce(be[:, :], cmp[:, :, :], AX, ALU.add))
                V.tensor_scalar(block_expert[:, :], be[:, :], float(NE - 1), None, ALU.min).then_inc(blocks_known, 1)
                step(V.tensor_tensor(el[:, :, :], counts[:, 0:NT, :], start[:, :].unsqueeze(1).to_broadcast([P, NT, NE]),
                                     ALU.add))
                step(V.tensor_tensor(el[:, :, :], pk[:, 0, :, :], el[:, :, :], ALU.add))
                for k, o in enumerate((oh1, oh2)):
                    step(V.tensor_tensor(e32[:, :, :], o[:, :, :], el[:, :, :], ALU.mult))
                    step(V.tensor_reduce(dest_f[:, k, :], e32[:, :, :], AX, ALU.add))
                step(V.tensor_copy(dest[:, :, :], dest_f[:, :, :]))
                step(V.tensor_copy(lo_i[:, :, :], dest_f[:, :, :]))
                step(V.tensor_scalar(lo_i[:, :, :], lo_i[:, :, :], P - 1, None, ALU.bitwise_and))
                step(V.tensor_copy(lo[:, :, :], lo_i[:, :, :]))
                step(V.tensor_tensor(hi[:, :, :], dest_f[:, :, :], lo[:, :, :], ALU.subtract))
                def spread(x, n):
                    return x[:, :, :].rearrange("p k t -> p (k t)").unsqueeze(2).to_broadcast([P, 2 * NT, n])

                V.tensor_tensor(d1[:, :, :], c.const("iota").unsqueeze(1).to_broadcast([P, 2 * NT, P]), spread(lo, P),
                                ALU.is_equal)
                step(V.tensor_tensor(d2[:, :, :], c.const("blk").unsqueeze(1).to_broadcast([P, 2 * NT, NBLK]),
                                     spread(hi, NBLK), ALU.is_equal))
                for k in range(2):
                    ins = V.tensor_tensor(d2[:, k * NT:(k + 1) * NT, :], d2[:, k * NT:(k + 1) * NT, :],
                                          c.const("tokid").unsqueeze(2).to_broadcast([P, NT, NBLK]), ALU.mult)
                ins.then_inc(placed, 1)
                step(V.tensor_scalar(nb[:, :], pend[:, NE - 1:NE], 1.0 / P, None, ALU.mult))
                V.tensor_copy(n_blocks[:, 0:1], nb[:, :])
                step(V.tensor_scalar(n_blocks[:, 1:2], nb[:, :], -1.0, None, ALU.add))
                step(V.tensor_scalar(n_blocks[:, 2:3], n_blocks[:, 1:2], 1, None, ALU.bitwise_and))
                step(V.tensor_scalar(n_blocks[:, 1:2], n_blocks[:, 1:2], 1, None, ALU.arith_shift_right))
                dve.wait_ge(tabled, 1)
                V.memset(slot_token[:, NBLK:], 0)
                step(V.tensor_copy(slot_token[:, 0:NBLK], pt[:, 0:NBLK]))


class ExpertWeights:

    def __init__(self, c, stack, block_expert):
        nc = c.nc
        self.io, self.block_expert, KF = c.io, block_expert, FF // P
        self.w1s = stack.enter_context(nc.sbuf_tensor("ex_w1", [P, 2, KC * FF], F32))
        self.w3s = stack.enter_context(nc.sbuf_tensor("ex_w3", [P, 2, KC * FF], F32))
        self.w2s = stack.enter_context(nc.sbuf_tensor("ex_w2", [P, 2, KF * D], F32))
        self.w1_in, self.w3_in, self.w2_in = ([c.sem(f"ex_{n}_in{j}") for j in range(2)] for n in ("w1", "w3", "w2"))
        self.w1 = c.io["w1_2"].rearrange("e (p k) f -> e p (k f)", k=KC)
        self.w3 = c.io["w3_2"].rearrange("e (p k) f -> e p (k f)", k=KC)
        self.w2 = c.io["w2_2"].rearrange("e (p k) d -> e p (k d)", k=KF)

    def load(self, sp, i, j, used=None):
        b = 2 * i + j
        at = slice(b, b + 1) if isinstance(b, int) else bass.ds(b, 1)
        e = sp.value_load(self.block_expert[0:1, at], min_val=0, max_val=NE - 1)
        for n, (slots, w, w_in) in enumerate(((self.w1s, self.w1, self.w1_in), (self.w3s, self.w3, self.w3_in),
                                              (self.w2s, self.w2, self.w2_in))):
            if used:
                sp.wait_ge(used[n][j], i)
            sp.dma_start(slots[:, j, :], w[bass.ds(e, 1)].rearrange("e p n -> (e p) n")).then_inc(w_in[j], 16)


def experts(c, weights, xn, y_slots, slot_token, n_blocks):
    nc = c.nc
    KF = FF // P
    y_b = y_slots.rearrange("(b p) d -> b p d", p=P)
    with ExitStack() as s:
        def sb(name, shape, dt=F32):
            return s.enter_context(nc.sbuf_tensor(f"ex_{name}", shape, dt))

        w1s, w3s, w2s = weights.w1s, weights.w3s, weights.w2s
        w1_in, w3_in, w2_in = weights.w1_in, weights.w3_in, weights.w2_in
        idx, xg, xT = sb("idx", [P, 2], I32), sb("x", [P, 2, D]), sb("xT", [P, 2, D])
        a, h, hT, y = sb("a", [P, 2, FF]), sb("h", [P, 2, FF]), sb("hT", [P, 2, FF]), sb("y", [P, 2, D])
        p_x = s.enter_context(nc.psum_tensor("ex_px", [P, D], F32))
        p_a = s.enter_context(nc.psum_tensor("ex_pa", [P, FF], F32))
        p_b = s.enter_context(nc.psum_tensor("ex_pb", [P, FF], F32))
        p_h = s.enter_context(nc.psum_tensor("ex_ph", [P, FF], F32))
        p_y = s.enter_context(nc.psum_tensor("ex_py", [P, D], F32))

        def pair(name):
            return [c.sem(f"ex_{name}{j}") for j in range(2)]

        idx_ready, x_in, x_turned, x_kept = pair("idx"), pair("x_in"), pair("x_turned"), pair("x_kept")
        a_done, b_done, a_ready, h_ready = pair("a_done"), pair("b_done"), pair("a_ready"), pair("h_ready")
        h_turned, h_kept, y_done, y_ready, y_out = (pair("h_turned"), pair("h_kept"), pair("y_done"), pair("y_ready"),
                                                    pair("y_out"))
        gathers = c.sem("ex_gathers")
        stored = c.sem("ex_stored")

        def wait(eng, sem, value):
            if not isinstance(value, int) or value > 0:
                eng.wait_ge(sem, value)

        def last(i, j):
            return (i - 1, 1) if j == 0 else (i, 0)

        def next_(i, j):
            return (i, 1) if j == 0 else (i + 1, 0)

        def upto_last(i, j):
            return i if j == 0 else i + 1

        def over_blocks(eng, body, tail=None):
            n = eng.value_load(n_blocks[0:1, 0:1], min_val=2 * S // P, max_val=NBLK)
            for j in range(2):
                body(0, j)
            with eng.Fori(1, NBLK // 2) as i:
                for j in range(2):
                    with eng.If(2 * i + j < n):
                        body(i, j)
            if tail:
                end = eng.value_load(n_blocks[0:1, 1:2], min_val=S // P - 1, max_val=NBLK // 2 - 1)
                odd = eng.value_load(n_blocks[0:1, 2:3], min_val=0, max_val=1)
                for j in range(2):
                    with eng.If(odd == j):
                        tail(end, j)
            return n

        with nc.Block() as block:
            @block.sync
            def _(sp):
                def load(i, j):
                    if not isinstance(i, int):
                        weights.load(sp, i, j, (a_done, b_done, y_done))
                    elif j == 1:
                        sp.wait_ge(x_in[0], 16)
                        weights.load(sp, i, j)

                over_blocks(sp, load)

            @block.gpsimd
            def _(pool):
                def gather(i, j):
                    b = 2 * i + j
                    at = slice(b, b + 1) if isinstance(b, int) else bass.ds(b, 1)
                    wait(pool, x_turned[j], i)
                    nc.gpsimd.tensor_copy(idx[:, j:j + 1], slot_token[:, at]).then_inc(idx_ready[j], 1)
                    pool.wait_ge(idx_ready[j], i + 1)
                    pool.sem_inc(gathers, 1)
                    nc.gpsimd.indirect_dma_start(xg[:, j, :], None, xn,
                                                 bass.IndirectOffsetOnAxis(idx[:, j:j + 1].bitcast(U32), 0)
                                                 ).then_inc(x_in[j], 16)

                gather(0, 0)
                over_blocks(pool, lambda i, j: gather(*next_(i, j)))

            @block.tensor
            def _(pe):
                def turn_x(i, j):
                    pe.wait_ge(x_in[j], 16 * i + 16)
                    wait(pe, x_kept[1 - j], upto_last(i, j))
                    for k in range(KC):
                        ins = pe.transpose(p_x[:, k * P:(k + 1) * P], xg[:, j, k::KC], c.const("ident"))
                    ins.then_inc(x_turned[j], 1)

                def up(i, j, ps, w, w_in, freed, done):
                    pe.wait_ge(w_in[j], 16 * i + 16)
                    wait(pe, freed[1 - j], upto_last(i, j))
                    for k in range(KC):
                        ins = pe.matmul(ps[:, :], xT[:, j, k * P:(k + 1) * P], w[:, j, k * FF:(k + 1) * FF],
                                        start=(k == 0), stop=(k == KC - 1))
                    ins.then_inc(done[j], 1)

                def turn_h(i, j):
                    pe.wait_ge(h_ready[j], i + 1)
                    wait(pe, h_kept[1 - j], upto_last(i, j))
                    for k in range(KF):
                        ins = pe.transpose(p_h[:, k * P:(k + 1) * P], h[:, j, k::KF], c.const("ident"))
                    ins.then_inc(h_turned[j], 1)

                def down(i, j):
                    pe.wait_ge(h_kept[j], i + 1)
                    pe.wait_ge(w2_in[j], 16 * i + 16)
                    wait(pe, y_ready[1 - j], upto_last(i, j))
                    for n in range(2):
                        for k in range(KF):
                            ins = pe.matmul(p_y[:, n * BANK:(n + 1) * BANK], hT[:, j, k * P:(k + 1) * P],
                                            w2s[:, j, k * D + n * BANK:k * D + (n + 1) * BANK],
                                            start=(k == 0), stop=(k == KF - 1))
                    ins.then_inc(y_done[j], 1)

                def body(i, j):
                    first = isinstance(i, int) and i == 0 and j == 0
                    pe.wait_ge(x_kept[j], i + 1)
                    up(i, j, p_a, w1s, w1_in, a_ready, a_done)
                    if not first:
                        turn_h(*last(i, j))
                    up(i, j, p_b, w3s, w3_in, h_ready, b_done)
                    turn_x(*next_(i, j))
                    if not first:
                        down(*last(i, j))

                def tail(i, j):
                    turn_h(i, j)
                    down(i, j)

                turn_x(0, 0)
                over_blocks(pe, body, tail)

            @block.scalar
            def _(act):
                def silu(i, j):
                    act.wait_ge(a_done[j], i + 1)
                    wait(act, h_ready[j], i)
                    nc.scalar.activation(a[:, j, :], p_a[:, :], ACT.Silu).then_inc(a_ready[j], 1)

                def store(i, j):
                    b = 2 * i + j
                    at = slice(b, b + 1) if isinstance(b, int) else bass.ds(b, 1)
                    act.wait_ge(y_done[j], i + 1)
                    wait(act, y_out[j], 16 * i)
                    nc.scalar.activation(y[:, j, :], p_y[:, :], ACT.Copy).then_inc(y_ready[j], 1)
                    act.wait_ge(y_ready[j], i + 1)
                    act.dma_start(y_b[at].rearrange("e p n -> (e p) n"), y[:, j, :]).then_inc(y_out[j], 16)

                def body(i, j):
                    silu(i, j)
                    if not (isinstance(i, int) and i == 0 and j == 0):
                        store(*last(i, j))

                n = over_blocks(act, body, store)
                act.wait_ge(y_out[0], ((n + 1) >> 1) * 16)
                act.wait_ge(y_out[1], (n >> 1) * 16)
                act.sem_inc(stored, 1)

            @block.vector
            def _(dve):
                def keep_x(i, j):
                    dve.wait_ge(x_turned[j], i + 1)
                    wait(dve, b_done[j], i)
                    nc.vector.tensor_copy(xT[:, j, :], p_x[:, :]).then_inc(x_kept[j], 1)

                def keep_h(i, j):
                    dve.wait_ge(h_turned[j], i + 1)
                    wait(dve, y_done[j], i)
                    nc.vector.tensor_copy(hT[:, j, :], p_h[:, :]).then_inc(h_kept[j], 1)

                def body(i, j):
                    if not (isinstance(i, int) and i == 0 and j == 0):
                        keep_h(*last(i, j))
                    dve.wait_ge(b_done[j], i + 1)
                    dve.wait_ge(a_ready[j], i + 1)
                    wait(dve, h_turned[j], i)
                    nc.vector.tensor_tensor(h[:, j, :], a[:, j, :], p_b[:, :], ALU.mult).then_inc(h_ready[j], 1)
                    keep_x(*next_(i, j))

                keep_x(0, 0)
                over_blocks(dve, body, keep_h)


def combine(c, x3, y_slots, dest, gates, out):
    nc, io = c.nc, c.io
    x_t, out_t = x3.rearrange("(t p) d -> t p d", p=P), out.rearrange("(t p) d -> t p d", p=P)
    with ExitStack() as s:
        def sb(name, shape, dt=F32):
            return s.enter_context(nc.sbuf_tensor(f"cb_{name}", shape, dt))

        x, y = sb("x", [P, NT, D]), sb("y", [P, NT, 2, D])
        sq, gain, ss, eps = sb("sq", [P, D]), sb("gain", [P, D]), sb("ss", [P, 3, NT]), sb("eps", [P, 1])
        gain_in, eps_ready, added, rms_ready, ready = (c.sem(f"cb_{n}") for n in ("gain_in", "eps", "added", "rms", "ready"))
        x_in, y_in = ([c.sem(f"cb_{n}{t}") for t in range(NT)] for n in ("x_in", "y_in"))
        out_done = c.sem("cb_out_done")
        with nc.Block() as block:
            @block.sync
            def _(sp):
                sp.dma_start(gain[:, :], io["norm_f_g_2"].partition_broadcast(P)).then_inc(gain_in, 16)
                for t in range(NT):
                    sp.dma_start(x[:, t, :], x_t[t]).then_inc(x_in[t], 16)
                for t in range(NT):
                    sp.wait_ge(ready, t + 1)
                    sp.dma_start(out_t[t], x[:, t, :]).then_inc(out_done, 16)
                sp.wait_ge(out_done, 16 * NT)

            @block.gpsimd
            def _(pool):
                for t in range(NT):
                    for k in range(2):
                        nc.gpsimd.indirect_dma_start(y[:, t, k, :], None, y_slots,
                                                     bass.IndirectOffsetOnAxis(dest[:, k, t:t + 1].bitcast(U32), 0)
                                                     ).then_inc(y_in[t], 16)

            @block.scalar
            def _(act):
                act.wait_ge(eps_ready, 1)
                for t in range(NT):
                    act.wait_ge(added, t + 1)
                    c.astep(act, nc.scalar.activation(sq[:, :], x[:, t, :], ACT.Square, accum_out=ss[:, 0, t:t + 1]))
                    nc.scalar.activation(ss[:, 1, t:t + 1], ss[:, 0, t:t + 1], ACT.Sqrt, scale=1.0 / D, bias=eps[:, :]
                                         ).then_inc(rms_ready, 1)

            @block.vector
            def _(dve):
                nc.vector.memset(eps[:, :], EPS).then_inc(eps_ready, 1)
                dve.wait_ge(gain_in, 16)

                def add(t):
                    xx = x[:, t, :]
                    dve.wait_ge(x_in[t], 16)
                    dve.wait_ge(y_in[t], 32)
                    c.vstep(dve, nc.vector.scalar_tensor_tensor(xx, y[:, t, 0, :], gates[:, 0, t:t + 1], xx,
                                                                ALU.mult, ALU.add))
                    nc.vector.scalar_tensor_tensor(xx, y[:, t, 1, :], gates[:, 1, t:t + 1], xx, ALU.mult, ALU.add
                                                   ).then_inc(added, 1)

                def norm(t):
                    xx = x[:, t, :]
                    dve.wait_ge(rms_ready, t + 1)
                    c.vstep(dve, nc.vector.reciprocal(ss[:, 2, t:t + 1], ss[:, 1, t:t + 1]))
                    nc.vector.scalar_tensor_tensor(xx, xx, ss[:, 2, t:t + 1], gain[:, :], ALU.mult, ALU.mult
                                                   ).then_inc(ready, 1)

                for t in range(NT):
                    add(t)
                    if t >= 1:
                        norm(t - 1)
                norm(NT - 1)


def mixture(c, x3, xn, y_slots, out):
    nc, io = c.nc, c.io
    with ExitStack() as s:
        gates = s.enter_context(nc.sbuf_tensor("gates", [P, 2, NT], F32))
        dest = s.enter_context(nc.sbuf_tensor("dest", [P, 2, NT], I32))
        slot_token = s.enter_context(nc.sbuf_tensor("slot_token", [P, NBLK + 1], I32))
        block_expert = s.enter_context(nc.sbuf_tensor("block_expert", [P, NBLK], I32))
        n_blocks = s.enter_context(nc.sbuf_tensor("n_blocks", [P, 3], I32))
        with ExitStack() as s1:
            weights = ExpertWeights(c, s1, block_expert)
            with ExitStack() as s2:
                bias = s2.enter_context(nc.sbuf_tensor("rt_bias", [P, NG + NE], F32))
                logits = s2.enter_context(nc.psum_tensor("rt_scores", [P, NT, 64], F32))
                with ExitStack() as s3:
                    wr = s3.enter_context(nc.sbuf_tensor("rt_w", [P, KC, NG + NE], F32))
                    hT = s3.enter_context(nc.sbuf_tensor("h4T", [P, KC, S], F32))
                    norm_transposed(c, "n4", x3, io["norm_moe_g_2"], None, plain=hT, keep=xn, gain_row=io["norm_moe_g_2"],
                                    router=(wr, bias, logits))
                route(c, logits, bias, weights, gates, dest, slot_token, block_expert, n_blocks)
            experts(c, weights, xn, y_slots, slot_token, n_blocks)
        combine(c, x3, y_slots, dest, gates, out)


INS = ["x", "norm_pre_g", "w_in", "conv_w", "w_out", "norm_post_g", "mem_2", "norm_mix_g_2", "w_in_2", "b_gate_2",
       "b_if_2", "conv_w_2", "conv_b_2", "mh_norm_g_2", "sgu_norm_g_2", "b_s_2", "w_out_2", "norm_x_g_2",
       "norm_mem_g_2", "w_xq_2", "w_xkv_2", "w_xo_2", "norm_moe_g_2", "w_rg_2", "b_rg_2", "w_re_2", "b_re_2", "w1_2",
       "w3_2", "w2_2", "norm_f_g_2"]
WHOLE = {"norm_pre_g", "w_in", "conv_w", "w_out", "norm_post_g", "norm_f_g_2"}


def build(nc, io):
    def scratch(name, rows):
        return nc.dram_tensor(name, (rows, D), F32, kind="Internal").ap()

    x1, x2, x3, xn = (scratch(f"{n}_rows", S) for n in ("x1", "x2", "x3", "xn"))
    og, yb, y_slots = scratch("og_rows", S), scratch("yb_rows", S), scratch("y_slots", NBLK * P)
    qk1, v1 = (nc.dram_tensor(n, shape, F32, kind="Internal").ap()
               for n, shape in (("qk1_columns", (2 * AW // P, P, S)), ("v1_rows", (S, AW))))
    qk2, v2 = (nc.dram_tensor(n, shape, F32, kind="Internal").ap()
               for n, shape in (("qk2_columns", (2 * D // P, P, S)), ("v2_rows", (S, D))))
    with ExitStack() as ctx:
        c = Core(nc, io, ctx)
        load_constants(c)
        first_block(c, io["x"], x1, qk1, v1)
        c.retire_semaphores()
        second_mixer(c, x1, x2, og, yb, qk2, v2)
        c.retire_semaphores()
        cross_attention(c, x2, x3, y_slots)
        c.retire_semaphores()
        mixture(c, x3, xn, y_slots, io["out"])


def kernel(**inputs):
    import concourse.bacc as bacc
    from concourse.bass_utils import run_bass_kernel_spmd as run

    nc = bacc.Bacc("TRN2", target_bir_lowering=False, num_devices=1)
    arrays = {}
    for name in INS:
        a = np.asarray(inputs[name])
        arrays[name] = np.ascontiguousarray(a if name in WHOLE else a[0])
    arrays["w_s_T"] = np.ascontiguousarray(np.asarray(inputs["w_s_2"])[0].transpose(0, 2, 1))
    arrays["consts"] = shape_constants()
    io = {n: nc.dram_tensor(n, a.shape, mybir.dt.from_np(a.dtype), kind="ExternalInput").ap() for n, a in arrays.items()}
    io["out"] = nc.dram_tensor("out", (S, D), F32, kind="ExternalOutput").ap()
    build(nc, io)
    r = run(nc, [arrays], core_ids=[0])
    return r.results[0]["out"].reshape(1, S, D)
```
